# Optimizing a Trainium2 kernel written in Bass

```python
import math
import jax, jax.numpy as jnp
from jax import lax
import numpy as np

D_MODEL = 1024
BATCH = 1
SEQ = 512
DEPTH = 1

CHUNK = 64
MIX_WIDTH = D_MODEL
POOL_WIDTH = D_MODEL // 2
POOL_GROUPS = 4
POOL_GROUP_DIM = POOL_WIDTH // POOL_GROUPS
POOL_WINDOWS = (2, 4, 8, 16)
GDN_WIDTH = MIX_WIDTH - POOL_WIDTH
GDN_HEADS = 4
GDN_HEAD_DIM = GDN_WIDTH // GDN_HEADS
CONV_WIDTH = 4
D_FF = 4 * D_MODEL
EPS = 1e-6
IN_WIDTH = POOL_WIDTH + 4 * GDN_WIDTH + 2 * GDN_HEADS


def rms_norm(x, w):
    xf = x.astype(jnp.float32)
    y = xf * lax.rsqrt(jnp.mean(xf * xf, axis=-1, keepdims=True) + EPS)
    return (y * w.astype(jnp.float32)).astype(x.dtype)

def l2_norm(t):
    return t * lax.rsqrt(jnp.sum(t * t, axis=-1, keepdims=True) + EPS)

def pool_mixer(u, w_pool, pool_scale):
    B, S, _ = u.shape
    uf = u.astype(jnp.float32)
    cs = jnp.cumsum(uf, axis=1)
    count = jnp.arange(1, S + 1, dtype=jnp.float32)[None, :, None]
    outs = []
    for g, w in enumerate(POOL_WINDOWS):
        sl = slice(g * POOL_GROUP_DIM, (g + 1) * POOL_GROUP_DIM)
        c = cs[..., sl]
        prev = jnp.pad(c, ((0, 0), (w, 0), (0, 0)))[:, :S]
        mean = (c - prev) / jnp.minimum(count, float(w))
        outs.append(mean - uf[..., sl])
    pooled = jnp.stack(outs, axis=2).astype(u.dtype)
    mixed = jnp.einsum('bsgc,gcd->bsgd', pooled, w_pool)
    return mixed.reshape(B, S, POOL_WIDTH) * pool_scale

def causal_conv_silu(x, w):
    C = x.shape[-1]
    y = lax.conv_general_dilated(x, w[:, None, :].astype(x.dtype), window_strides=(1,),
                                 padding=[(CONV_WIDTH - 1, 0)],
                                 dimension_numbers=('NWC', 'WIO', 'NWC'),
                                 feature_group_count=C)
    return jax.nn.silu(y)

def gated_delta_net(q, k, v, z, a, b, a_log, dt_bias, gdn_norm):
    B, S, _ = q.shape
    H, Dh, C = GDN_HEADS, GDN_HEAD_DIM, CHUNK
    N = S // C
    f32 = jnp.float32

    def heads(t):
        return t.astype(f32).reshape(B, N, C, H, Dh).transpose(0, 3, 1, 2, 4)

    def per_head(t):
        return t.reshape(B, N, C, H).transpose(0, 3, 1, 2)

    qh = l2_norm(heads(q)) * (Dh ** -0.5)
    kh = l2_norm(heads(k))
    vh = heads(v)
    beta = per_head(jax.nn.sigmoid(b.astype(f32)))
    g = -jnp.exp(a_log.astype(f32)) * jax.nn.softplus(a.astype(f32) + dt_bias.astype(f32))
    gcum = jnp.cumsum(per_head(g), axis=-1)

    idx = jnp.arange(C)
    incl = idx[:, None] >= idx[None, :]
    strict = idx[:, None] > idx[None, :]
    diff = gcum[..., :, None] - gcum[..., None, :]
    decay_incl = jnp.exp(jnp.where(incl, diff, -jnp.inf))
    decay_strict = jnp.where(strict, decay_incl, 0.0)

    kb = kh * beta[..., None]
    m = jnp.einsum('bhncd,bhnjd->bhncj', kb, kh) * decay_strict
    lhs = jnp.eye(C, dtype=f32) + m
    rhs = jnp.concatenate([vh * beta[..., None], kb * jnp.exp(gcum)[..., None]], axis=-1)
    sol = lax.linalg.triangular_solve(lhs, rhs, left_side=True, lower=True)
    value, k_cumdecay = sol[..., :Dh], sol[..., Dh:]
    attn_inner = jnp.einsum('bhncd,bhnjd->bhncj', qh, kh) * decay_incl
    q_dec = qh * jnp.exp(gcum)[..., None]
    g_last = gcum[..., -1]
    k_dec = kh * jnp.exp(g_last[..., None] - gcum)[..., None]

    def step(state, inp):
        qd, kc, val, ai, kd, gl = inp
        v_new = val - jnp.einsum('bhcd,bhde->bhce', kc, state)
        o = jnp.einsum('bhcd,bhde->bhce', qd, state) + jnp.einsum('bhcj,bhje->bhce', ai, v_new)
        state = state * jnp.exp(gl)[..., None, None] + jnp.einsum('bhcd,bhce->bhde', kd, v_new)
        return state, o

    xs = (jnp.moveaxis(q_dec, 2, 0), jnp.moveaxis(k_cumdecay, 2, 0), jnp.moveaxis(value, 2, 0),
          jnp.moveaxis(attn_inner, 2, 0), jnp.moveaxis(k_dec, 2, 0), jnp.moveaxis(g_last, 2, 0))
    state0 = jnp.zeros((B, H, Dh, Dh), f32)
    _, o = lax.scan(step, state0, xs)
    o = o.transpose(1, 0, 3, 2, 4).reshape(B, S, H, Dh)
    o = o * lax.rsqrt(jnp.mean(o * o, axis=-1, keepdims=True) + EPS) * gdn_norm.astype(f32)
    o = o * jax.nn.silu(z.astype(f32).reshape(B, S, H, Dh))
    return o.reshape(B, S, GDN_WIDTH).astype(q.dtype)

def first_inputs(seed: int = 0) -> dict:
    key = jax.random.key(seed)
    ks = jax.random.split(key, 16)
    nrm = jax.random.normal
    H, Dh = GDN_HEADS, GDN_HEAD_DIM
    x = nrm(ks[0], (BATCH, SEQ, D_MODEL), jnp.float32)
    norm_mix = 1.0 + 0.02 * nrm(ks[1], (DEPTH, D_MODEL), jnp.float32)
    w_in = nrm(ks[2], (DEPTH, D_MODEL, IN_WIDTH), jnp.float32) * D_MODEL ** -0.5
    conv_w = nrm(ks[3], (DEPTH, CONV_WIDTH, 3 * GDN_WIDTH), jnp.float32) * CONV_WIDTH ** -0.5
    w_pool = nrm(ks[4], (DEPTH, POOL_GROUPS, POOL_GROUP_DIM, POOL_GROUP_DIM), jnp.float32) * POOL_GROUP_DIM ** -0.5
    pool_scale = 1.0 + 0.1 * nrm(ks[5], (DEPTH, POOL_WIDTH), jnp.float32)
    a_log = jnp.log(jax.random.uniform(ks[6], (DEPTH, H), jnp.float32, 1.0, 16.0))
    dt = jnp.exp(jax.random.uniform(ks[7], (DEPTH, H), jnp.float32, math.log(1e-3), math.log(1e-1)))
    dt_bias = dt + jnp.log(-jnp.expm1(-dt))
    gdn_norm = 1.0 + 0.02 * nrm(ks[8], (DEPTH, Dh), jnp.float32)
    w_out = nrm(ks[9], (DEPTH, MIX_WIDTH, D_MODEL), jnp.float32) * MIX_WIDTH ** -0.5
    norm_mlp = 1.0 + 0.02 * nrm(ks[10], (DEPTH, D_MODEL), jnp.float32)
    w_up = nrm(ks[11], (DEPTH, D_MODEL, D_FF), jnp.float32) * D_MODEL ** -0.5
    w_down = nrm(ks[12], (DEPTH, D_FF, D_MODEL), jnp.float32) * D_FF ** -0.5
    norm_final = 1.0 + 0.02 * nrm(ks[13], (D_MODEL,), jnp.float32)
    return {"x": x, "norm_mix": norm_mix, "w_in": w_in, "conv_w": conv_w, "w_pool": w_pool,
            "pool_scale": pool_scale, "a_log": a_log, "dt_bias": dt_bias, "gdn_norm": gdn_norm,
            "w_out": w_out, "norm_mlp": norm_mlp, "w_up": w_up, "w_down": w_down,
            "norm_final": norm_final}

def first_block(x, norm_mix, w_in, conv_w, w_pool, pool_scale, a_log, dt_bias, gdn_norm,
              w_out, norm_mlp, w_up, w_down, norm_final):
    P, G, H = POOL_WIDTH, GDN_WIDTH, GDN_HEADS
    h = x
    for l in range(DEPTH):
        u = rms_norm(h, norm_mix[l])
        proj = u @ w_in[l]
        pool_out = pool_mixer(proj[..., :P], w_pool[l], pool_scale[l])
        qkv = causal_conv_silu(proj[..., P:P + 3 * G], conv_w[l])
        z = proj[..., P + 3 * G:P + 4 * G]
        a = proj[..., P + 4 * G:P + 4 * G + H]
        b = proj[..., P + 4 * G + H:P + 4 * G + 2 * H]
        gdn_out = gated_delta_net(qkv[..., :G], qkv[..., G:2 * G], qkv[..., 2 * G:], z, a, b,
                                  a_log[l], dt_bias[l], gdn_norm[l])
        mix = jnp.concatenate([pool_out, gdn_out], axis=-1)
        h = h + mix @ w_out[l]
        u = rms_norm(h, norm_mlp[l])
        h = h + jnp.square(jax.nn.relu(u @ w_up[l])) @ w_down[l]
    return rms_norm(h, norm_final)


DEPTH_2 = 2

N_MIXERS = 2
NEG_INF = -1e30
FORCE_SCORE = 1e9

N_HEADS = 16
HEAD_DIM = 64
N_KV_GROUPS = 4
HEADS_PER_GROUP = N_HEADS // N_KV_GROUPS
ATTN_WIDTH = N_HEADS * HEAD_DIM
KV_WIDTH = N_KV_GROUPS * HEAD_DIM
CMP_BLOCK = 32
CMP_STRIDE = 16
CMP_HIDDEN = 256
SEL_BLOCK = 64
SEL_TOPK = 16
WINDOW = 512
Q_BLOCK = 64
NSA_IN = ATTN_WIDTH + 6 * KV_WIDTH + 3 * N_HEADS + ATTN_WIDTH

SSM_WIDTH = D_MODEL
SSM_GROUP = 16
SSM_GROUPS = SSM_WIDTH // SSM_GROUP
SSM_STATE = 64
SCAN_CHUNK = 128
DT_MIN = 1e-3
DT_MAX = 1e-1


def _rmsnorm(x, g):
    xf = x.astype(jnp.float32)
    y = xf * lax.rsqrt(jnp.mean(xf * xf, axis=-1, keepdims=True) + EPS) * g.astype(jnp.float32)
    return y.astype(x.dtype)

def _masked_softmax(s, mask):
    s = jnp.where(mask, s, NEG_INF)
    m = jnp.max(s, axis=-1, keepdims=True)
    p = jnp.where(mask, jnp.exp(s - m), 0.0)
    return p / jnp.maximum(jnp.sum(p, axis=-1, keepdims=True), 1e-30)

def _alibi_slopes():
    h = jnp.arange(1, N_HEADS + 1, dtype=jnp.float32)
    return jnp.exp2(-8.0 * h / N_HEADS).reshape(N_KV_GROUPS, HEADS_PER_GROUP)

def _compress(k, cmp_idx, pe, w1, w2):
    bsz = k.shape[0]
    n_cmp = cmp_idx.shape[0]
    blk = k[:, cmp_idx] + pe[:, None, :]
    blk = jnp.transpose(blk, (0, 1, 3, 2, 4)).reshape(bsz, n_cmp, N_KV_GROUPS, CMP_BLOCK * HEAD_DIM)
    return jax.nn.silu(blk @ w1) @ w2

def _nsa_mixer(h, w_in, cmp_k_pe, cmp_k_w1, cmp_k_w2, cmp_v_pe, cmp_v_w1, cmp_v_w2, w_out):
    f32 = jnp.float32
    bsz, seq, _ = h.shape
    G, R = N_KV_GROUPS, HEADS_PER_GROUP
    n_cmp = (seq - CMP_BLOCK) // CMP_STRIDE + 1
    n_blocks = seq // SEL_BLOCK
    n_sel = min(SEL_TOPK, n_blocks)

    splits = [ATTN_WIDTH + i * KV_WIDTH for i in range(7)] + [ATTN_WIDTH + 6 * KV_WIDTH + 3 * N_HEADS]
    q, kc, vc, ks, vs, kw, vw, gates, z = jnp.split(h @ w_in, splits, axis=-1)
    q = q.reshape(bsz, seq, G, R, HEAD_DIM) * (HEAD_DIM ** -0.5)
    kc, vc, ks, vs, kw, vw = [a.reshape(bsz, seq, G, HEAD_DIM) for a in (kc, vc, ks, vs, kw, vw)]
    gates = jax.nn.sigmoid(gates.astype(f32)).reshape(bsz, seq, 3, G, R)
    slopes = _alibi_slopes()

    cmp_start = jnp.arange(n_cmp) * CMP_STRIDE
    cmp_idx = cmp_start[:, None] + jnp.arange(CMP_BLOCK)[None, :]
    k_cmp = _compress(kc, cmp_idx, cmp_k_pe, cmp_k_w1, cmp_k_w2)
    v_cmp = _compress(vc, cmp_idx, cmp_v_pe, cmp_v_w1, cmp_v_w2)
    cmp_end = cmp_start + CMP_BLOCK - 1
    cmp_center = cmp_start.astype(f32) + 0.5 * (CMP_BLOCK - 1)

    sel_start = jnp.arange(n_blocks) * SEL_BLOCK
    overlap = ((cmp_start[:, None] <= sel_start[None, :] + SEL_BLOCK - 1)
               & (cmp_end[:, None] >= sel_start[None, :])).astype(f32)

    ks_blk = jnp.transpose(ks.reshape(bsz, n_blocks, SEL_BLOCK, G, HEAD_DIM), (0, 3, 1, 2, 4))
    vs_blk = jnp.transpose(vs.reshape(bsz, n_blocks, SEL_BLOCK, G, HEAD_DIM), (0, 3, 1, 2, 4))
    gather = jax.vmap(jax.vmap(lambda kb, ix: kb[ix]))

    kw_pad = jnp.pad(kw, ((0, 0), (WINDOW, 0), (0, 0), (0, 0)))
    vw_pad = jnp.pad(vw, ((0, 0), (WINDOW, 0), (0, 0), (0, 0)))

    def block(qi):
        q0 = qi * Q_BLOCK
        t = q0 + jnp.arange(Q_BLOCK, dtype=jnp.int32)
        tf = t.astype(f32)
        qb = lax.dynamic_slice_in_dim(q, q0, Q_BLOCK, axis=1)
        gb = lax.dynamic_slice_in_dim(gates, q0, Q_BLOCK, axis=1)

        s_c = jnp.einsum('bqgrd,bngd->bgrqn', qb, k_cmp, preferred_element_type=f32)
        s_c = s_c - slopes[None, :, :, None, None] * (tf[:, None] - cmp_center[None, :])
        p_c = _masked_softmax(s_c, (cmp_end[None, :] <= t[:, None]))
        o_c = jnp.einsum('bgrqn,bngd->bqgrd', p_c, v_cmp)

        imp = jnp.einsum('bgrqn,nj->bgqj', p_c, overlap)
        j = jnp.arange(n_blocks)[None, :]
        jt = (t // SEL_BLOCK)[:, None]
        forced = (j == 0) | (j == jt) | (j == jt - 1)
        imp = jnp.where(forced, FORCE_SCORE, jnp.where(j > jt, -FORCE_SCORE, imp))
        _, sel_idx = lax.top_k(imp, n_sel)

        k_sel = gather(ks_blk, sel_idx)
        v_sel = gather(vs_blk, sel_idx).reshape(bsz, G, Q_BLOCK, n_sel * SEL_BLOCK, HEAD_DIM)
        pos_s = sel_idx[..., None] * SEL_BLOCK + jnp.arange(SEL_BLOCK)
        d_s = t[None, None, :, None, None] - pos_s
        s_s = jnp.einsum('bqgrd,bgqnkd->bgrqnk', qb, k_sel, preferred_element_type=f32)
        s_s = s_s - slopes[None, :, :, None, None, None] * d_s[:, :, None].astype(f32)
        s_s = s_s.reshape(bsz, G, R, Q_BLOCK, n_sel * SEL_BLOCK)
        m_s = (d_s >= 0)[:, :, None].reshape(bsz, G, 1, Q_BLOCK, n_sel * SEL_BLOCK)
        p_s = _masked_softmax(s_s, m_s)
        o_s = jnp.einsum('bgrqm,bgqmd->bqgrd', p_s, v_sel)

        kwb = lax.dynamic_slice_in_dim(kw_pad, q0, Q_BLOCK + WINDOW, axis=1)
        vwb = lax.dynamic_slice_in_dim(vw_pad, q0, Q_BLOCK + WINDOW, axis=1)
        pos_w = q0 - WINDOW + jnp.arange(Q_BLOCK + WINDOW, dtype=jnp.int32)
        d_w = t[:, None] - pos_w[None, :]
        m_w = (pos_w[None, :] >= 0) & (d_w >= 0) & (d_w < WINDOW)
        s_w = jnp.einsum('bqgrd,bkgd->bgrqk', qb, kwb, preferred_element_type=f32)
        s_w = s_w - slopes[None, :, :, None, None] * d_w.astype(f32)
        p_w = _masked_softmax(s_w, m_w)
        o_w = jnp.einsum('bgrqk,bkgd->bqgrd', p_w, vwb)

        return (gb[:, :, 0, :, :, None] * o_c + gb[:, :, 1, :, :, None] * o_s
                + gb[:, :, 2, :, :, None] * o_w)

    o = lax.map(block, jnp.arange(seq // Q_BLOCK, dtype=jnp.int32))
    o = jnp.moveaxis(o, 0, 1).reshape(bsz, seq, ATTN_WIDTH)
    o = (o * jax.nn.silu(z.astype(f32))).astype(h.dtype)
    return o @ w_out

def _complex_affine_combine(left, right):
    ar_i, ai_i, br_i, bi_i = left
    ar_j, ai_j, br_j, bi_j = right
    ar = ar_j * ar_i - ai_j * ai_i
    ai = ar_j * ai_i + ai_j * ar_i
    br = ar_j * br_i - ai_j * bi_i + br_j
    bi = ar_j * bi_i + ai_j * br_i + bi_j
    return ar, ai, br, bi

def _s5_mixer(h, w_in, log_dt, lambda_re, lambda_im, b_re, b_im, c_re, c_im, d_skip, w_glu, w_out):
    f32 = jnp.float32
    bsz, seq, _ = h.shape
    G, C, P = SSM_GROUPS, SSM_GROUP, SSM_STATE
    u, z = jnp.split(h @ w_in, 2, axis=-1)
    u = u.astype(f32).reshape(bsz, seq, G, C)

    dt = jnp.exp(log_dt.astype(f32))[:, None]
    lre = jnp.minimum(lambda_re.astype(f32), -1e-4)
    lim = lambda_im.astype(f32)
    mag = jnp.exp(lre * dt)
    ab_re = mag * jnp.cos(lim * dt)
    ab_im = mag * jnp.sin(lim * dt)
    den = lre * lre + lim * lim
    nr = ab_re - 1.0
    coef_re = (nr * lre + ab_im * lim) / den
    coef_im = (ab_im * lre - nr * lim) / den
    br32, bi32 = b_re.astype(f32), b_im.astype(f32)
    bb_re = coef_re[..., None] * br32 - coef_im[..., None] * bi32
    bb_im = coef_re[..., None] * bi32 + coef_im[..., None] * br32
    cr32, ci32 = c_re.astype(f32), c_im.astype(f32)

    n_chunks = seq // SCAN_CHUNK
    u_chunks = jnp.moveaxis(u.reshape(bsz, n_chunks, SCAN_CHUNK, G, C), 1, 0)
    a_re = jnp.broadcast_to(ab_re, (bsz, SCAN_CHUNK, G, P))
    a_im = jnp.broadcast_to(ab_im, (bsz, SCAN_CHUNK, G, P))

    def chunk_step(carry, u_c):
        x_re, x_im = carry
        bu_re = jnp.einsum('gpc,bkgc->bkgp', bb_re, u_c)
        bu_im = jnp.einsum('gpc,bkgc->bkgp', bb_im, u_c)
        ar, ai, sr, si = lax.associative_scan(_complex_affine_combine, (a_re, a_im, bu_re, bu_im), axis=1)
        xr = sr + ar * x_re[:, None] - ai * x_im[:, None]
        xi = si + ar * x_im[:, None] + ai * x_re[:, None]
        y = jnp.einsum('gcp,bkgp->bkgc', cr32, xr) - jnp.einsum('gcp,bkgp->bkgc', ci32, xi)
        return (xr[:, -1], xi[:, -1]), y

    x0 = jnp.zeros((bsz, G, P), f32)
    _, y = lax.scan(chunk_step, (x0, x0), u_chunks)
    y = jnp.moveaxis(y, 0, 1).reshape(bsz, seq, G, C) + d_skip.astype(f32) * u
    y = jax.nn.gelu(y.reshape(bsz, seq, SSM_WIDTH)).astype(h.dtype)
    ga, gb = jnp.split(y @ w_glu, 2, axis=-1)
    y = ga * jax.nn.sigmoid(gb)
    y = y * jax.nn.silu(z)
    return y @ w_out

def _normal(key, shape, scale):
    return jax.random.normal(key, shape, jnp.float32) * scale

def _nsa_params(key, p):
    ks = jax.random.split(key, 9)
    return {
        p + 'norm': 1.0 + _normal(ks[0], (D_MODEL,), 0.02),
        p + 'w_in': _normal(ks[1], (D_MODEL, NSA_IN), D_MODEL ** -0.5),
        p + 'cmp_k_pe': _normal(ks[2], (CMP_BLOCK, HEAD_DIM), 0.02),
        p + 'cmp_k_w1': _normal(ks[3], (CMP_BLOCK * HEAD_DIM, CMP_HIDDEN), (CMP_BLOCK * HEAD_DIM) ** -0.5),
        p + 'cmp_k_w2': _normal(ks[4], (CMP_HIDDEN, HEAD_DIM), CMP_HIDDEN ** -0.5),
        p + 'cmp_v_pe': _normal(ks[5], (CMP_BLOCK, HEAD_DIM), 0.02),
        p + 'cmp_v_w1': _normal(ks[6], (CMP_BLOCK * HEAD_DIM, CMP_HIDDEN), (CMP_BLOCK * HEAD_DIM) ** -0.5),
        p + 'cmp_v_w2': _normal(ks[7], (CMP_HIDDEN, HEAD_DIM), CMP_HIDDEN ** -0.5),
        p + 'w_out': _normal(ks[8], (ATTN_WIDTH, D_MODEL), ATTN_WIDTH ** -0.5),
    }

def _s5_params(key, p):
    ks = jax.random.split(key, 12)
    n = jnp.arange(SSM_STATE, dtype=jnp.float32)[None, :]
    return {
        p + 'norm': 1.0 + _normal(ks[0], (D_MODEL,), 0.02),
        p + 'w_in': _normal(ks[1], (D_MODEL, 2 * SSM_WIDTH), D_MODEL ** -0.5),
        p + 'log_dt': jax.random.uniform(ks[2], (SSM_GROUPS,), jnp.float32, math.log(DT_MIN), math.log(DT_MAX)),
        p + 'lambda_re': -0.5 + _normal(ks[3], (SSM_GROUPS, SSM_STATE), 0.01),
        p + 'lambda_im': math.pi * n + _normal(ks[4], (SSM_GROUPS, SSM_STATE), 0.01),
        p + 'b_re': _normal(ks[5], (SSM_GROUPS, SSM_STATE, SSM_GROUP), (2 * SSM_GROUP) ** -0.5),
        p + 'b_im': _normal(ks[6], (SSM_GROUPS, SSM_STATE, SSM_GROUP), (2 * SSM_GROUP) ** -0.5),
        p + 'c_re': _normal(ks[7], (SSM_GROUPS, SSM_GROUP, SSM_STATE), SSM_STATE ** -0.5),
        p + 'c_im': _normal(ks[8], (SSM_GROUPS, SSM_GROUP, SSM_STATE), SSM_STATE ** -0.5),
        p + 'd': _normal(ks[9], (SSM_GROUPS, SSM_GROUP), 1.0),
        p + 'w_glu': _normal(ks[10], (SSM_WIDTH, 2 * SSM_WIDTH), SSM_WIDTH ** -0.5),
        p + 'w_out': _normal(ks[11], (SSM_WIDTH, D_MODEL), SSM_WIDTH ** -0.5),
    }

def second_inputs(seed: int = 0) -> dict:
    key = jax.random.key(seed)
    kx, k0, k1, k2, k3, kf = jax.random.split(key, 6)
    inputs = {'x': jax.random.normal(kx, (BATCH, SEQ, D_MODEL), jnp.float32)}
    inputs.update(_nsa_params(k0, 'l0_'))
    inputs.update(_s5_params(k1, 'l1_'))
    inputs.update(_nsa_params(k2, 'l2_'))
    inputs.update(_s5_params(k3, 'l3_'))
    inputs['final_norm'] = 1.0 + _normal(kf, (D_MODEL,), 0.02)
    return inputs

def second_block(x,
              l0_norm, l0_w_in, l0_cmp_k_pe, l0_cmp_k_w1, l0_cmp_k_w2, l0_cmp_v_pe, l0_cmp_v_w1, l0_cmp_v_w2, l0_w_out,
              l1_norm, l1_w_in, l1_log_dt, l1_lambda_re, l1_lambda_im, l1_b_re, l1_b_im, l1_c_re, l1_c_im, l1_d, l1_w_glu, l1_w_out,
              l2_norm, l2_w_in, l2_cmp_k_pe, l2_cmp_k_w1, l2_cmp_k_w2, l2_cmp_v_pe, l2_cmp_v_w1, l2_cmp_v_w2, l2_w_out,
              l3_norm, l3_w_in, l3_log_dt, l3_lambda_re, l3_lambda_im, l3_b_re, l3_b_im, l3_c_re, l3_c_im, l3_d, l3_w_glu, l3_w_out,
              final_norm):
    nsa_layers = [
        (l0_norm, l0_w_in, l0_cmp_k_pe, l0_cmp_k_w1, l0_cmp_k_w2, l0_cmp_v_pe, l0_cmp_v_w1, l0_cmp_v_w2, l0_w_out),
        (l2_norm, l2_w_in, l2_cmp_k_pe, l2_cmp_k_w1, l2_cmp_k_w2, l2_cmp_v_pe, l2_cmp_v_w1, l2_cmp_v_w2, l2_w_out),
    ]
    s5_layers = [
        (l1_norm, l1_w_in, l1_log_dt, l1_lambda_re, l1_lambda_im, l1_b_re, l1_b_im, l1_c_re, l1_c_im, l1_d, l1_w_glu, l1_w_out),
        (l3_norm, l3_w_in, l3_log_dt, l3_lambda_re, l3_lambda_im, l3_b_re, l3_b_im, l3_c_re, l3_c_im, l3_d, l3_w_glu, l3_w_out),
    ]
    h = x
    for i in range(DEPTH_2):
        if i % N_MIXERS == 0:
            params = nsa_layers[i // N_MIXERS]
            y = _nsa_mixer(_rmsnorm(h, params[0]), *params[1:])
        else:
            params = s5_layers[i // N_MIXERS]
            y = _s5_mixer(_rmsnorm(h, params[0]), *params[1:])
        h = h + y.astype(h.dtype)
    return _rmsnorm(h, final_norm)


def setup_inputs(seed=0):
    out = dict(first_inputs(seed))
    for name, value in second_inputs(seed + 1).items():
        if name != "x":
            out[name + "_2"] = value
    return out


def reference(
    x, norm_mix, w_in, conv_w, w_pool, pool_scale, a_log, dt_bias, gdn_norm, w_out, norm_mlp,
    w_up, w_down, norm_final, l0_norm_2, l0_w_in_2, l0_cmp_k_pe_2, l0_cmp_k_w1_2, l0_cmp_k_w2_2,
    l0_cmp_v_pe_2, l0_cmp_v_w1_2, l0_cmp_v_w2_2, l0_w_out_2, l1_norm_2, l1_w_in_2, l1_log_dt_2,
    l1_lambda_re_2, l1_lambda_im_2, l1_b_re_2, l1_b_im_2, l1_c_re_2, l1_c_im_2, l1_d_2,
    l1_w_glu_2, l1_w_out_2, l2_norm_2, l2_w_in_2, l2_cmp_k_pe_2, l2_cmp_k_w1_2, l2_cmp_k_w2_2,
    l2_cmp_v_pe_2, l2_cmp_v_w1_2, l2_cmp_v_w2_2, l2_w_out_2, l3_norm_2, l3_w_in_2, l3_log_dt_2,
    l3_lambda_re_2, l3_lambda_im_2, l3_b_re_2, l3_b_im_2, l3_c_re_2, l3_c_im_2, l3_d_2,
    l3_w_glu_2, l3_w_out_2, final_norm_2,
):
    x = first_block(
        x, norm_mix, w_in, conv_w, w_pool, pool_scale, a_log, dt_bias, gdn_norm, w_out,
        norm_mlp, w_up, w_down, norm_final,
    )
    return second_block(
        x, l0_norm_2, l0_w_in_2, l0_cmp_k_pe_2, l0_cmp_k_w1_2, l0_cmp_k_w2_2, l0_cmp_v_pe_2,
        l0_cmp_v_w1_2, l0_cmp_v_w2_2, l0_w_out_2, l1_norm_2, l1_w_in_2, l1_log_dt_2,
        l1_lambda_re_2, l1_lambda_im_2, l1_b_re_2, l1_b_im_2, l1_c_re_2, l1_c_im_2, l1_d_2,
        l1_w_glu_2, l1_w_out_2, l2_norm_2, l2_w_in_2, l2_cmp_k_pe_2, l2_cmp_k_w1_2,
        l2_cmp_k_w2_2, l2_cmp_v_pe_2, l2_cmp_v_w1_2, l2_cmp_v_w2_2, l2_w_out_2, l3_norm_2,
        l3_w_in_2, l3_log_dt_2, l3_lambda_re_2, l3_lambda_im_2, l3_b_re_2, l3_b_im_2, l3_c_re_2,
        l3_c_im_2, l3_d_2, l3_w_glu_2, l3_w_out_2, final_norm_2,
    )


_drawn_inputs = setup_inputs


def setup_inputs(seed=0):
    import zlib

    import numpy as np

    out = dict(_drawn_inputs(seed))
    spreads = {}
    factors = {'norm_mix': 3.092,
     'gdn_norm': 7.112,
     'norm_mlp': 3.416,
     'l0_norm_2': 7.109,
     'l0_cmp_k_pe_2': 8.0,
     'l0_cmp_v_pe_2': 34.094,
     'l1_norm_2': 27.38,
     'l1_log_dt_2': 83.176,
     'l1_lambda_re_2': 200.0,
     'l1_lambda_im_2': 70.744,
     'l1_b_re_2': 139.92,
     'l1_b_im_2': 133.24,
     'l1_c_re_2': 130.688,
     'l1_c_im_2': 111.784,
     'final_norm_2': 23.804}
    for name, (base, spread) in spreads.items():
        noise = np.random.default_rng([zlib.crc32(name.encode()), seed]).standard_normal(out[name].shape)
        drawn = base * np.exp(spread * noise) if base else spread * noise
        out[name] = __import__('jax').numpy.asarray(drawn.astype(out[name].dtype))
    for name, factor in factors.items():
        out[name] = (out[name] * factor).astype(out[name].dtype)
    return out
```

```python
import numpy as np
import concourse.bass as bass
from concourse import mybir
from contextlib import ExitStack

D = 1024
T = 512
KT = D // 128
TT = T // 128
EPS = 1e-6
NEG = -1e30

NHG = 4
CH = 64
NCH = T // CH
FT = 4 * D // 128
PAD = 16
PW = T + PAD
CONV = 4

NH = 16
NG = 4
DH = 64
CMPB, CMPS = 32, 16
NCMP = (T - CMPB) // CMPS + 1

SG = 64
SC = 16
SP = 64
FR = 8
NC8 = T // FR
NPAIR = SG // 2

SLOTS = dict(inp=20, out=8, up=32, down=32, nsa=16, val=4, zed=8, nout=8, sin=16, glu=16, sout=8)
TILES = dict(inp=20, out=8, up=32, down=8, nsa=16, val=4, zed=8, nout=8, sin=16, glu=16, sout=8)


def bases(counts):
    at, out = 0, {}
    for name, n in counts.items():
        out[name] = at
        at += n
    return out, at


SLOT0, NSLOT = bases(SLOTS)
TILE0, NTILE = bases(TILES)

_mid = round((2 * np.pi - 6.28125) * 2.0 ** 21) / 2.0 ** 21
TWO_PI = [6.28125, _mid, 2 * np.pi - 6.28125 - _mid]
PI32 = float(np.nextafter(np.float32(np.pi), np.float32(0)))
ROUND = 1.5 * 2.0 ** 23

CONST_W = dict(ident=128, ones=128, cumsum=128, block=128, half=256, maskneg=128, neg16=128,
               low32=128, low64=128, dist=512, cdist=TT * NCMP, cmask=TT * NCMP, slope=NH,
               invcount=4 * PAD)
CONST_AT, NCONST = bases(CONST_W)
PARAM_W = dict(norm_mix=8, norm_mlp=8, norm_final=8, l0_norm=8, l1_norm=8, final_norm=8,
               conv=12 * CONV, pool_scale=4, gdn_norm=1, a_log=16, dt_bias=16, kpe=CMPB, vpe=CMPB,
               d_skip=8, log_dt=NPAIR, lre=NPAIR, lim=NPAIR)
PARAM_AT, NPARAM = bases(PARAM_W)


def build(nc, A, out_dram):
    f32 = mybir.dt.float32
    ALU = mybir.AluOpType
    ACT = mybir.ActivationFunctionType
    AX = mybir.AxisListType
    i32 = mybir.dt.int32

    ctx = ExitStack()
    with ctx:
        def sb(name, shape):
            return ctx.enter_context(nc.sbuf_tensor(name, shape, f32))

        def sem(name):
            return ctx.enter_context(nc.semaphore(name))

        hT = sb("hT", [128, KT, T])
        uT = sb("uT", [128, KT, T])
        mixT = sb("mixT", [128, KT, T])
        RING = 4
        ring = sb("ring", [128, RING, 1024])
        bigA = sb("bigA", [128, 16704])
        bigB = sb("bigB", [128, 16384])
        consts = sb("const_table", [128, NCONST])
        params = sb("param_table", [128, NPARAM])
        rms = sb("rms", [128, T])
        small = sb("small", [128, 704])
        ps = ctx.enter_context(nc.psum_tensor("ps", [128, 8, 512], f32))

        def const(name):
            a = CONST_AT[name]
            return consts[:, a:a + CONST_W[name]]

        def param(name):
            a = PARAM_AT[name]
            return params[:, a:a + PARAM_W[name]]

        def view(t, at, *dims):
            n = int(np.prod(dims))
            v = t[:, at:at + n]
            if len(dims) == 2:
                return v.rearrange("p (a b) -> p a b", b=dims[1])
            if len(dims) == 3:
                return v.rearrange("p (a b c) -> p a b c", b=dims[1], c=dims[2])
            return v

        uflat = uT[:, :, :].rearrange("p a b -> p (a b)")
        ident, ones = const("ident"), const("ones")

        projT = view(bigA, 0, 20, PW)
        qkvT = view(bigA, 20 * PW, 12, T)
        ffT = view(bigA, 0, FT, T)
        GA = TT * NHG * 128
        arr = [view(bigB, i * GA, TT, NHG * 128) for i in range(8)]
        brr = [view(bigA, 4 * PW + i * GA, TT, NHG * 128) for i in range(3)]
        urr = [view(uflat, i * GA, TT, NHG * 128) for i in range(2)]
        dec, kd, kbe, vb, Mm, aiT, Aa, Xx = arr
        A2, A2T, A4 = brr
        A4T, Rr = urr
        kcT, val, AT, A8, Yy, Bm32, Bm64, aS = kbe, vb, Xx, Aa, A2, A2T, A4, A2
        gB = Mm
        abS = small[:, 0:32].rearrange("p (t c) -> p t c", c=8)
        w_ab = small[:, 32:96]
        gx, ga, ge, gl, gg, bta, gc, eg, ekd, beg = (small[:, 96 + 16 * i:112 + 16 * i] for i in range(10))
        nalog = small[:, 256:272]
        egl = small[:, 272:304]
        Sst = view(mixT[:, :, :].rearrange("p a b -> p (a b)"), 4 * T, 2, 512)
        vnew = mixT[:, 6, :]
        l2n = mixT[:, 4:6, :]
        sqb = urr
        gdnO = view(uflat, 0, NHG, T)
        w_pool = view(bigB, 0, 4, 128)
        ptmp = [bigB[:, 1024:1024 + PW], bigB[:, 2048:2048 + PW]]
        pooled = view(bigB, 4096, 4, T)

        eps_ap, one_ap = small[:, 304:305], small[:, 305:306]

        nsT = view(bigA, 0, 16, T)
        zsT = view(bigA, 8192, KT, T)
        vtok = view(bigA, 12288, TT, 512)
        blk = view(bigA, 14336, 2, CMPB, NCMP)
        kcmp = view(bigA, 16320, 2, NCMP)
        vcmp = bigA[0:NCMP, 16384:16384 + NG * DH]
        w1 = [bigB[:, 0:8192], bigB[:, 8192:16384]]
        w2 = [mixT[:, 6, 0:128], mixT[:, 6, 128:256]]
        w_gate = mixT[:, 7, 0:384]
        hid = [view(mixT[:, 5, :], 256 * i, 2, 2, 2 * NCMP) for i in range(2)]
        gate = small[:, 308:500].rearrange("p (t b h) -> p t b h", b=3, h=NH)
        pcT = bigB[0:NCMP, 0:NH * T].rearrange("p (h q) -> p h q", q=T)
        pc = [view(bigB, 13312 + i * 496, NH, NCMP) for i in range(TT)]
        dsl = view(bigB, 8192, 2, 512)
        prob = view(bigB, 9216, 3, 2, 512)
        probT = view(bigB, 12288, 3, 2, 512)
        cm, cs_ = small[:, 500:516], small[:, 516:532]
        amax = small[:, 532:538].rearrange("p (u b) -> p u b", b=2)
        anmax = small[:, 538:544].rearrange("p (u b) -> p u b", b=2)
        asum = small[:, 544:550].rearrange("p (u b) -> p u b", b=2)
        UNITS = [(t, half, qt) for t in range(KT) for half in range(2) for qt in range(TT)]

        suP = view(bigA, 0, KT, T)
        szT = view(bigA, 4096, KT, T)
        uc = view(bigA, 8192, SG, NC8)
        wri = [view(bigA, 12288 + 2048 * i, NPAIR, NC8) for i in range(2)]
        yF = view(bigA, 12288, KT, T)
        ptab = [view(bigA, 12288 + 288 * i, 9, NPAIR) for i in range(4)]
        pk = [bigA[:, 13440 + 32 * i:13472 + 32 * i] for i in range(16)]
        BWT = [view(bigB, 4096 * i, NPAIR, 128) for i in range(2)]
        Tm = view(bigB, 0, SG // 2, 128)
        Kl = bigB[0:SC, 4096:8192].rearrange("p (g c) -> p g c", c=128)
        Eri = [view(bigB, 8192 + 2048 * i, NPAIR, NC8) for i in range(2)]
        tmpS = [bigB[:, 12288 + 1024 * i:13312 + 1024 * i] for i in range(2)]
        rho = view(bigB, 12288, NPAIR, NC8)
        rot = [bigB[:, 2048 * i:2048 * i + 2048] for i in range(2)]
        bc = [view(bigB, 14336 + 512 * i, NPAIR, SC) for i in range(4)]
        CA = [view(uflat, 0, NPAIR, 128), view(mixT[:, :, :].rearrange("p a b -> p (a b)"), 0, NPAIR, 128)]
        prev = [view(bigA, 13984 + 256 * i, NPAIR, FR) for i in range(2)]
        mag = view(bigA, 14496, 9, NPAIR)
        mag8 = small[:, 308:340]
        rK = [small[:, 340 + 32 * i:372 + 32 * i] for i in range(6)]
        baS = [mixT[:, 2 * i:2 * i + 2, :].rearrange("p a b -> p (a b)") for i in range(2)]
        sg = view(bigB, 0, 2, T)
        gprod = view(bigB, 1024, 2, T)

        s_w1 = [sem("cmp_w1k_loaded"), sem("cmp_w1v_loaded")]
        s_w2 = sem("cmp_w2_loaded")
        s_wgate = sem("w_gate_loaded")
        v_done = sem("v_tile_ready")
        g_mm, g_out = sem("gate_product"), sem("gates_ready")
        blk_done, cmp_h, cmp_act, cmp_mm, cmp_out = (sem(f"compress_{n}") for n in
                                                     ("windows", "hidden", "silu", "product", "ready"))
        cs_sub = sem("cmp_max_subtracted")
        cs_mm, cs_x, cs_exp, cs_p, cs_t, cs_ev = (sem(f"cmp_{n}") for n in
                                                  ("scores", "shifted", "exp", "probs", "transposed", "probsT"))
        ds_ready = sem("slopes_ready")
        at_qk, at_s, at_m, at_e, at_p, at_t, at_ev, at_v, at_o = (sem(f"att_{n}") for n in
            ("scores", "scores_read", "max", "exp", "probs", "transposed", "probsT", "value", "out"))
        s_bc = sem("ssm_bc_loaded")
        ssm_a, ssm_b = sem("ssm_scalar_engine"), sem("ssm_params")
        ba_done, bt_mm, bt_ev = sem("ssm_b_powers"), sem("ssm_b_transposed"), sem("ssm_b_stored")
        ca_done = sem("ssm_c_powers")
        uc_in = sem("u_regrouped")
        w_mm, w_ev = sem("chunk_input_product"), sem("chunk_input_stored")
        rot_in, x_done = sem("rotated"), sem("chunk_states")
        k_mm, k_ev = sem("lag_kernel_product"), sem("lag_kernel_stored")
        t_zero, t_in = sem("lag_matrix_zero"), sem("lag_matrix_filled")
        y_mm, y_ev, y_in, y_d, y_g = (sem(f"y_{n}") for n in ("product", "stored", "regrouped", "skip", "gelu"))
        glu_s, glu_o = sem("glu_sigmoid"), sem("glu_out")

        s_x = sem("x_loaded")
        s_const = sem("consts_loaded")
        s_param = sem("params_loaded")
        s_wab = sem("w_ab_loaded")
        s_wpool = sem("w_pool_loaded")
        slot_loaded = [sem(f"slot{j}_loaded") for j in range(RING)]
        slot_used = sem("slot_used")
        tile_evicted = sem("tile_evicted")
        rms_sq, rms_sum, rms_std, rms_out = sem("rms_squares"), sem("rms_sum"), sem("rms_std"), sem("rms_out")
        dvc = sem("dve_chain")
        acc_ = sem("act_chain")
        plc = sem("pool_chain")
        pads0 = sem("pads_zero")
        ab_ready, ab_copied = sem("ab_ready"), sem("ab_copied")
        pooled_done, pool_mm, pool_out = sem("pooled"), sem("pool_product"), sem("pool_out")
        conv_step, conv_silu = sem("conv_step"), sem("conv_silu")
        l2_sq, l2_sum, l2_std, l2_out = sem("l2_squares"), sem("l2_sum"), sem("l2_std"), sem("l2_out")
        gate_a, gate_b = sem("gate_scalar_engine"), sem("gate_vector_engine")
        gate_mm = sem("gate_cumsum")
        row_mm, row_dec, row_exp, dec_exp = sem("row_sums"), sem("row_masked"), sem("row_exp"), sem("decay_ready")
        qd_done = sem("q_decayed")
        rnd_mm, rnd_ev = sem("round_product"), sem("round_evicted")
        sc_k, sc_v, sc_u, sc_s, sc_o, sc_oe = (sem(f"scan_{n}") for n in
                                              ("k_state", "v_new", "update", "state", "out", "out_copied"))
        go_sq, go_sum, go_std, go_out = sem("gdn_squares"), sem("gdn_sum"), sem("gdn_std"), sem("gdn_out")
        ff_sq = sem("ff_squared")
        out_done = sem("out_written")

        block = ctx.enter_context(nc.Block())

        ROUNDS = ["attn", "attnT", "ktok", "vtok", "gram", "AT", "A2", "A2T", "R2", "A4", "A4T", "R4",
                  "A8", "R8", "X32", "Y32", "R32", "X64", "Y64", "R64", "val", "kcT"]

        def hd(x, tt, h):
            return x[:, tt, h * 128:(h + 1) * 128]

        @block.sync
        def _(sp):
            for j in range(RING):
                sp.dma_start(ring[:, j, :], A["wstream"][j]).then_inc(slot_loaded[j], 16)
            with sp.Fori(1, NSLOT // RING) as m:
                for j in range(RING):
                    sp.wait_ge(slot_used, m * RING + j - RING + 1)
                    sp.dma_start(ring[:, j, :], A["wstream"][m * RING + j]).then_inc(slot_loaded[j], 16)

        @block.tensor
        def _(pe):
            def rms_pe(n):
                for k in range(KT):
                    pe.wait_ge(rms_sq, n * KT + k + 1)
                    i = pe.matmul(ps[:, 4, :], ones, uT[:, k, :], start=k == 0, stop=k == KT - 1)
                i.then_inc(rms_sum, 1)

            def tile_group(name, m, first=False, rhs=None):
                rhs = uT if rhs is None else rhs
                for j in range(4):
                    pe.wait_ge(slot_loaded[j], (m + SLOT0[name] // 4 + 1) * 16)
                    if not first:
                        pe.wait_ge(tile_evicted, m * 4 + TILE0[name] + j - 3)
                    for k in range(KT):
                        i = pe.matmul(ps[:, j, :], ring[:, j, k * 128:(k + 1) * 128], rhs[:, k, :],
                                      start=k == 0, stop=k == KT - 1)
                    i.then_inc(slot_used, 1)

            def linear(name, peeled=False, rhs=None):
                lo = 0
                if peeled:
                    tile_group(name, 0, first=True, rhs=rhs)
                    lo = 1
                with pe.Fori(lo, TILES[name] // 4) as m:
                    tile_group(name, m, rhs=rhs)

            pe.wait_ge(s_const, 16)
            rms_pe(0)
            pe.wait_ge(rms_out, KT)
            linear("inp", peeled=True)
            pe.wait_ge(s_wab, 16)
            for tt in range(TT):
                for k in range(KT):
                    i = pe.matmul(ps[:, 5, tt * 8:(tt + 1) * 8], uT[:, k, tt * 128:(tt + 1) * 128],
                                  w_ab[:, k * 8:(k + 1) * 8], start=k == 0, stop=k == KT - 1)
            i.then_inc(ab_ready, 1)
            pe.wait_ge(s_wpool, 16)
            for g in range(4):
                pe.wait_ge(pooled_done, g + 1)
                pe.wait_ge(tile_evicted, TILES["inp"])
                pe.matmul(ps[:, g, :], w_pool[:, g, :], pooled[:, g, :], start=True, stop=True).then_inc(pool_mm, 1)
            for i in range(8):
                pe.wait_ge(l2_sq, i + 1)
                if i < 1:
                    pe.wait_ge(ab_copied, 1)
                if i >= 2:
                    pe.wait_ge(l2_std, i - 1)
                pe.matmul(ps[:, 4 + i % 2, :], ones, uT[:, i, :], start=True, stop=True).then_inc(l2_sum, 1)
            pe.wait_ge(gate_b, 2)
            pe.wait_ge(pool_out, 4)
            pe.matmul(ps[:, 0, 0:16], const("cumsum"), gg, start=True, stop=True)
            pe.matmul(ps[:, 0, 16:32], const("block"), gg, start=True, stop=True)
            for c in range(2):
                i = pe.matmul(ps[:, 0, 32 + 16 * c:48 + 16 * c], const("half")[:, 128 * c:128 * c + 128], gg,
                              start=True, stop=True)
            i.then_inc(gate_mm, 1)
            for tt in range(TT):
                if tt == 0:
                    pe.wait_ge(gate_b, 3)
                    pe.wait_ge(l2_std, 8)
                for h in range(NHG):
                    i = pe.matmul(ps[:, 4 + tt, h * 128:(h + 1) * 128], hd(gB, tt, h), const("cumsum"),
                                  start=True, stop=True)
                i.then_inc(row_mm, 1)

            def qk(i, tt, h):
                return qkvT[:, i * 4 + h, tt * 128:(tt + 1) * 128]

            def operands(name, tt, h):
                return {
                    "attn": lambda: (qk(0, tt, h), qk(1, tt, h)),
                    "attnT": lambda: (hd(aS, tt, h), None),
                    "ktok": lambda: (qk(1, tt, h), None),
                    "vtok": lambda: (qk(2, tt, h), None),
                    "gram": lambda: (qk(1, tt, h), qk(1, tt, h)),
                    "AT": lambda: (hd(Aa, tt, h), None),
                    "A2": lambda: (hd(AT, tt, h), hd(Aa, tt, h)),
                    "A2T": lambda: (hd(Aa, tt, h), hd(AT, tt, h)),
                    "R2": lambda: (hd(A2, tt, h), hd(Rr, tt, h)),
                    "A4": lambda: (hd(A2T, tt, h), hd(A2, tt, h)),
                    "A4T": lambda: (hd(A2, tt, h), hd(A2T, tt, h)),
                    "R4": lambda: (hd(A4, tt, h), hd(Rr, tt, h)),
                    "A8": lambda: (hd(A4T, tt, h), hd(A4, tt, h)),
                    "R8": lambda: (hd(A8, tt, h), hd(Rr, tt, h)),
                    "X32": lambda: (hd(Rr, tt, h), None),
                    "Y32": lambda: (hd(Bm32, tt, h), hd(Rr, tt, h)),
                    "R32": lambda: (hd(Xx, tt, h), hd(Yy, tt, h)),
                    "X64": lambda: (hd(Rr, tt, h), None),
                    "Y64": lambda: (hd(Bm64, tt, h), hd(Rr, tt, h)),
                    "R64": lambda: (hd(Xx, tt, h), hd(Yy, tt, h)),
                    "val": lambda: (hd(Rr, tt, h), hd(vb, tt, h)),
                    "kcT": lambda: (hd(kbe, tt, h), hd(Rr, tt, h)),
                }[name]()

            pe.wait_ge(l2_out, 8)
            pe.wait_ge(dec_exp, TT)
            pe.wait_ge(row_exp, TT)
            for r, name in enumerate(ROUNDS):
                for tt in range(TT):
                    if r:
                        pe.wait_ge(rnd_ev, 4 * (r - 1) + tt + 1)
                    for h in range(NHG):
                        left, right = operands(name, tt, h)
                        o = ps[:, 4 + tt, h * 128:(h + 1) * 128]
                        if right is None:
                            i = pe.transpose(o, left, ident)
                        else:
                            i = pe.matmul(o, left, right, start=True, stop=True)
                    i.then_inc(rnd_mm, 1)

            pe.wait_ge(rnd_ev, 4 * len(ROUNDS))
            pe.wait_ge(qd_done, TT)
            for c in range(NCH):
                tt, half = c // 2, c % 2
                P = slice(64 * half, 64 * half + 64)
                S = Sst[:, c % 2, :]
                pe.wait_ge(sc_s, c + 1)
                for h in range(NHG):
                    i = pe.matmul(ps[P, 4, h * 128:(h + 1) * 128], kcT[:, tt, h * 128 + 64 * half:h * 128 + 64 * half + 64],
                                  S[:, h * 128:(h + 1) * 128], start=True, stop=True)
                i.then_inc(sc_k, 1)
                pe.wait_ge(sc_v, c + 1)
                for h in range(NHG):
                    i = pe.matmul(ps[:, 6, h * 128:(h + 1) * 128], kd[P, tt, h * 128:(h + 1) * 128],
                                  vnew[P, h * 128:(h + 1) * 128], start=True, stop=True)
                i.then_inc(sc_u, 1)
                if c >= 2:
                    pe.wait_ge(sc_oe, c - 1)
                for h in range(NHG):
                    o = ps[:, 5 + 2 * half, h * CH:(h + 1) * CH]
                    pe.matmul(o, S[:, h * 128:(h + 1) * 128], qkvT[:, h, c * CH:(c + 1) * CH], start=True, stop=False)
                    i = pe.matmul(o, vnew[P, h * 128:(h + 1) * 128],
                                  aiT[P, tt, h * 128 + 64 * half:h * 128 + 64 * half + 64], start=False, stop=True)
                i.then_inc(sc_o, 1)
            for h in range(NHG):
                pe.wait_ge(go_sq, h + 1)
                pe.matmul(ps[:, h, :], ones, urr[1].rearrange("p a b -> p (a b)")[:, h * T:(h + 1) * T],
                          start=True, stop=True).then_inc(go_sum, 1)
            pe.wait_ge(go_out, NHG)
            linear("out", rhs=mixT)
            rms_pe(1)
            pe.wait_ge(rms_out, 2 * KT)
            linear("up")
            pe.wait_ge(ff_sq, FT)
            with pe.Fori(0, 2) as m:
                for t in range(4):
                    pe.wait_ge(tile_evicted, m * 4 + TILE0["down"] + t - 3)
                    for j in range(4):
                        pe.wait_ge(slot_loaded[j], (m * 4 + SLOT0["down"] // 4 + t + 1) * 16)
                        for k in range(KT):
                            i = pe.matmul(ps[:, t, :], ring[:, j, k * 128:(k + 1) * 128], ffT[:, j * KT + k, :],
                                          start=j == 0 and k == 0, stop=j == 3 and k == KT - 1)
                        i.then_inc(slot_used, 1)
            rms_pe(2)
            rms_pe(3)
            pe.wait_ge(rms_out, 4 * KT)
            linear("nsa")
            for j in range(4):
                pe.wait_ge(slot_loaded[j], (SLOT0["val"] // 4 + 1) * 16)
            for tt in range(TT):
                pe.wait_ge(tile_evicted, TILE0["val"] + tt - 3)
                for k in range(KT):
                    i = pe.matmul(ps[:, tt, :], uT[:, k, tt * 128:(tt + 1) * 128],
                                  ring[:, k // 2, k % 2 * 512:k % 2 * 512 + 512], start=k == 0, stop=k == KT - 1)
                    if tt == TT - 1 and k % 2 == 1:
                        i.then_inc(slot_used, 1)
                    elif k == KT - 1:
                        i.then_inc(v_done, 1)
            pe.wait_ge(s_wgate, 16)
            for tt in range(TT):
                for k in range(KT):
                    i = pe.matmul(ps[:, 5, tt * 48:(tt + 1) * 48], uT[:, k, tt * 128:(tt + 1) * 128],
                                  w_gate[:, k * 48:(k + 1) * 48], start=k == 0, stop=k == KT - 1)
            i.then_inc(g_mm, 1)
            linear("zed")
            pe.wait_ge(g_out, 1)
            for x in range(2):
                pe.wait_ge(s_w1[x], 16)
                pe.wait_ge(blk_done, x + 1)
                if x:
                    pe.wait_ge(cmp_act, 1)
                for ht in range(2):
                    for l in range(CMPB):
                        for half in range(2):
                            P = slice(64 * half, 64 * half + 64)
                            i = pe.matmul(ps[:, 4 + 2 * half, ht * 64:ht * 64 + 2 * NCMP],
                                          w1[x][P, l * 256 + ht * 128:l * 256 + ht * 128 + 128], blk[P, :, l, :],
                                          start=l == 0, stop=l == CMPB - 1)
                i.then_inc(cmp_h, 1)
            pe.wait_ge(s_w2, 32)
            pe.wait_ge(cmp_act, 1)
            for half in range(2):
                for ht in range(2):
                    i = pe.matmul(ps[64 * half:64 * half + 64, 7, 0:2 * NCMP], w2[0][:, ht * 64:(ht + 1) * 64],
                                  hid[0][:, ht, half, :], start=ht == 0, stop=ht == 1)
            i.then_inc(cmp_mm, 1)
            pe.wait_ge(cmp_act, 2)
            for g in range(NG):
                for ht in range(2):
                    i = pe.matmul(ps[0:NCMP, 5, g * DH:(g + 1) * DH],
                                  hid[1][:, ht, g % 2, g // 2 * NCMP:g // 2 * NCMP + NCMP],
                                  w2[1][:, ht * 64:(ht + 1) * 64], start=ht == 0, stop=ht == 1)
            i.then_inc(cmp_mm, 1)
            pe.wait_ge(cmp_out, 2)
            pe.wait_ge(tile_evicted, TILE0["zed"] + 8)
            for tt in range(TT):
                if tt >= 2:
                    pe.wait_ge(cs_x, tt - 1)
                for t in range(KT):
                    for half in range(2):
                        P = slice(64 * half, 64 * half + 64)
                        i = pe.matmul(ps[:, tt % 2 * 2 + half, t * NCMP:(t + 1) * NCMP],
                                      nsT[P, t, tt * 128:(tt + 1) * 128], kcmp[P, t // 4, :], start=True, stop=True)
                i.then_inc(cs_mm, 1)
            for tt in range(TT):
                pe.wait_ge(cs_p, tt + 1)
                for b in range(4):
                    n = tt * 4 + b
                    if n >= 2:
                        pe.wait_ge(cs_ev, n - 1)
                    for h in range(4):
                        i = pe.transpose(ps[0:NCMP, 4 + n % 2, h * 128:(h + 1) * 128], pc[tt][:, b * 4 + h, :], ident)
                    i.then_inc(cs_t, 1)
            pe.wait_ge(cs_ev, 16)

            def scores(u):
                t, half, qt = UNITS[u]
                P = slice(64 * half, 64 * half + 64)
                W = (qt + 1) * 128
                if u >= 2:
                    pe.wait_ge(at_s, u - 1)
                for b in range(2):
                    i = pe.matmul(ps[:, u % 2 * 2 + b, 0:W], nsT[P, t, qt * 128:(qt + 1) * 128],
                                  nsT[P, 12 + 2 * b + t // 4, 0:W], start=True, stop=True)
                i.then_inc(at_qk, 1)

            def turn(u):
                t, half, qt = UNITS[u]
                pe.wait_ge(at_p, u + 1)
                if u >= 1:
                    pe.wait_ge(at_ev, u)
                for b in range(2):
                    for kt in range(qt + 1):
                        i = pe.transpose(ps[:, 4 + b, kt * 128:(kt + 1) * 128], prob[:, u % 3, b, kt * 128:(kt + 1) * 128], ident)
                i.then_inc(at_t, 1)

            def values(u):
                t, half, qt = UNITS[u]
                pe.wait_ge(at_ev, u + 1)
                if t >= 2 and half == 0 and qt == 0:
                    pe.wait_ge(at_o, t - 1)
                o = ps[64 * half:64 * half + 64, 6 + t % 2, qt * 128:(qt + 1) * 128]
                g = t // 4 * 2 + half
                for b in range(2):
                    for kt in range(qt + 1):
                        pe.matmul(o, vtok[:, kt, b * 256 + g * DH:b * 256 + (g + 1) * DH],
                                  probT[:, u % 3, b, kt * 128:(kt + 1) * 128], start=b == 0 and kt == 0, stop=False)
                pe.matmul(o, vcmp[:, g * DH:(g + 1) * DH], pcT[:, half * 8 + t, qt * 128:(qt + 1) * 128],
                          start=False, stop=True).then_inc(at_v, 1)

            for n in range(len(UNITS) + 3):
                if n < len(UNITS):
                    scores(n)
                if 2 <= n <= len(UNITS) + 1:
                    turn(n - 2)
                if n >= 3:
                    values(n - 3)
            pe.wait_ge(at_o, KT)
            linear("nout", rhs=mixT)
            rms_pe(4)
            pe.wait_ge(rms_out, 5 * KT)
            linear("sin")
            for c in range(4):
                pe.wait_ge(ba_done, c + 1)
                for ri in range(2):
                    for q in range(2):
                        if c or ri:
                            pe.wait_ge(bt_ev, c * 4 + ri * 2 + q - 1)
                        for g in range(4):
                            i = pe.transpose(ps[:, 4 + q, g * 128:(g + 1) * 128],
                                             baS[ri][:, (q * 4 + g) * 128:(q * 4 + g + 1) * 128], ident)
                        i.then_inc(bt_mm, 1)
            pe.wait_ge(uc_in, 64 * 16)
            pe.wait_ge(bt_ev, 16)
            for n in range(8):
                ri, q = n // 4, n % 4
                if n >= 2:
                    pe.wait_ge(w_ev, n - 1)
                for gp in range(8):
                    for g2 in range(2):
                        i = pe.matmul(ps[64 * g2:64 * g2 + 64, 4 + n % 2, gp * 64:gp * 64 + 64],
                                      BWT[ri][:, q * 8 + gp, 64 * g2:64 * g2 + 64], uc[:, 2 * (q * 8 + gp) + g2, :],
                                      start=True, stop=True)
                i.then_inc(w_mm, 1)
            for part in range(2):
                if part == 0:
                    pe.wait_ge(ca_done, 4)
                    pe.wait_ge(tile_evicted, TILE0["sin"] + 16)
                for n in range(4):
                    m = part * 4 + n
                    if m >= 2:
                        pe.wait_ge(k_ev, m - 1)
                    for q in range(4):
                        for half in range(2):
                            pair = m * 4 + q
                            P = slice(64 * half, 64 * half + 64)
                            bank = m % 2 * 2 + half
                            for ri in range(2):
                                pe.matmul(ps[0:SC, bank, q * 128:q * 128 + SC], bc[ri][P, pair, :], bc[2 + ri][P, pair, :],
                                          start=ri == 0, stop=ri == 1)
                            for ri in range(2):
                                i = pe.matmul(ps[0:SC, bank, q * 128 + SC:(q + 1) * 128], bc[ri][P, pair, :],
                                              CA[ri][P, pair, 0:112], start=ri == 0, stop=ri == 1)
                    i.then_inc(k_mm, 1)
                pe.wait_ge(t_in, (part + 1) * 8 * 16)
                pe.wait_ge(x_done, 1)
                for n in range(2):
                    m = part * 2 + n
                    if m >= 2:
                        pe.wait_ge(y_ev, m - 1)
                    for q in range(8):
                        for half in range(2):
                            pair = m * 8 + q
                            g = 2 * pair + half
                            P = slice(64 * half, 64 * half + 64)
                            bank = 4 + n * 2 + half
                            pe.matmul(ps[:, bank, q * 64:(q + 1) * 64], Tm[:, g - part * 32, :], uc[:, g, :],
                                      start=True, stop=False)
                            o = ps[:, bank, q * 64 + 1:(q + 1) * 64]
                            pe.matmul(o, CA[0][P, pair, :], wri[0][P, pair, 0:NC8 - 1], start=False, stop=False)
                            i = pe.matmul(o, CA[1][P, pair, :], wri[1][P, pair, 0:NC8 - 1], start=False, stop=True)
                    i.then_inc(y_mm, 1)
            pe.wait_ge(y_g, KT)
            linear("glu")
            pe.wait_ge(glu_o, KT)
            linear("sout", rhs=mixT)
            rms_pe(5)

        @block.scalar
        def _(act):
            count = [0]

            def own(i):
                count[0] += 1
                i.then_inc(acc_, 1)
                act.wait_ge(acc_, count[0])

            act.dma_start(hT[:, :, :], A["x"]).then_inc(s_x, 16)
            act.dma_start(consts[:, :], A["consts"]).then_inc(s_const, 16)
            act.dma_start(params[:, :], A["params"]).then_inc(s_param, 16)
            act.dma_start(w_ab, A["w_ab"]).then_inc(s_wab, 16)
            act.dma_start(bigB[:, 0:512], A["w_pool"]).then_inc(s_wpool, 16)

            def rms_act(n):
                for k in range(KT):
                    act.activation(uT[:, k, :], hT[:, k, :], ACT.Square).then_inc(rms_sq, 1)
                act.wait_ge(rms_sum, n + 1)
                act.activation(rms[:, :], ps[:, 4, :], ACT.Sqrt, scale=1.0 / D, bias=eps_ap).then_inc(rms_std, 1)

            act.wait_ge(s_x, 16)
            act.wait_ge(pads0, 3)
            rms_act(0)

            def evict(name, lo, hi, f):
                with act.Fori(lo // 4, hi // 4) as m:
                    for j in range(4):
                        act.wait_ge(slot_used, m * 4 + SLOT0[name] + j + 1)
                        f(m * 4 + j, ps[:, j, :]).then_inc(tile_evicted, 1)

            evict("inp", 0, 16, lambda n, p: act.activation(projT[:, n, PAD:PW], p, ACT.Copy))
            evict("inp", 16, 20, lambda n, p: act.activation(projT[:, n, PAD:PW], p, ACT.Silu))
            with act.Fori(0, 12) as n:
                act.wait_ge(conv_step, n * 4 + 4)
                act.activation(qkvT[:, n, :], qkvT[:, n, :], ACT.Silu).then_inc(conv_silu, 1)
            for g in range(4):
                act.wait_ge(pool_mm, g + 1)
                act.activation(mixT[:, g, :], ps[:, g, :], ACT.Copy, scale=param("pool_scale")[:, g:g + 1]).then_inc(pool_out, 1)
            act.wait_ge(conv_silu, 8)
            act.wait_ge(ab_ready, 1)
            act.wait_ge(conv_silu, 12)
            for i in range(8):
                act.activation(uT[:, i, :], qkvT[:, i, :], ACT.Square).then_inc(l2_sq, 1)
            for i in range(8):
                act.wait_ge(l2_sum, i + 1)
                if i >= 2:
                    act.wait_ge(l2_out, i - 1)
                act.activation(l2n[:, i % 2, :], ps[:, 4 + i % 2, :], ACT.Sqrt, bias=eps_ap).then_inc(l2_std, 1)
            act.wait_ge(gate_b, 1)
            own(act.activation(ge, ga, ACT.Exp, scale=-1.0))
            act.activation(gl, ge, ACT.Ln, bias=one_ap).then_inc(gate_a, 1)
            act.activation(nalog, param("a_log"), ACT.Exp).then_inc(gate_a, 1)
            act.activation(bta.rearrange("p (t h) -> p t h", h=4), abS[:, :, 4:8], ACT.Sigmoid).then_inc(gate_a, 1)
            act.wait_ge(gate_b, 4)
            act.activation(eg, ps[:, 0, 0:16], ACT.Exp).then_inc(gate_a, 1)
            act.activation(egl, ps[:, 0, 32:64], ACT.Exp).then_inc(gate_a, 1)
            act.activation(ekd, gl, ACT.Exp).then_inc(gate_a, 1)
            for tt in range(TT):
                act.wait_ge(row_dec, tt + 1)
                for h in range(NHG):
                    i = act.activation(hd(dec, tt, h), hd(dec, tt, h), ACT.Exp, bias=gc[:, tt * 4 + h:tt * 4 + h + 1])
                i.then_inc(dec_exp, 1)
            for tt in range(TT):
                act.wait_ge(row_mm, tt + 1)
                act.activation(A4T[:, tt, :], ps[:, 4 + tt, :], ACT.Exp).then_inc(row_exp, 1)
            for c in range(NCH):
                act.wait_ge(sc_o, c + 1)
                src = ps[:, 5 + 2 * (c % 2), 0:NHG * CH].rearrange("p (h c) -> p h c", c=CH)
                act.activation(gdnO[:, :, c * CH:(c + 1) * CH], src, ACT.Copy).then_inc(sc_oe, 1)
            act.wait_ge(sc_oe, NCH)
            sq = urr[1].rearrange("p a b -> p (a b)")
            for h in range(NHG):
                act.activation(sq[:, h * T:(h + 1) * T], gdnO[:, h, :], ACT.Square).then_inc(go_sq, 1)
            for h in range(NHG):
                act.wait_ge(go_sum, h + 1)
                act.activation(qkvT[:, h, :], ps[:, h, :], ACT.Sqrt, scale=1.0 / 128, bias=eps_ap).then_inc(go_std, 1)
            act.wait_ge(tile_evicted, TILE0["out"] + 8)
            rms_act(1)
            with act.Fori(0, FT // 4) as m:
                for j in range(4):
                    act.wait_ge(slot_used, m * 4 + SLOT0["up"] + j + 1)
                    act.activation(mixT[:, j, :], ps[:, j, :], ACT.Relu).then_inc(tile_evicted, 1)
                    act.wait_ge(tile_evicted, m * 4 + TILE0["up"] + j + 1)
                    act.activation(ffT[:, m * 4 + j, :], mixT[:, j, :], ACT.Square).then_inc(ff_sq, 1)
            act.wait_ge(tile_evicted, TILE0["down"] + 8)
            rms_act(2)
            act.wait_ge(rms_out, 3 * KT)
            rms_act(3)
            evict("nsa", 0, 8, lambda n, p: act.activation(nsT[:, n, :], p, ACT.Copy, scale=DH ** -0.5))
            evict("nsa", 8, 16, lambda n, p: act.activation(nsT[:, n, :], p, ACT.Copy))
            for tt in range(TT):
                if tt < TT - 1:
                    act.wait_ge(v_done, tt + 1)
                else:
                    act.wait_ge(slot_used, SLOT0["val"] + 4)
                act.activation(vtok[:, tt, :], ps[:, tt, :], ACT.Copy).then_inc(tile_evicted, 1)
            act.wait_ge(g_mm, 1)
            act.activation(small[:, 308:500], ps[:, 5, 0:192], ACT.Sigmoid).then_inc(g_out, 1)
            evict("zed", 0, 8, lambda n, p: act.activation(zsT[:, n, :], p, ACT.Silu))
            for x in range(2):
                act.wait_ge(cmp_h, x + 1)
                src = ps[:, 4:8:2, 0:128].rearrange("p h (t c) -> p h t c", c=64)[:, :, :, 0:2 * NCMP]
                for half in range(2):
                    i = act.activation(hid[x][:, :, half, :], src[:, half, :, :], ACT.Silu)
                i.then_inc(cmp_act, 1)
            for tt in range(TT):
                act.wait_ge(cs_x, tt + 1)
                f = pc[tt].rearrange("p h n -> p (h n)")
                act.wait_ge(cs_sub, tt + 1)
                act.activation(f, f, ACT.Exp).then_inc(cs_exp, 1)
            for n in range(16):
                act.wait_ge(cs_t, n + 1)
                tt, b = n // 4, n % 4
                act.activation(pcT[:, b * 4:b * 4 + 4, tt * 128:(tt + 1) * 128],
                               ps[0:NCMP, 4 + n % 2, :].rearrange("p (h q) -> p h q", q=128), ACT.Copy).then_inc(cs_ev, 1)
            for n in range(len(UNITS) + 2):
                if n < len(UNITS):
                    t, half, qt = UNITS[n]
                    W = (qt + 1) * 128
                    act.wait_ge(at_m, n + 1)
                    for b in range(2):
                        i = act.activation(prob[:, n % 3, b, 0:W], prob[:, n % 3, b, 0:W], ACT.Exp,
                                           bias=anmax[:, n % 3, b:b + 1], accum_out=asum[:, n % 3, b:b + 1])
                    i.then_inc(at_e, 1)
                if n >= 2:
                    u = n - 2
                    W = (UNITS[u][2] + 1) * 128
                    act.wait_ge(at_t, u + 1)
                    if u >= 3:
                        act.wait_ge(at_v, u - 2)
                    act.activation(probT[:, u % 3, :, 0:W], ps[:, 4:6, 0:W], ACT.Copy).then_inc(at_ev, 1)
            act.wait_ge(tile_evicted, TILE0["nout"] + 8)
            for x, name in enumerate(("ssm_b_re", "ssm_b_im", "ssm_c_re", "ssm_c_im")):
                act.dma_start(bc[x].rearrange("p g c -> p (g c)"), A[name]).then_inc(s_bc, 16)
            rms_act(4)
            act.activation(pk[0], param("log_dt"), ACT.Exp).then_inc(ssm_a, 1)
            act.wait_ge(ssm_b, 1)
            for k in range(9):
                i = act.activation(mag[:, k, :], pk[1], ACT.Exp, scale=float(k))
            i.then_inc(ssm_a, 1)
            act.activation(pk[6], pk[5], ACT.Sin).then_inc(ssm_a, 1)
            act.activation(pk[7], pk[5], ACT.Sin, scale=0.5).then_inc(ssm_a, 1)
            evict("sin", 0, 8, lambda n, p: act.activation(
                suP[:, n, :].rearrange("p (j c) -> p c j", c=NC8), p.rearrange("p (c j) -> p c j", j=FR), ACT.Copy))
            act.wait_ge(tile_evicted, TILE0["sin"] + 8)
            ucg = uc.rearrange("p (t g) c -> p t g c", g=8)
            for g in range(8):
                for j in range(FR):
                    act.dma_start(ucg[16 * j:16 * j + 16, :, g, :], suP[16 * g:16 * g + 16, :, j * NC8:(j + 1) * NC8]).then_inc(uc_in, 16)
            evict("sin", 8, 16, lambda n, p: act.activation(szT[:, n - 8, :], p, ACT.Silu))
            for c in range(4):
                for ri in range(2):
                    for q in range(2):
                        act.wait_ge(bt_mm, c * 4 + ri * 2 + q + 1)
                        act.activation(BWT[ri].rearrange("p g c -> p (g c)")[:, (c * 8 + q * 4) * 128:(c * 8 + q * 4 + 4) * 128],
                                       ps[:, 4 + q, :], ACT.Copy).then_inc(bt_ev, 1)
            act.wait_ge(ca_done, 4)
            for n in range(8):
                ri, q = n // 4, n % 4
                act.wait_ge(w_mm, n + 1)
                act.activation(wri[ri].rearrange("p g c -> p (g c)")[:, q * 512:(q + 1) * 512], ps[:, 4 + n % 2, :], ACT.Copy).then_inc(w_ev, 1)
            act.wait_ge(rot_in, 1)
            for part in range(2):
                for n in range(4):
                    m = part * 4 + n
                    act.wait_ge(k_mm, m + 1)
                    if part == 1 and n == 0:
                        act.wait_ge(t_in, 8 * 16)
                    act.activation(Kl[:, n * 8:n * 8 + 8, :].rearrange("p (q h) c -> p h q c", h=2),
                                   ps[0:SC, m % 2 * 2:m % 2 * 2 + 2, :].rearrange("p h (q c) -> p h q c", c=128),
                                   ACT.Copy).then_inc(k_ev, 1)
                act.wait_ge(k_ev, (part + 1) * 4)
                act.wait_ge(t_zero, part + 1)
                for j in range(FR):
                    act.dma_start(Tm[16 * j:16 * j + 16, :, 16 * j:128], Kl[:, :, 0:128 - 16 * j]).then_inc(t_in, 16)
                for n in range(2):
                    m = part * 2 + n
                    act.wait_ge(y_mm, m + 1)
                    act.activation(uc[:, m * 16:m * 16 + 16, :].rearrange("p (q h) c -> p h q c", h=2),
                                   ps[:, 4 + n * 2:6 + n * 2, :].rearrange("p h (q c) -> p h q c", c=NC8),
                                   ACT.Copy).then_inc(y_ev, 1)
            act.wait_ge(y_ev, 4)
            for g in range(8):
                for j in range(FR):
                    act.dma_start(yF[16 * g:16 * g + 16, :, j * NC8:(j + 1) * NC8], ucg[16 * j:16 * j + 16, :, g, :]).then_inc(y_in, 16)
            for k in range(KT):
                act.wait_ge(y_d, k + 1)
                act.activation(uT[:, k, :], uT[:, k, :], ACT.Gelu_apprx_tanh).then_inc(y_g, 1)
            with act.Fori(0, 4) as m:
                for x in range(2):
                    act.wait_ge(slot_used, m * 4 + SLOT0["glu"] + 2 * x + 2)
                    act.wait_ge(tile_evicted, m * 4 + TILE0["glu"] + 2 * x - 2)
                    act.activation(sg[:, x, :], ps[:, 2 * x + 1, :], ACT.Sigmoid).then_inc(glu_s, 1)
            act.wait_ge(tile_evicted, NTILE)
            rms_act(5)
            act.wait_ge(rms_out, 6 * KT)
            act.dma_start(out_dram, hT[:, :, :]).then_inc(out_done, 16)
            act.wait_ge(out_done, 16)

        @block.gpsimd
        def _(pool):
            count = [0]

            def own(i):
                count[0] += 1
                i.then_inc(plc, 1)
                pool.wait_ge(plc, count[0])

            pool.memset(projT[:, :, 0:PAD], 0.0).then_inc(pads0, 1)
            pool.memset(small[:, 304:305], EPS).then_inc(pads0, 1)
            pool.memset(small[:, 305:306], 1.0).then_inc(pads0, 1)
            pool.wait_ge(pads0, 3)
            pool.wait_ge(s_const, 16)
            for g in range(4):
                pool.wait_ge(tile_evicted, g + 1)
                w, src = 1, projT[:, g, :]
                for d in range(g + 1):
                    dst = ptmp[d % 2]
                    own(pool.tensor_tensor(dst[:, 2 * w - 1:PW], src[:, 2 * w - 1:PW], src[:, w - 1:PW - w], ALU.add))
                    src, w = dst, 2 * w
                mean = ptmp[(g + 1) % 2]
                own(pool.tensor_scalar(mean[:, PAD:PW], src[:, PAD:PW], 1.0 / w, 0.0, ALU.mult, ALU.add))
                own(pool.tensor_tensor(mean[:, PAD:PAD + w], src[:, PAD:PAD + w], const("invcount")[:, g * PAD:g * PAD + w], ALU.mult))
                i = pool.tensor_tensor(pooled[:, g, :], mean[:, PAD:PW], projT[:, g, PAD:PW], ALU.subtract)
                i.then_inc(pooled_done, 1)
                pool.wait_ge(pooled_done, g + 1)
            pool.wait_ge(tile_evicted, TILE0["out"] + 8)
            for x, n in enumerate("kv"):
                pool.dma_start(w1[x], A[f"cmp_{n}_w1"]).then_inc(s_w1[x], 16)
                pool.dma_start(w2[x], A[f"cmp_{n}_w2"]).then_inc(s_w2, 16)
            pool.dma_start(w_gate, A["w_gate"]).then_inc(s_wgate, 16)
            pool.wait_ge(cmp_h, 2)
            for n in range(NH):
                t, half = n // 2, n % 2
                if n >= 2:
                    pool.wait_ge(at_s, 4 * (n - 1))
                pool.tensor_scalar(dsl[:, n % 2, :], const("dist"), const("slope")[:, half * 8 + t:half * 8 + t + 1], 0.0,
                                   ALU.mult, ALU.add).then_inc(ds_ready, 1)

        @block.vector
        def _(dve):
            count = [0]

            def own(i):
                count[0] += 1
                i.then_inc(dvc, 1)
                dve.wait_ge(dvc, count[0])

            def rms_dve(n, weight, dst):
                dve.wait_ge(rms_std, n + 1)
                own(dve.reciprocal(rms[:, :], rms[:, :]))
                for k in range(KT):
                    dve.scalar_tensor_tensor(dst[:, k, :], hT[:, k, :], param(weight)[:, k:k + 1], rms[:, :],
                                             ALU.mult, ALU.mult).then_inc(rms_out, 1)

            def residual(name):
                with dve.Fori(0, 2) as m:
                    for j in range(4):
                        per = SLOTS[name] // TILES[name]
                        dve.wait_ge(slot_used, (m * 4 + j + 1) * per + SLOT0[name])
                        dve.tensor_tensor(hT[:, m * 4 + j, :], hT[:, m * 4 + j, :], ps[:, j, :], ALU.add).then_inc(tile_evicted, 1)

            dve.wait_ge(s_param, 16)
            dve.wait_ge(s_x, 16)
            rms_dve(0, "norm_mix", uT)
            cw = param("conv")
            with dve.Fori(0, 12) as n:
                dve.wait_ge(tile_evicted, n + 5)
                x = projT[:, n + 4, :]
                y = qkvT[:, n, :]
                dve.tensor_scalar(y, projT[:, n + 4, PAD - 3:PW - 3], cw[:, bass.ds(n * CONV, 1)], None, ALU.mult).then_inc(conv_step, 1)
                for i in range(1, CONV):
                    dve.wait_ge(conv_step, n * 4 + i)
                    dve.scalar_tensor_tensor(y, projT[:, n + 4, PAD - 3 + i:PW - 3 + i], cw[:, bass.ds(n * CONV + i, 1)], y,
                                             ALU.mult, ALU.add).then_inc(conv_step, 1)
            dve.wait_ge(ab_ready, 1)
            dve.tensor_copy(abS.rearrange("p t c -> p (t c)"), ps[:, 5, 0:32]).then_inc(ab_copied, 1)
            dve.wait_ge(ab_copied, 1)
            own(dve.tensor_tensor(gx.rearrange("p (t h) -> p t h", h=4), abS[:, :, 0:4],
                                  param("dt_bias").rearrange("p (t h) -> p t h", h=4), ALU.add))
            own(dve.tensor_scalar(gg, gx, -1.0, None, ALU.mult))
            dve.tensor_tensor(ga, gx, gg, ALU.max).then_inc(gate_b, 1)
            for i in range(8):
                dve.wait_ge(l2_std, i + 1)
                own(dve.reciprocal(l2n[:, i % 2, :], l2n[:, i % 2, :]))
                dve.scalar_tensor_tensor(qkvT[:, i, :], qkvT[:, i, :], 128 ** -0.5 if i < 4 else 1.0, l2n[:, i % 2, :],
                                         ALU.mult, ALU.mult).then_inc(l2_out, 1)
            dve.wait_ge(gate_a, 3)
            own(dve.scalar_tensor_tensor(gx, gx, 0.0, gl, ALU.max, ALU.add))
            dve.scalar_tensor_tensor(gg, gx, -1.0, nalog, ALU.mult, ALU.mult).then_inc(gate_b, 1)
            dve.wait_ge(gate_b, 2)
            dve.wait_ge(pool_mm, 4)
            dve.tensor_copy(gB.rearrange("p t (h c) -> p (t h) c", c=128),
                            gg.unsqueeze(2).to_broadcast([128, 16, 128])).then_inc(gate_b, 1)
            dve.wait_ge(gate_mm, 1)
            own(dve.tensor_copy(gc, ps[:, 0, 0:16]))
            dve.tensor_tensor(gl, ps[:, 0, 16:32], gc, ALU.subtract).then_inc(gate_b, 1)
            dve.wait_ge(gate_a, 4)
            own(dve.tensor_tensor(beg, bta, eg, ALU.mult))
            mneg = const("maskneg").unsqueeze(1).to_broadcast([128, 4, 128])
            for tt in range(TT):
                dve.wait_ge(row_mm, tt + 1)
                dve.scalar_tensor_tensor(dec[:, tt, :].rearrange("p (h c) -> p h c", c=128),
                                         ps[:, 4 + tt, :].rearrange("p (h c) -> p h c", c=128), -1.0, mneg,
                                         ALU.mult, ALU.add).then_inc(row_dec, 1)
            dve.wait_ge(dec_exp, TT)
            dve.wait_ge(gate_a, 6)

            def masked(dst, tt, mask):
                return dve.tensor_tensor(dst[:, tt, :].rearrange("p (h c) -> p h c", c=128),
                                         Mm[:, tt, :].rearrange("p (h c) -> p h c", c=128),
                                         const(mask).unsqueeze(1).to_broadcast([128, 4, 128]), ALU.mult)

            for r, name in enumerate(ROUNDS):
                for tt in range(TT):
                    dve.wait_ge(rnd_mm, 4 * r + tt + 1)
                    p = ps[:, 4 + tt, :]

                    def by_head(dst, scalars):
                        for h in range(NHG):
                            i = dve.tensor_scalar(hd(dst, tt, h), p[:, h * 128:(h + 1) * 128],
                                                  scalars[:, tt * 4 + h:tt * 4 + h + 1], None, ALU.mult)
                        return i

                    if name == "attn":
                        i = dve.tensor_tensor(aS[:, tt, :], p, dec[:, tt, :], ALU.mult)
                    elif name == "attnT":
                        i = dve.tensor_copy(aiT[:, tt, :], p)
                    elif name == "ktok":
                        by_head(kd, ekd)
                        i = by_head(kbe, beg)
                    elif name == "vtok":
                        i = by_head(vb, bta)
                    elif name == "gram":
                        for h in range(NHG):
                            i = dve.scalar_tensor_tensor(hd(Mm, tt, h), p[:, h * 128:(h + 1) * 128],
                                                         bta[:, tt * 4 + h:tt * 4 + h + 1], hd(dec, tt, h),
                                                         ALU.mult, ALU.mult)
                        own(i)
                        i = masked(Aa, tt, "neg16")
                    elif name == "AT":
                        dve.tensor_copy(AT[:, tt, :], p)
                        i = dve.tensor_tensor(Rr[:, tt, :].rearrange("p (h c) -> p h c", c=128),
                                              p.rearrange("p (h c) -> p h c", c=128),
                                              ident.unsqueeze(1).to_broadcast([128, 4, 128]), ALU.add)
                    elif name in ("R2", "R4", "R8"):
                        i = dve.tensor_tensor(Rr[:, tt, :], p, Rr[:, tt, :], ALU.add)
                    elif name in ("R32", "R64"):
                        i = dve.tensor_tensor(Rr[:, tt, :], Rr[:, tt, :], p, ALU.subtract)
                    elif name == "A4T":
                        dve.tensor_copy(A4T[:, tt, :], p)
                        i = masked(Bm32, tt, "low32")
                    elif name == "A8":
                        dve.tensor_copy(A8[:, tt, :], p)
                        i = masked(Bm64, tt, "low64")
                    else:
                        dst = {"A2": A2, "A2T": A2T, "A4": A4, "X32": Xx, "X64": Xx, "Y32": Yy, "Y64": Yy,
                               "val": val, "kcT": kcT}[name]
                        i = dve.tensor_copy(dst[:, tt, :], p)
                    i.then_inc(rnd_ev, 1)
                if name == "attn":
                    dve.wait_ge(row_exp, TT)
                    for tt in range(TT):
                        q = qkvT[:, 0:4, tt * 128:(tt + 1) * 128]
                        dve.tensor_tensor(q, q, A4T[:, tt, :].rearrange("p (h c) -> p h c", c=128), ALU.mult).then_inc(qd_done, 1)
            dve.memset(Sst[:, 0, :], 0.0).then_inc(sc_s, 1)
            for c in range(NCH):
                tt, half = c // 2, c % 2
                P = slice(64 * half, 64 * half + 64)
                dve.wait_ge(sc_k, c + 1)
                if c >= 2:
                    dve.wait_ge(sc_o, c - 1)
                dve.tensor_tensor(vnew[P, :], val[P, tt, :], ps[P, 4, :], ALU.subtract).then_inc(sc_v, 1)
                dve.wait_ge(sc_u, c + 1)
                if c >= 1:
                    dve.wait_ge(sc_o, c)
                for h in range(NHG):
                    i = dve.scalar_tensor_tensor(Sst[:, (c + 1) % 2, h * 128:(h + 1) * 128], Sst[:, c % 2, h * 128:(h + 1) * 128],
                                                 egl[:, half * 16 + tt * 4 + h:half * 16 + tt * 4 + h + 1],
                                                 ps[:, 6, h * 128:(h + 1) * 128], ALU.mult, ALU.add)
                i.then_inc(sc_s, 1)
            dve.wait_ge(sc_s, NCH + 1)
            dve.wait_ge(sc_o, NCH)
            for h in range(NHG):
                dve.wait_ge(go_std, h + 1)
                own(dve.reciprocal(qkvT[:, h, :], qkvT[:, h, :]))
                own(dve.scalar_tensor_tensor(gdnO[:, h, :], gdnO[:, h, :], param("gdn_norm"), qkvT[:, h, :], ALU.mult, ALU.mult))
                dve.tensor_tensor(mixT[:, 4 + h, :], gdnO[:, h, :], projT[:, 16 + h, PAD:PW], ALU.mult).then_inc(go_out, 1)
            residual("out")
            rms_dve(1, "norm_mlp", uT)
            residual("down")
            rms_dve(2, "norm_final", hT)
            rms_dve(3, "l0_norm", uT)
            for x, name in enumerate(("kpe", "vpe")):
                dve.wait_ge(tile_evicted, TILE0["nsa"] + 16)
                if x:
                    dve.wait_ge(cmp_h, 1)
                for gp in range(2):
                    row = nsT[:, 8 + 2 * x + gp, :]
                    two = row.rearrange("p (n s) -> p s n", s=CMPS)
                    pe_ = param(name).unsqueeze(2).to_broadcast([128, CMPB, NCMP])
                    for o in range(2):
                        i = dve.tensor_tensor(blk[:, gp, o * CMPS:(o + 1) * CMPS, :], two[:, :, o:o + NCMP],
                                              pe_[:, o * CMPS:(o + 1) * CMPS, :], ALU.add)
                i.then_inc(blk_done, 1)
            dve.wait_ge(cmp_mm, 1)
            dve.tensor_copy(kcmp.rearrange("p g n -> p (g n)"), ps[:, 7, 0:2 * NCMP]).then_inc(cmp_out, 1)
            dve.wait_ge(cmp_mm, 2)
            dve.tensor_copy(vcmp, ps[0:NCMP, 5, 0:NG * DH]).then_inc(cmp_out, 1)
            dve.wait_ge(cmp_h, 2)
            dve.wait_ge(g_out, 1)

            def wide(x):
                return x.unsqueeze(2).to_broadcast([128, NH, NCMP])

            for tt in range(TT):
                cols = slice(tt * NCMP, (tt + 1) * NCMP)
                own(dve.tensor_tensor(pc[tt], wide(const("slope")), const("cdist")[:, cols].unsqueeze(1).to_broadcast([128, NH, NCMP]), ALU.mult))
                dve.wait_ge(cs_mm, tt + 1)
                two = pc[tt].rearrange("p (a h) n -> p a (h n)", a=2)
                dve.tensor_tensor(two, two, ps[:, tt % 2 * 2:tt % 2 * 2 + 2, 0:8 * NCMP], ALU.add).then_inc(cs_x, 1)
                dve.wait_ge(cs_x, tt + 1)
                own(dve.tensor_reduce(cm, pc[tt], AX.X, ALU.max))
                dve.tensor_tensor(pc[tt], pc[tt], wide(cm), ALU.subtract).then_inc(cs_sub, 1)
            for tt in range(TT):
                cols = slice(tt * NCMP, (tt + 1) * NCMP)
                dve.wait_ge(cs_exp, tt + 1)
                own(dve.tensor_tensor(pc[tt], pc[tt], const("cmask")[:, cols].unsqueeze(1).to_broadcast([128, NH, NCMP]), ALU.mult))
                own(dve.tensor_reduce(cs_, pc[tt], AX.X, ALU.add))
                own(dve.tensor_scalar(cs_, cs_, 1e-30, None, ALU.max))
                own(dve.reciprocal(cs_, cs_))
                own(dve.tensor_tensor(cs_, cs_, gate[:, tt, 0, :], ALU.mult))
                dve.tensor_tensor(pc[tt], pc[tt], wide(cs_), ALU.mult).then_inc(cs_p, 1)

            def shift(u):
                t, half, qt = UNITS[u]
                W = (qt + 1) * 128
                n = u // 4
                dve.wait_ge(ds_ready, n + 1)
                dve.wait_ge(at_qk, u + 1)
                if u >= 3:
                    dve.wait_ge(at_t, u - 2)
                for b in range(2):
                    i = dve.tensor_tensor_reduce(prob[:, u % 3, b, 0:W], ps[:, u % 2 * 2 + b, 0:W],
                                                 dsl[:, n % 2, 512 - W:512], 1.0, -3e38, ALU.add, ALU.max,
                                                 amax[:, u % 3, b:b + 1])
                i.then_inc(at_s, 1)
                dve.wait_ge(at_s, u + 1)
                dve.tensor_scalar(anmax[:, u % 3, :], amax[:, u % 3, :], -1.0, None, ALU.mult).then_inc(at_m, 1)

            def weigh(u):
                t, half, qt = UNITS[u]
                W = (qt + 1) * 128
                dve.wait_ge(at_e, u + 1)
                own(dve.reciprocal(asum[:, u % 3, :], asum[:, u % 3, :]))
                own(dve.tensor_tensor(asum[:, u % 3, :], asum[:, u % 3, :], gate[:, qt, 1:3, half * 8 + t], ALU.mult))
                for b in range(2):
                    i = dve.tensor_scalar(prob[:, u % 3, b, 0:W], prob[:, u % 3, b, 0:W], asum[:, u % 3, b:b + 1], None, ALU.mult)
                i.then_inc(at_p, 1)

            def finish(t):
                dve.wait_ge(at_v, 8 * (t + 1))
                dve.tensor_tensor(mixT[:, t, :], ps[:, 6 + t % 2, :], zsT[:, t, :], ALU.mult).then_inc(at_o, 1)

            for n in range(len(UNITS) + 1):
                if n < len(UNITS):
                    shift(n)
                if n >= 1:
                    weigh(n - 1)
                if n >= 12 and n % 8 == 4:
                    finish(n // 8 - 1)
            finish(KT - 1)
            residual("nout")
            rms_dve(4, "l1_norm", uT)
            dt, x_, lre, th, r_, s1, sh, c1, den, nr, cr, ci, t1, t2 = (
                pk[0], pk[1], pk[2], pk[3], pk[5], pk[6], pk[7], pk[8], pk[9], pk[10], pk[11], pk[12], pk[13], pk[14])
            dve.wait_ge(ssm_a, 1)
            own(dve.tensor_scalar(lre, param("lre"), -1e-4, None, ALU.min))
            own(dve.tensor_tensor(th, param("lim"), dt, ALU.mult))
            own(dve.tensor_tensor(x_, lre, dt, ALU.mult))
            own(dve.tensor_scalar(t1, th, 1.0 / (2 * np.pi), ROUND, ALU.mult, ALU.add))
            own(dve.tensor_scalar(t1, t1, ROUND, None, ALU.subtract))
            own(dve.scalar_tensor_tensor(r_, t1, -TWO_PI[0], th, ALU.mult, ALU.add))
            own(dve.scalar_tensor_tensor(r_, t1, -TWO_PI[1], r_, ALU.mult, ALU.add))
            own(dve.scalar_tensor_tensor(r_, t1, -TWO_PI[2], r_, ALU.mult, ALU.add))
            dve.tensor_scalar(r_, r_, PI32, -PI32, ALU.min, ALU.max).then_inc(ssm_b, 1)
            dve.wait_ge(ssm_a, 4)
            own(dve.tensor_tensor(c1, sh, sh, ALU.mult))
            own(dve.tensor_scalar(c1, c1, -2.0, 1.0, ALU.mult, ALU.add))
            U, V, Pr, Pi = ptab

            def cmul(o_re, o_im, a_re, a_im, b_re, b_im, ta, tb, last=None):
                own(dve.tensor_tensor(ta, a_re, b_re, ALU.mult))
                own(dve.tensor_tensor(tb, a_im, b_im, ALU.mult))
                own(dve.tensor_tensor(o_re, ta, tb, ALU.subtract))
                own(dve.tensor_tensor(ta, a_re, b_im, ALU.mult))
                own(dve.tensor_tensor(tb, a_im, b_re, ALU.mult))
                i = dve.tensor_tensor(o_im, ta, tb, ALU.add)
                if last is None:
                    own(i)
                return i

            dve.memset(U[:, 0, :], 1.0)
            dve.memset(V[:, 0, :], 0.0)
            own(dve.tensor_copy(U[:, 1, :], c1))
            own(dve.tensor_copy(V[:, 1, :], s1))
            for m in (1, 2, 4):
                bcast = lambda x: x[:, m:m + 1, :].to_broadcast([128, m, NPAIR])
                tv = [tmpS[q][:, 0:m * NPAIR].rearrange("p (m g) -> p m g", g=NPAIR) for q in range(2)]
                cmul(U[:, m + 1:2 * m + 1, :], V[:, m + 1:2 * m + 1, :], U[:, 1:m + 1, :], V[:, 1:m + 1, :],
                     bcast(U), bcast(V), *tv)
            own(dve.tensor_tensor(Pr, U, mag, ALU.mult))
            own(dve.tensor_tensor(Pi, V, mag, ALU.mult))
            own(dve.tensor_tensor(den, lre, lre, ALU.mult))
            own(dve.tensor_tensor(t1, param("lim"), param("lim"), ALU.mult))
            own(dve.tensor_tensor(den, den, t1, ALU.add))
            own(dve.reciprocal(den, den))
            own(dve.tensor_scalar(nr, Pr[:, 1, :], -1.0, None, ALU.add))
            own(dve.tensor_tensor(t1, nr, lre, ALU.mult))
            own(dve.tensor_tensor(t2, Pi[:, 1, :], param("lim"), ALU.mult))
            own(dve.tensor_tensor(cr, t1, t2, ALU.add))
            own(dve.tensor_tensor(cr, cr, den, ALU.mult))
            own(dve.tensor_tensor(t1, Pi[:, 1, :], lre, ALU.mult))
            own(dve.tensor_tensor(t2, nr, param("lim"), ALU.mult))
            own(dve.tensor_tensor(ci, t1, t2, ALU.subtract))
            own(dve.tensor_tensor(ci, ci, den, ALU.mult))
            dve.wait_ge(s_bc, 64)
            wide16 = lambda x: x.unsqueeze(2).to_broadcast([128, NPAIR, SC])
            tv = [tmpS[q][:, 0:512].rearrange("p (g c) -> p g c", c=SC) for q in range(2)]
            own(dve.tensor_tensor(tv[0], bc[0], wide16(cr), ALU.mult))
            own(dve.tensor_tensor(tv[1], bc[1], wide16(ci), ALU.mult))
            own(dve.tensor_tensor(tv[0], tv[0], tv[1], ALU.subtract))
            own(dve.tensor_tensor(tv[1], bc[0], wide16(ci), ALU.mult))
            own(dve.tensor_tensor(bc[1], bc[1], wide16(cr), ALU.mult))
            own(dve.tensor_tensor(bc[1], bc[1], tv[1], ALU.add))
            own(dve.tensor_copy(bc[0], tv[0]))
            own(dve.tensor_scalar(bc[3], bc[3], -1.0, None, ALU.mult))
            Er, Ei = Eri
            own(dve.tensor_copy(rK[0], U[:, 8, :]))
            own(dve.tensor_copy(rK[1], V[:, 8, :]))
            own(dve.tensor_copy(mag8, mag[:, 8, :]))
            own(dve.memset(Er[:, :, 0], 1.0))
            own(dve.memset(Ei[:, :, 0], 0.0))
            m = 1
            while m < NC8:
                bcast = lambda x: x.unsqueeze(2).to_broadcast([128, NPAIR, m])
                tv = [tmpS[q][:, 0:m * NPAIR].rearrange("p (g m) -> p g m", m=m) for q in range(2)]
                cmul(Er[:, :, m:2 * m], Ei[:, :, m:2 * m], Er[:, :, 0:m], Ei[:, :, 0:m], bcast(rK[0]), bcast(rK[1]), *tv)
                if 2 * m < NC8:
                    own(dve.tensor_tensor(rK[2], rK[0], rK[0], ALU.mult))
                    own(dve.tensor_tensor(rK[3], rK[1], rK[1], ALU.mult))
                    own(dve.tensor_tensor(rK[4], rK[0], rK[1], ALU.mult))
                    own(dve.tensor_tensor(rK[0], rK[2], rK[3], ALU.subtract))
                    own(dve.tensor_scalar(rK[1], rK[4], 2.0, None, ALU.mult))
                m *= 2
            for c in range(4):
                gs = slice(c * 8, c * 8 + 8)
                bb = [bc[q][:, gs, :].unsqueeze(2).to_broadcast([128, 8, FR, SC]) for q in range(2)]
                pp = [prev[q][:, gs, :].unsqueeze(3).to_broadcast([128, 8, FR, SC]) for q in range(2)]
                if c == 0:
                    for j in range(FR):
                        dve.tensor_copy(prev[0][:, :, j], Pr[:, FR - 1 - j, :])
                        i = dve.tensor_copy(prev[1][:, :, j], Pi[:, FR - 1 - j, :])
                    own(i)
                else:
                    dve.wait_ge(bt_mm, 4 * c)
                o = [x.rearrange("p (g j c) -> p g j c", g=8, j=FR) for x in baS]
                tv = [x.rearrange("p (g j c) -> p g j c", g=8, j=FR) for x in tmpS]
                i = cmul(o[0], o[1], pp[0], pp[1], bb[0], bb[1], *tv, last=True)
                i.then_inc(ba_done, 1)
                dve.wait_ge(ba_done, c + 1)
            dve.wait_ge(slot_used, SLOT0["sin"] + 16)
            dve.wait_ge(bt_mm, 16)
            for c in range(4):
                gs = slice(c * 8, c * 8 + 8)
                cc = [bc[2 + q][:, gs, :].unsqueeze(2).to_broadcast([128, 8, FR, SC]) for q in range(2)]
                pp = [p[:, 1:9, gs].rearrange("p k g -> p g k").unsqueeze(3).to_broadcast([128, 8, FR, SC]) for p in (Pr, Pi)]
                o = [CA[q][:, gs, :].rearrange("p g (k c) -> p g k c", c=SC) for q in range(2)]
                tv = [x.rearrange("p (g j c) -> p g j c", g=8, j=FR) for x in tmpS]
                own(dve.tensor_tensor(tv[0], pp[0], cc[0], ALU.mult))
                own(dve.tensor_tensor(tv[1], pp[1], cc[1], ALU.mult))
                own(dve.tensor_tensor(o[0], tv[0], tv[1], ALU.add))
                own(dve.tensor_tensor(tv[0], pp[0], cc[1], ALU.mult))
                own(dve.tensor_tensor(tv[1], pp[1], cc[0], ALU.mult))
                dve.tensor_tensor(o[1], tv[0], tv[1], ALU.subtract).then_inc(ca_done, 1)
                dve.wait_ge(ca_done, c + 1)
            own(dve.tensor_copy(rho, mag8.unsqueeze(2).to_broadcast([128, NPAIR, NC8])))
            own(dve.memset(rho[:, :, 0], 0.0))
            flat = lambda x: x.rearrange("p g c -> p (g c)")
            Ef = [flat(x) for x in Eri]
            wf = [flat(x) for x in wri]
            dve.wait_ge(w_ev, 8)
            own(dve.tensor_tensor(rot[0], wf[0], Ef[1], ALU.mult))
            own(dve.tensor_tensor(rot[1], wf[1], Ef[1], ALU.mult))
            own(dve.tensor_tensor(wf[0], wf[0], Ef[0], ALU.mult))
            own(dve.tensor_tensor(wf[1], wf[1], Ef[0], ALU.mult))
            own(dve.tensor_tensor(wf[0], wf[0], rot[1], ALU.add))
            dve.tensor_tensor(wf[1], wf[1], rot[0], ALU.subtract).then_inc(rot_in, 1)
            dve.wait_ge(rot_in, 1)
            dve.memset(Tm, 0.0).then_inc(t_zero, 1)
            own(dve.tensor_tensor_scan(wf[0], flat(rho), wf[0], 0.0, ALU.mult, ALU.add))
            own(dve.tensor_tensor_scan(wf[1], flat(rho), wf[1], 0.0, ALU.mult, ALU.add))
            own(dve.tensor_tensor(flat(rho), wf[1], Ef[1], ALU.mult))
            own(dve.tensor_tensor(Ef[1], wf[0], Ef[1], ALU.mult))
            own(dve.tensor_tensor(wf[0], wf[0], Ef[0], ALU.mult))
            own(dve.tensor_tensor(wf[1], wf[1], Ef[0], ALU.mult))
            own(dve.tensor_tensor(wf[0], wf[0], flat(rho), ALU.subtract))
            dve.tensor_tensor(wf[1], wf[1], Ef[1], ALU.add).then_inc(x_done, 1)
            dve.wait_ge(y_mm, 2)
            dve.memset(Tm, 0.0).then_inc(t_zero, 1)
            dve.wait_ge(y_in, 64 * 16)
            for k in range(KT):
                o = uT[:, k, :].rearrange("p (c j) -> p j c", j=FR)
                u_ = suP[:, k, :].rearrange("p (j c) -> p j c", c=NC8)
                y_ = yF[:, k, :].rearrange("p (j c) -> p j c", c=NC8)
                dve.scalar_tensor_tensor(o, u_, param("d_skip")[:, k:k + 1], y_, ALU.mult, ALU.add).then_inc(y_d, 1)
            with dve.Fori(0, 4) as m:
                for x in range(2):
                    dve.wait_ge(glu_s, m * 2 + x + 1)
                    dve.tensor_tensor(gprod[:, x, :], ps[:, 2 * x, :], sg[:, x, :], ALU.mult).then_inc(tile_evicted, 2)
                    dve.wait_ge(tile_evicted, m * 4 + TILE0["glu"] + 2 * x + 2)
                    dve.tensor_tensor(mixT[:, m * 2 + x, :], gprod[:, x, :], szT[:, m * 2 + x, :], ALU.mult).then_inc(glu_o, 1)
            residual("sout")
            rms_dve(5, "final_norm", hT)


def constants():
    p, c = np.arange(128)[:, None], np.arange(128)[None, :]
    same = p // CH == c // CH
    t = {}
    t["ident"] = p == c
    t["ones"] = np.ones((128, 128))
    t["cumsum"] = same & (p <= c)
    t["block"] = same
    t["half"] = np.concatenate([np.broadcast_to(p // CH == i, (128, 128)) for i in range(2)], 1)
    t["maskneg"] = np.where(same & (c <= p), 0.0, NEG)
    t["neg16"] = np.where((p // 16 == c // 16) & (c < p), -1.0, 0.0)
    t["low32"] = (p // 32 == c // 32) & (p // 16 > c // 16)
    t["low64"] = (p // 64 == c // 64) & (p // 32 > c // 32)
    k = np.arange(T)[None, :]
    ahead = k - (T - 128) - p
    t["dist"] = np.where(ahead <= 0, ahead, NEG)
    n = np.arange(NCMP)[None, None, :]
    tok = p[:, :, None] + 128 * np.arange(TT)[None, :, None]
    seen = CMPS * n + CMPB - 1 <= tok
    t["cdist"] = np.where(seen, CMPS * n + 0.5 * (CMPB - 1) - tok, NEG).reshape(128, -1)
    t["cmask"] = seen.reshape(128, -1)
    t["slope"] = np.broadcast_to(2.0 ** (-8.0 * (np.array(HALF_ORDER) + 1) / NH), (128, NH))
    t["invcount"] = np.broadcast_to(np.concatenate(
        [1.0 / np.minimum(np.arange(1, PAD + 1), 2 ** (g + 1)) for g in range(4)]), (128, 4 * PAD))
    return np.concatenate([np.asarray(t[name], np.float32) for name in CONST_W], 1)


def slots(w):
    k, m = w.shape
    return w.reshape(k // 128, 128, m // 128, 128).transpose(2, 1, 0, 3).reshape(m // 128, 128, k)


def by_partition(v):
    return v.reshape(-1, 128).T


def tall(w):
    return w.reshape(-1, 128, w.shape[1]).transpose(1, 0, 2).reshape(128, -1)


def lay_out(i):
    a = {}
    w_in = i["w_in"][0]
    nsa = i["l0_w_in_2"]
    qcols = np.concatenate([h * DH + np.arange(DH) for h in HEAD_ORDER])
    s = NH * DH
    kv = NG * DH
    zcols = s + 6 * kv + 3 * NH + qcols
    branches = [nsa[:, s + b * kv:s + (b + 1) * kv] for b in range(6)]
    nsa_feature = np.concatenate([nsa[:, qcols], branches[0], branches[1], branches[2], branches[4]], 1)
    v_both = np.concatenate([branches[3], branches[5]], 1)
    val = v_both.reshape(4, 2, 128, 512).transpose(0, 2, 1, 3).reshape(4, 128, 1024)
    glu = i["l1_w_glu_2"].reshape(D, 2, KT, 128).transpose(0, 2, 1, 3).reshape(D, 2 * D)
    down = i["w_down"][0].reshape(4, D, D)
    down = np.stack([slots(d) for d in down], 1).reshape(32, 128, 1024)
    a["wstream"] = np.concatenate([
        slots(w_in[:, :20 * 128]), slots(i["w_out"][0]), slots(i["w_up"][0]), down,
        slots(nsa_feature), val, slots(nsa[:, zcols]), slots(i["l0_w_out_2"][qcols]),
        slots(i["l1_w_in_2"]), slots(glu), slots(i["l1_w_out_2"])])
    a["x"] = i["x"][0].T.reshape(KT, 128, T).transpose(1, 0, 2)
    a["consts"] = constants()
    a["w_ab"] = tall(w_in[:, 20 * 128:])
    a["w_gate"] = tall(nsa[:, s + 6 * kv + np.concatenate([b * NH + np.array(HALF_ORDER) for b in range(3)])])
    a["w_pool"] = i["w_pool"][0].transpose(1, 0, 2).reshape(128, 512)
    twice = lambda v: np.concatenate([v, v], 0)
    for n in "kv":
        w1 = i[f"l0_cmp_{n}_w1_2"].reshape(CMPB, DH, 256).transpose(1, 0, 2).reshape(DH, -1)
        a[f"cmp_{n}_w1"] = twice(w1)
        a[f"cmp_{n}_w2"] = tall(i[f"l0_cmp_{n}_w2_2"])
    pair = lambda v: v.reshape(NPAIR, 128, -1).transpose(1, 0, 2).reshape(128, -1)
    a["ssm_b_re"] = pair(i["l1_b_re_2"])
    a["ssm_b_im"] = pair(i["l1_b_im_2"])
    a["ssm_c_re"] = pair(i["l1_c_re_2"].transpose(0, 2, 1))
    a["ssm_c_im"] = pair(i["l1_c_im_2"].transpose(0, 2, 1))
    t = dict(norm_mix=by_partition(i["norm_mix"]), norm_mlp=by_partition(i["norm_mlp"]),
             norm_final=by_partition(i["norm_final"]), l0_norm=by_partition(i["l0_norm_2"]),
             l1_norm=by_partition(i["l1_norm_2"]), final_norm=by_partition(i["final_norm_2"]),
             conv=i["conv_w"][0].reshape(CONV, 12, 128).transpose(2, 1, 0).reshape(128, -1),
             pool_scale=by_partition(i["pool_scale"]), gdn_norm=i["gdn_norm"].T,
             a_log=np.broadcast_to(np.tile(i["a_log"][0], TT), (128, 16)),
             dt_bias=np.broadcast_to(np.tile(i["dt_bias"][0], TT), (128, 16)),
             kpe=twice(i["l0_cmp_k_pe_2"].T), vpe=twice(i["l0_cmp_v_pe_2"].T),
             d_skip=by_partition(i["l1_d_2"]),
             log_dt=np.repeat(i["l1_log_dt_2"].reshape(NPAIR, 2).T, SP, 0),
             lre=pair(i["l1_lambda_re_2"]), lim=pair(i["l1_lambda_im_2"]))
    a["params"] = np.concatenate([t[name] for name in PARAM_W], 1)
    return {n: np.ascontiguousarray(v) for n, v in a.items()}


HEAD_ORDER = [(2 * gp + g2) * 4 + r for gp in range(2) for r in range(4) for g2 in range(2)]
HALF_ORDER = HEAD_ORDER[0::2] + HEAD_ORDER[1::2]


def kernel(**inputs):
    from concourse import bacc
    from concourse.bass_utils import run_bass_kernel_spmd

    nc = bacc.Bacc("TRN2", target_bir_lowering=False, num_devices=1)
    arrays = lay_out({n: np.asarray(v) for n, v in inputs.items()})
    A = {n: nc.dram_tensor(n, v.shape, mybir.dt.from_np(v.dtype), kind="ExternalInput").ap() for n, v in arrays.items()}
    out = nc.dram_tensor("out", (128, KT, T), mybir.dt.float32, kind="ExternalOutput").ap()
    build(nc, A, out)
    r = run_bass_kernel_spmd(nc, [arrays], core_ids=[0])
    y = r.results[0]["out"]
    return y.transpose(1, 0, 2).reshape(D, T).T.reshape(1, T, D)
```

```python
import numpy as np
import concourse.bass as bass
from concourse import mybir
from contextlib import ExitStack

D = 1024
T = 512
KT = D // 128
TT = T // 128
EPS = 1e-6
NEG = -1e30

NHG = 4
CH = 64
NCH = T // CH
FT = 4 * D // 128
PAD = 16
PW = T + PAD
CONV = 4

NH = 16
NG = 4
DH = 64
CMPB, CMPS = 32, 16
NCMP = (T - CMPB) // CMPS + 1

SG = 64
SC = 16
SP = 64
FR = 8
NC8 = T // FR
NPAIR = SG // 2

SLOTS = dict(inp=20, out=8, up0=16, down0=16, up1=16, down1=16, nsa=16, val=4, zed=8, nout=8, sin=16, glu=16, sout=8)
TILES = dict(inp=20, out=8, up0=16, down0=8, up1=16, down1=8, nsa=16, val=4, zed=8, nout=8, sin=16, glu=16, sout=8)


def bases(counts):
    at, out = 0, {}
    for name, n in counts.items():
        out[name] = at
        at += n
    return out, at


SLOT0, NSLOT = bases(SLOTS)
TILE0, NTILE = bases(TILES)

_mid = round((2 * np.pi - 6.28125) * 2.0 ** 21) / 2.0 ** 21
TWO_PI = [6.28125, _mid, 2 * np.pi - 6.28125 - _mid]
PI32 = float(np.nextafter(np.float32(np.pi), np.float32(0)))
ROUND = 1.5 * 2.0 ** 23

CONST_W = dict(ident=128, ones=128, cumsum=128, block=128, half=256, maskneg=128, neg16=128,
               low32=128, low64=128, dist=512, cdist=TT * NCMP, cmask=TT * NCMP, slope=NH,
               invcount=4 * PAD)
CONST_AT, NCONST = bases(CONST_W)
PARAM_W = dict(norm_mix=8, norm_mlp=8, norm_final=8, l0_norm=8, l1_norm=8, final_norm=8,
               conv=12 * CONV, pool_scale=4, gdn_norm=1, a_log=16, dt_bias=16, kpe=CMPB // 2, vpe=CMPB // 2,
               d_skip=8, log_dt=NPAIR, lre=NPAIR, lim=NPAIR)
PARAM_AT, NPARAM = bases(PARAM_W)


def build(nc, A, scratch, out_dram):
    f32 = mybir.dt.float32
    ALU = mybir.AluOpType
    ACT = mybir.ActivationFunctionType
    AX = mybir.AxisListType
    i32 = mybir.dt.int32

    ctx = ExitStack()
    with ctx:
        def sb(name, shape):
            return ctx.enter_context(nc.sbuf_tensor(name, shape, f32))

        def sem(name):
            return ctx.enter_context(nc.semaphore(name))

        f32r = mybir.dt.float32r
        plan = [nc.sbuf_base + -nc.sbuf_base % 64]

        def place(name, shape, dtype=f32, over=None, at=0):
            size = 4 * int(np.prod(shape[1:]))
            if over is None:
                start = plan[0]
                plan[0] += size + -size % 64
            else:
                start = PLACE[over] + at
            PLACE[name] = start
            return nc.alloc_sbuf_tensor_at(name, shape, dtype, offset=start)

        PLACE = {}
        KB = 1024
        hT = place("hT", [128, KT, T])
        uT = place("uT", [128, KT, T])
        mixT = place("mixT", [128, KT, T])
        uH = place("uH", [128, KT, T], f32r, over="uT")
        uL = place("uL", [128, KT, T], f32r, over="mixT")
        RING_FF = 4
        RING = 4
        raw = place("raw", [128, RING, 512])
        wh = place("wh", [128, RING, 512], f32r)
        wl = place("wl", [128, RING, 512], f32r)
        bigA = place("bigA", [128, 16704])
        bigB = place("bigB", [128, 16384])
        ffH = place("ffH", [128, FT // 2, T], f32r, over="bigA")
        ffL = place("ffL", [128, FT // 2, T], f32r, over="bigA", at=32 * KB)
        mH = place("mH", [128, KT, T], f32r, over="bigB")
        mL = place("mL", [128, KT, T], f32r, over="bigB", at=16 * KB)
        consts = place("const_table", [128, NCONST])
        params = place("param_table", [128, NPARAM])
        rms = place("rms", [128, T])
        xs = place("xs", [128, 2, T])
        small = place("small", [128, 704])
        ps = ctx.enter_context(nc.psum_tensor("ps", [128, 8, 512], f32))

        def const(name):
            a = CONST_AT[name]
            return consts[:, a:a + CONST_W[name]]

        def param(name):
            a = PARAM_AT[name]
            return params[:, a:a + PARAM_W[name]]

        def view(t, at, *dims):
            n = int(np.prod(dims))
            v = t[:, at:at + n]
            if len(dims) == 2:
                return v.rearrange("p (a b) -> p a b", b=dims[1])
            if len(dims) == 3:
                return v.rearrange("p (a b c) -> p a b c", b=dims[1], c=dims[2])
            return v

        uflat = uT[:, :, :].rearrange("p a b -> p (a b)")
        ident, ones = const("ident"), const("ones")

        projT = view(bigA, 0, 20, PW)
        qkvT = view(bigA, 20 * PW, 12, T)
        GA = TT * NHG * 128
        arr = [view(bigB, i * GA, TT, NHG * 128) for i in range(8)]
        brr = [view(bigA, 4 * PW + i * GA, TT, NHG * 128) for i in range(3)]
        urr = [view(uflat, i * GA, TT, NHG * 128) for i in range(2)]
        dec, kd, kbe, vb, Mm, aiT, Aa, Xx = arr
        A2, A2T, A4 = brr
        A4T, Rr = urr
        kcT, val, AT, A8, Yy, Bm32, Bm64, aS = kbe, vb, Xx, Aa, A2, A2T, A4, A2
        gB = Mm
        abS = small[:, 0:32].rearrange("p (t c) -> p t c", c=8)
        w_ab = small[:, 32:96]
        gx, ga, ge, gl, gg, bta, gc, eg, ekd, beg = (small[:, 96 + 16 * i:112 + 16 * i] for i in range(10))
        nalog = small[:, 256:272]
        egl = small[:, 272:304]
        Sst = view(mixT[:, :, :].rearrange("p a b -> p (a b)"), 4 * T, 2, 512)
        vnew = mixT[:, 6, :]
        l2n = mixT[:, 4:6, :]
        sqb = urr
        gdnO = view(uflat, 0, NHG, T)
        w_pool = view(bigB, 0, 4, 128)
        ptmp = [bigB[:, 1024:1024 + PW], bigB[:, 2048:2048 + PW]]
        pooled = view(bigB, 4096, 4, T)

        eps_ap, one_ap, zero_ap = small[:, 304:305], small[:, 305:306], small[:, 307:308]

        nsT = view(bigA, 0, 16, T)
        zsT = view(bigA, 8192, KT, T)
        vtok = view(bigA, 12288, TT, 512)
        relu, squared = view(bigB, 8192, 4, T), view(bigB, 10240, 4, T)
        swapped = view(bigB, 8192, 4, T)
        blk = [view(bigB, 10240 + 1984 * i, NG, CMPB // 2, NCMP) for i in range(2)]
        kcmp = view(bigA, 16320, 2, NCMP)
        vcmp = bigA[0:NCMP, 16384:16384 + NG * DH]
        w1 = [bigB[:, 0:4096], bigB[:, 4096:8192]]
        w2 = [bigB[:, 14208:14336], bigB[:, 14336:14464]]
        w_gate = bigB[:, 14464:14848]
        hid = [view(bigB, 14848 + 248 * i, 2, NG, NCMP) for i in range(2)]
        gate = small[:, 308:500].rearrange("p (t b h) -> p t b h", b=3, h=NH)
        pcT = bigB[0:NCMP, 0:NH * T].rearrange("p (h q) -> p h q", q=T)
        pc = [view(bigB, 13312 + i * 496, NH, NCMP) for i in range(TT)]
        dsl = view(bigB, 8192, 2, 512)
        prob = view(bigB, 9216, 3, 2, 512)
        probT = view(bigB, 12288, 3, 2, 512)
        cm, cs_ = small[:, 500:516], small[:, 516:532]
        amax = small[:, 532:538].rearrange("p (u b) -> p u b", b=2)
        anmax = small[:, 538:544].rearrange("p (u b) -> p u b", b=2)
        asum = small[:, 544:550].rearrange("p (u b) -> p u b", b=2)
        UNITS = [(t, half, qt) for t in range(KT) for half in range(2) for qt in range(TT)]

        suP = view(bigA, 0, KT, T)
        szT = view(bigA, 4096, KT, T)
        uc = view(bigA, 8192, SG, NC8)
        wri = [view(bigA, 12288 + 2048 * i, NPAIR, NC8) for i in range(2)]
        yF = view(bigB, 8192, KT, T)
        yD = view(bigB, 12288, KT, T)
        ptab = ([view(bigA, 12288 + 288 * i, 9, NPAIR) for i in range(2)]
                + [view(consts, CONST_AT["dist"] + 288 * i, 9, NPAIR) for i in range(2)])
        pk = [bigA[:, 13440 + 32 * i:13472 + 32 * i] for i in range(16)]
        BWT = [view(bigB, 4096 * i, NPAIR, 128) for i in range(2)]
        Tm = view(bigB, 4096, SG // 2, 128)
        Kl = bigB[0:SC, 0:4096].rearrange("p (g c) -> p g c", c=128)
        Eri = [view(bigB, 8192 + 2048 * i, NPAIR, NC8) for i in range(2)]
        tmpS = [bigB[:, 12288 + 1024 * i:13312 + 1024 * i] for i in range(2)]
        rho = view(bigB, 12288, NPAIR, NC8)
        rot = [bigB[:, 2048 * i:2048 * i + 2048] for i in range(2)]
        bc = [view(bigB, 14336 + 512 * i, NPAIR, SC) for i in range(4)]
        CA = [view(uflat, 0, NPAIR, 128), view(mixT[:, :, :].rearrange("p a b -> p (a b)"), 0, NPAIR, 128)]
        mag = view(bigA, 13952, 9, NPAIR)
        mag8 = small[:, 308:340]
        rK = [small[:, 340 + 32 * i:372 + 32 * i] for i in range(6)]
        baS = [bigA[:, 14240 + 1024 * i:15264 + 1024 * i] for i in range(2)]
        sg = view(bigB, 8192, 2, T)
        gprod = view(bigB, 9216, 2, T)

        s_w1 = sem("cmp_w1_loaded")
        swapped_in = sem("halves_swapped")
        s_w2 = sem("cmp_w2_loaded")
        s_wgate = sem("w_gate_loaded")
        g_mm, g_out = sem("gate_product"), sem("gates_ready")
        blk_done, cmp_h, cmp_act, cmp_mm, cmp_out = (sem(f"compress_{n}") for n in
                                                     ("windows", "hidden", "silu", "product", "ready"))
        cs_sub = sem("cmp_max_subtracted")
        cs_mm, cs_x, cs_exp, cs_p, cs_t, cs_ev = (sem(f"cmp_{n}") for n in
                                                  ("scores", "shifted", "exp", "probs", "transposed", "probsT"))
        ds_ready = sem("slopes_ready")
        at_qk, at_s, at_m, at_e, at_p, at_t, at_ev, at_v, at_o = (sem(f"att_{n}") for n in
            ("scores", "scores_read", "max", "exp", "probs", "transposed", "probsT", "value", "out"))
        s_bc = sem("ssm_bc_loaded")
        ssm_a, ssm_b = sem("ssm_scalar_engine"), sem("ssm_params")
        ba_done, bt_mm, bt_ev = sem("ssm_b_powers"), sem("ssm_b_transposed"), sem("ssm_b_stored")
        ca_done, ca_pool = sem("ssm_c_powers"), sem("ssm_c_powers_gpsimd")
        tables, ca_chain = sem("ssm_tables"), sem("ssm_c_products")
        u_stored, uc_in = sem("u_stored"), sem("u_regrouped")
        w_mm, w_ev = sem("chunk_input_product"), sem("chunk_input_stored")
        rot_in, x_done = sem("rotated"), sem("chunk_states")
        k_mm, k_ev = sem("lag_kernel_product"), sem("lag_kernel_stored")
        t_zero, t_in = sem("lag_matrix_zero"), sem("lag_matrix_filled")
        y_mm, y_ev, y_stored, y_in, y_d, y_act, y_g = (sem(f"y_{n}") for n in (
            "product", "evicted", "stored", "regrouped", "skip", "gelu", "split"))
        glu_s, glu_m, glu_lead, glu_o = sem("glu_sigmoid"), sem("glu_gated"), sem("glu_lead"), sem("glu_out")
        y_lead = sem("y_lead")

        s_x = sem("x_loaded")
        s_const = sem("consts_loaded")
        s_param = sem("params_loaded")
        s_wab = sem("w_ab_loaded")
        s_wpool = sem("w_pool_loaded")
        half_loaded = [sem(f"half{j}_loaded") for j in range(RING)]
        half_lead, half_split = sem("half_lead"), sem("half_split")
        half_used = sem("half_used")
        x_full, x_lead = sem("x_full"), sem("x_lead")
        tile_evicted = sem("tile_evicted")
        rms_sq, rms_sum, rms_std, rms_out = sem("rms_squares"), sem("rms_sum"), sem("rms_std"), sem("rms_out")
        dvc = sem("dve_chain")
        acc_ = sem("act_chain")
        pads0 = sem("pads_zero")
        ab_ready, ab_copied = sem("ab_ready"), sem("ab_copied")
        pooled_done, pool_mm, pool_out = sem("pooled"), sem("pool_product"), sem("pool_out")
        conv_step, conv_silu = sem("conv_step"), sem("conv_silu")
        l2_sq, l2_sum, l2_std, l2_out = sem("l2_squares"), sem("l2_sum"), sem("l2_std"), sem("l2_out")
        gate_a, gate_b = sem("gate_scalar_engine"), sem("gate_vector_engine")
        gate_mm = sem("gate_cumsum")
        row_mm, row_dec, row_exp, dec_exp = sem("row_sums"), sem("row_masked"), sem("row_exp"), sem("decay_ready")
        qd_done = sem("q_decayed")
        rnd_mm, rnd_ev = sem("round_product"), sem("round_evicted")
        sc_k, sc_v, sc_u, sc_s, sc_o, sc_oe = (sem(f"scan_{n}") for n in
                                              ("k_state", "v_new", "update", "state", "out", "out_copied"))
        go_sq, go_sum, go_std, go_out = sem("gdn_squares"), sem("gdn_sum"), sem("gdn_std"), sem("gdn_out")
        ff_sq, ff_lead, ff_room = sem("ff_squared"), sem("ff_lead"), sem("ff_places_freed")
        m_split = sem("mixed_split")
        out_done = sem("out_written")

        LIM = 2 * NSLOT
        block = ctx.enter_context(nc.Block())

        ROUNDS = ["attn", "attnT", "ktok", "vtok", "gram", "AT", "A2", "A2T", "R2", "A4", "A4T", "R4",
                  "A8", "R8", "X32", "Y32", "R32", "X64", "Y64", "R64", "val", "kcT"]

        def hd(x, tt, h):
            return x[:, tt, h * 128:(h + 1) * 128]

        @block.sync
        def _(sp):
            for j in range(RING):
                sp.dma_start(raw[:, j, :], A["wstream"][j]).then_inc(half_loaded[j], 16)
            with sp.Fori(1, LIM // RING) as m:
                for j in range(RING):
                    sp.wait_ge(half_split, m * RING + j - RING + 1)
                    sp.dma_start(raw[:, j, :], A["wstream"][m * RING + j]).then_inc(half_loaded[j], 16)

        @block.tensor
        def _(pe):
            u_parts = (uH, uL)

            def rms_pe(n):
                for k in range(KT):
                    pe.wait_ge(rms_sq, n * KT + k + 1)
                    i = pe.matmul(ps[:, 4, :], ones, uT[:, k, :], start=k == 0, stop=k == KT - 1)
                i.then_inc(rms_sum, 1)

            def product(out, left, right, first, last):
                (lh, ll), (rh, rl) = left, right
                pe.matmul(out, lh, rh, start=first, stop=False)
                pe.matmul(out, lh, rl, start=False, stop=False)
                return pe.matmul(out, ll, rh, start=False, stop=last)

            def half_slot(out, n, j, right, first, last, ready=None):
                pe.wait_ge(half_split, n + 1)
                for k in range(4):
                    if ready is not None:
                        pe.wait_ge(ready[0], ready[1] + k + 1)
                    i = product(out, (wh[:, j, k * 128:(k + 1) * 128], wl[:, j, k * 128:(k + 1) * 128]),
                                right(k), first and k == 0, last and k == 3)
                i.then_inc(half_used, 1)

            def tile_group(name, m, x, first=False, ready=None):
                for t in range(4):
                    if not first:
                        pe.wait_ge(tile_evicted, m * 4 + TILE0[name] + t - 3)
                    for h in range(2):
                        half_slot(ps[:, t, :], m * 8 + 2 * SLOT0[name] + 2 * t + h, (2 * t + h) % RING,
                                  lambda k: (x[0][:, h * 4 + k, :], x[1][:, h * 4 + k, :]), h == 0, h == 1,
                                  (ready[0], ready[1] + 4 * h) if ready is not None and t == 0 else None)

            def linear(name, x=(uH, uL), first=False, ready=None):
                tile_group(name, 0, x, first=first, ready=ready)
                with pe.Fori(1, TILES[name] // 4) as m:
                    tile_group(name, m, x)

            pe.wait_ge(s_const, 16)
            rms_pe(0)
            linear("inp", first=True, ready=(rms_out, 0))
            pe.wait_ge(s_wab, 16)
            for tt in range(TT):
                for k in range(KT):
                    for part in range(2):
                        i = pe.matmul(ps[:, 5, tt * 8:(tt + 1) * 8], u_parts[part][:, k, tt * 128:(tt + 1) * 128].bitcast(f32),
                                      w_ab[:, k * 8:(k + 1) * 8], start=k == 0 and part == 0, stop=k == KT - 1 and part == 1)
            i.then_inc(ab_ready, 1)
            pe.wait_ge(s_wpool, 16)
            for g in range(4):
                pe.wait_ge(pooled_done, g + 1)
                pe.wait_ge(tile_evicted, TILES["inp"])
                pe.matmul(ps[:, g, :], w_pool[:, g, :], pooled[:, g, :], start=True, stop=True).then_inc(pool_mm, 1)
            for i in range(8):
                pe.wait_ge(l2_sq, i + 1)
                if i < 1:
                    pe.wait_ge(ab_copied, 1)
                if i >= 2:
                    pe.wait_ge(l2_std, i - 1)
                pe.matmul(ps[:, 4 + i % 2, :], ones, uT[:, i, :], start=True, stop=True).then_inc(l2_sum, 1)
            pe.wait_ge(gate_b, 2)
            pe.wait_ge(pool_out, 4)
            pe.matmul(ps[:, 0, 0:16], const("cumsum"), gg, start=True, stop=True)
            pe.matmul(ps[:, 0, 16:32], const("block"), gg, start=True, stop=True)
            for c in range(2):
                i = pe.matmul(ps[:, 0, 32 + 16 * c:48 + 16 * c], const("half")[:, 128 * c:128 * c + 128], gg,
                              start=True, stop=True)
            i.then_inc(gate_mm, 1)
            for tt in range(TT):
                if tt == 0:
                    pe.wait_ge(gate_b, 3)
                    pe.wait_ge(l2_std, 8)
                for h in range(NHG):
                    i = pe.matmul(ps[:, 4 + tt, h * 128:(h + 1) * 128], hd(gB, tt, h), const("cumsum"),
                                  start=True, stop=True)
                i.then_inc(row_mm, 1)

            def qk(i, tt, h):
                return qkvT[:, i * 4 + h, tt * 128:(tt + 1) * 128]

            def operands(name, tt, h):
                return {
                    "attn": lambda: (qk(0, tt, h), qk(1, tt, h)),
                    "attnT": lambda: (hd(aS, tt, h), None),
                    "ktok": lambda: (qk(1, tt, h), None),
                    "vtok": lambda: (qk(2, tt, h), None),
                    "gram": lambda: (qk(1, tt, h), qk(1, tt, h)),
                    "AT": lambda: (hd(Aa, tt, h), None),
                    "A2": lambda: (hd(AT, tt, h), hd(Aa, tt, h)),
                    "A2T": lambda: (hd(Aa, tt, h), hd(AT, tt, h)),
                    "R2": lambda: (hd(A2, tt, h), hd(Rr, tt, h)),
                    "A4": lambda: (hd(A2T, tt, h), hd(A2, tt, h)),
                    "A4T": lambda: (hd(A2, tt, h), hd(A2T, tt, h)),
                    "R4": lambda: (hd(A4, tt, h), hd(Rr, tt, h)),
                    "A8": lambda: (hd(A4T, tt, h), hd(A4, tt, h)),
                    "R8": lambda: (hd(A8, tt, h), hd(Rr, tt, h)),
                    "X32": lambda: (hd(Rr, tt, h), None),
                    "Y32": lambda: (hd(Bm32, tt, h), hd(Rr, tt, h)),
                    "R32": lambda: (hd(Xx, tt, h), hd(Yy, tt, h)),
                    "X64": lambda: (hd(Rr, tt, h), None),
                    "Y64": lambda: (hd(Bm64, tt, h), hd(Rr, tt, h)),
                    "R64": lambda: (hd(Xx, tt, h), hd(Yy, tt, h)),
                    "val": lambda: (hd(Rr, tt, h), hd(vb, tt, h)),
                    "kcT": lambda: (hd(kbe, tt, h), hd(Rr, tt, h)),
                }[name]()

            pe.wait_ge(l2_out, 8)
            pe.wait_ge(dec_exp, TT)
            pe.wait_ge(row_exp, TT)
            for r, name in enumerate(ROUNDS):
                for tt in range(TT):
                    if r:
                        pe.wait_ge(rnd_ev, 4 * (r - 1) + tt + 1)
                    for h in range(NHG):
                        left, right = operands(name, tt, h)
                        o = ps[:, 4 + tt, h * 128:(h + 1) * 128]
                        if right is None:
                            i = pe.transpose(o, left, ident)
                        else:
                            i = pe.matmul(o, left, right, start=True, stop=True)
                    i.then_inc(rnd_mm, 1)

            pe.wait_ge(rnd_ev, 4 * len(ROUNDS))
            pe.wait_ge(qd_done, TT)
            for c in range(NCH):
                tt, half = c // 2, c % 2
                P = slice(64 * half, 64 * half + 64)
                S = Sst[:, c % 2, :]
                pe.wait_ge(sc_s, c + 1)
                for h in range(NHG):
                    i = pe.matmul(ps[P, 4, h * 128:(h + 1) * 128], kcT[:, tt, h * 128 + 64 * half:h * 128 + 64 * half + 64],
                                  S[:, h * 128:(h + 1) * 128], start=True, stop=True)
                i.then_inc(sc_k, 1)
                pe.wait_ge(sc_v, c + 1)
                for h in range(NHG):
                    i = pe.matmul(ps[:, 6, h * 128:(h + 1) * 128], kd[P, tt, h * 128:(h + 1) * 128],
                                  vnew[P, h * 128:(h + 1) * 128], start=True, stop=True)
                i.then_inc(sc_u, 1)
                if c >= 2:
                    pe.wait_ge(sc_oe, c - 1)
                for h in range(NHG):
                    o = ps[:, 5 + 2 * half, h * CH:(h + 1) * CH]
                    pe.matmul(o, S[:, h * 128:(h + 1) * 128], qkvT[:, h, c * CH:(c + 1) * CH], start=True, stop=False)
                    i = pe.matmul(o, vnew[P, h * 128:(h + 1) * 128],
                                  aiT[P, tt, h * 128 + 64 * half:h * 128 + 64 * half + 64], start=False, stop=True)
                i.then_inc(sc_o, 1)
            for h in range(NHG):
                pe.wait_ge(go_sq, h + 1)
                pe.matmul(ps[:, h, :], ones, urr[1].rearrange("p a b -> p (a b)")[:, h * T:(h + 1) * T],
                          start=True, stop=True).then_inc(go_sum, 1)
            pe.wait_ge(m_split, KT)
            linear("out", x=(mH, mL))
            rms_pe(1)
            for part in range(2):
                linear(f"up{part}", ready=(rms_out, KT) if part == 0 else None)
                pe.wait_ge(ff_room, RING_FF + FT // 2 * (part + 1))
                with pe.Fori(0, 2) as m:
                    for t in range(4):
                        pe.wait_ge(tile_evicted, m * 4 + TILE0[f"down{part}"] + t - 3)
                        for h in range(4):
                            half_slot(ps[:, t, :], m * 16 + 2 * SLOT0[f"down{part}"] + 4 * t + h, h,
                                      lambda k: (ffH[:, h * 4 + k, :], ffL[:, h * 4 + k, :]), h == 0, h == 3)
            rms_pe(2)
            rms_pe(3)
            linear("nsa", ready=(rms_out, 3 * KT))
            pe.wait_ge(tile_evicted, TILE0["val"])
            for k in range(KT):
                pe.wait_ge(half_split, 2 * SLOT0["val"] + k + 1)
                for tt in range(TT):
                    tok = slice(tt * 128, (tt + 1) * 128)
                    i = product(ps[:, tt, :], (uH[:, k, tok], uL[:, k, tok]), (wh[:, k % RING, :], wl[:, k % RING, :]),
                                k == 0, k == KT - 1)
                i.then_inc(half_used, 1)
            pe.wait_ge(s_wgate, 16)
            for tt in range(TT):
                for k in range(KT):
                    for part in range(2):
                        i = pe.matmul(ps[:, 5, tt * 48:(tt + 1) * 48], u_parts[part][:, k, tt * 128:(tt + 1) * 128].bitcast(f32),
                                      w_gate[:, k * 48:(k + 1) * 48], start=k == 0 and part == 0, stop=k == KT - 1 and part == 1)
            i.then_inc(g_mm, 1)
            linear("zed")
            pe.wait_ge(g_out, 1)
            pe.wait_ge(s_w1, 32)
            for x in range(2):
                pe.wait_ge(blk_done, x + 1)
                for ht in range(2):
                    for l in range(CMPB // 2):
                        i = pe.matmul(ps[:, 4 + x, ht * 128:ht * 128 + NG * NCMP],
                                      w1[x][:, l * 256 + ht * 128:l * 256 + ht * 128 + 128], blk[x][:, :, l, :],
                                      start=l == 0, stop=l == CMPB // 2 - 1)
                i.then_inc(cmp_h, 1)
            pe.wait_ge(s_w2, 32)
            pe.wait_ge(cmp_act, 1)
            for half in range(2):
                for ht in range(2):
                    i = pe.matmul(ps[64 * half:64 * half + 64, 7, 0:2 * NCMP], w2[0][:, ht * 64:(ht + 1) * 64],
                                  hid[0][:, ht, half::2, :], start=ht == 0, stop=ht == 1)
            i.then_inc(cmp_mm, 1)
            pe.wait_ge(cmp_act, 2)
            for g in range(NG):
                for ht in range(2):
                    i = pe.matmul(ps[0:NCMP, 6, g * DH:(g + 1) * DH], hid[1][:, ht, g, :],
                                  w2[1][:, ht * 64:(ht + 1) * 64], start=ht == 0, stop=ht == 1)
            i.then_inc(cmp_mm, 1)
            pe.wait_ge(cmp_out, 2)
            pe.wait_ge(tile_evicted, TILE0["zed"] + 8)
            for tt in range(TT):
                if tt >= 2:
                    pe.wait_ge(cs_x, tt - 1)
                for t in range(KT):
                    for half in range(2):
                        P = slice(64 * half, 64 * half + 64)
                        i = pe.matmul(ps[:, tt % 2 * 2 + half, t * NCMP:(t + 1) * NCMP],
                                      nsT[P, t, tt * 128:(tt + 1) * 128], kcmp[P, t // 4, :], start=True, stop=True)
                i.then_inc(cs_mm, 1)
            for tt in range(TT):
                pe.wait_ge(cs_p, tt + 1)
                for b in range(4):
                    n = tt * 4 + b
                    if n >= 2:
                        pe.wait_ge(cs_ev, n - 1)
                    for h in range(4):
                        i = pe.transpose(ps[0:NCMP, 4 + n % 2, h * 128:(h + 1) * 128], pc[tt][:, b * 4 + h, :], ident)
                    i.then_inc(cs_t, 1)
            pe.wait_ge(cs_ev, 16)

            def scores(u):
                t, half, qt = UNITS[u]
                P = slice(64 * half, 64 * half + 64)
                W = (qt + 1) * 128
                if u >= 2:
                    pe.wait_ge(at_s, u - 1)
                for b in range(2):
                    i = pe.matmul(ps[:, u % 2 * 2 + b, 0:W], nsT[P, t, qt * 128:(qt + 1) * 128],
                                  nsT[P, 12 + 2 * b + t // 4, 0:W], start=True, stop=True)
                i.then_inc(at_qk, 1)

            def turn(u):
                t, half, qt = UNITS[u]
                pe.wait_ge(at_p, u + 1)
                if u >= 1:
                    pe.wait_ge(at_ev, u)
                for b in range(2):
                    for kt in range(qt + 1):
                        i = pe.transpose(ps[:, 4 + b, kt * 128:(kt + 1) * 128], prob[:, u % 3, b, kt * 128:(kt + 1) * 128], ident)
                i.then_inc(at_t, 1)

            def values(u):
                t, half, qt = UNITS[u]
                pe.wait_ge(at_ev, u + 1)
                if t >= 2 and half == 0 and qt == 0:
                    pe.wait_ge(at_o, t - 1)
                o = ps[64 * half:64 * half + 64, 6 + t % 2, qt * 128:(qt + 1) * 128]
                g = t // 4 * 2 + half
                for b in range(2):
                    for kt in range(qt + 1):
                        pe.matmul(o, vtok[:, kt, b * 256 + g * DH:b * 256 + (g + 1) * DH],
                                  probT[:, u % 3, b, kt * 128:(kt + 1) * 128], start=b == 0 and kt == 0, stop=False)
                pe.matmul(o, vcmp[:, g * DH:(g + 1) * DH], pcT[:, half * 8 + t, qt * 128:(qt + 1) * 128],
                          start=False, stop=True).then_inc(at_v, 1)

            for n in range(len(UNITS) + 3):
                if n < len(UNITS):
                    scores(n)
                if 2 <= n <= len(UNITS) + 1:
                    turn(n - 2)
                if n >= 3:
                    values(n - 3)
            pe.wait_ge(at_o, KT)
            linear("nout")
            rms_pe(4)
            for c in range(4):
                tile_group("sin", c, u_parts, ready=(rms_out, 4 * KT) if c == 0 else None)
                pe.wait_ge(ba_done, c + 1)
                for ri in range(2):
                    for q in range(2):
                        if c or ri:
                            pe.wait_ge(bt_ev, c * 4 + ri * 2 + q - 1)
                        for g in range(4):
                            i = pe.transpose(ps[:, 4 + q, g * 128:(g + 1) * 128],
                                             baS[ri][:, (q * 4 + g) * 128:(q * 4 + g + 1) * 128], ident)
                        i.then_inc(bt_mm, 1)
            pe.wait_ge(uc_in, 8 * 16)
            for n in range(8):
                q, ri = n // 2, n % 2
                pe.wait_ge(bt_ev, min(16, 15 + n))
                if n >= 2:
                    pe.wait_ge(w_ev, n - 1)
                for gp in range(8):
                    for g2 in range(2):
                        i = pe.matmul(ps[64 * g2:64 * g2 + 64, 4 + n % 2, gp * 64:gp * 64 + 64],
                                      BWT[ri][:, q * 8 + gp, 64 * g2:64 * g2 + 64], uc[:, 2 * (q * 8 + gp) + g2, :],
                                      start=True, stop=True)
                i.then_inc(w_mm, 1)

            def lag_kernel(m):
                if m >= 2:
                    pe.wait_ge(k_ev, m - 1)
                for q in range(4):
                    for half in range(2):
                        pair = m * 4 + q
                        P = slice(64 * half, 64 * half + 64)
                        bank = m % 2 * 2 + half
                        for ri in range(2):
                            pe.matmul(ps[0:SC, bank, q * 128:q * 128 + SC], bc[ri][P, pair, :], bc[2 + ri][P, pair, :],
                                      start=ri == 0, stop=ri == 1)
                        for ri in range(2):
                            i = pe.matmul(ps[0:SC, bank, q * 128 + SC:(q + 1) * 128], bc[ri][P, pair, :],
                                          CA[ri][P, pair, 0:112], start=ri == 0, stop=ri == 1)
                i.then_inc(k_mm, 1)

            def chunk_outputs(m):
                if m >= 2:
                    pe.wait_ge(y_ev, m - 1)
                for q in range(8):
                    for half in range(2):
                        pair = m * 8 + q
                        g = 2 * pair + half
                        P = slice(64 * half, 64 * half + 64)
                        bank = 4 + m % 2 * 2 + half
                        pe.matmul(ps[:, bank, q * 64:(q + 1) * 64], Tm[:, g % 32, :], uc[:, g, :],
                                  start=True, stop=False)
                        o = ps[:, bank, q * 64 + 1:(q + 1) * 64]
                        pe.matmul(o, CA[0][P, pair, :], wri[0][P, pair, 0:NC8 - 1], start=False, stop=False)
                        i = pe.matmul(o, CA[1][P, pair, :], wri[1][P, pair, 0:NC8 - 1], start=False, stop=True)
                i.then_inc(y_mm, 1)

            pe.wait_ge(ca_done, 2)
            pe.wait_ge(tile_evicted, TILE0["sin"] + 16)
            for m in range(4):
                lag_kernel(m)
            pe.wait_ge(ca_pool, 8)
            lag_kernel(4)
            lag_kernel(5)
            pe.wait_ge(t_in, 8 * 16)
            pe.wait_ge(x_done, 1)
            chunk_outputs(0)
            chunk_outputs(1)
            lag_kernel(6)
            lag_kernel(7)
            pe.wait_ge(t_in, 16 * 16)
            chunk_outputs(2)
            chunk_outputs(3)
            linear("glu", ready=(y_g, 0))
            pe.wait_ge(glu_o, KT)
            linear("sout", x=(mH, mL))
            rms_pe(5)

        @block.scalar
        def _(act):
            count = [0]

            def own(i):
                count[0] += 1
                i.then_inc(acc_, 1)
                act.wait_ge(acc_, count[0])

            act.dma_start(hT[:, :, :], A["x"]).then_inc(s_x, 16)
            act.dma_start(consts[:, :], A["consts"]).then_inc(s_const, 16)
            act.dma_start(params[:, :], A["params"]).then_inc(s_param, 16)
            act.dma_start(w_ab, A["w_ab"]).then_inc(s_wab, 16)
            act.dma_start(bigB[:, 0:512], A["w_pool"]).then_inc(s_wpool, 16)

            def rms_act(n):
                for k in range(KT):
                    act.activation(uT[:, k, :], hT[:, k, :], ACT.Square).then_inc(rms_sq, 1)
                act.wait_ge(rms_sum, n + 1)
                act.activation(rms[:, :], ps[:, 4, :], ACT.Sqrt, scale=1.0 / D, bias=eps_ap).then_inc(rms_std, 1)

            full = [0]

            def lead(dst):
                n = full[0]
                full[0] += 1
                act.wait_ge(x_full, n + 1)
                act.activation(dst, xs[:, n % 2, :], ACT.Copy).then_inc(x_lead, 1)

            act.wait_ge(s_x, 16)
            act.wait_ge(pads0, 3)
            rms_act(0)
            for k in range(KT):
                lead(uH[:, k, :])

            def evict(name, lo, hi, f):
                with act.Fori(lo // 4, hi // 4) as m:
                    for j in range(4):
                        act.wait_ge(half_used, m * 8 + 2 * SLOT0[name] + 2 * j + 2)
                        f(m * 4 + j, ps[:, j, :]).then_inc(tile_evicted, 1)

            evict("inp", 0, 16, lambda n, p: act.activation(projT[:, n, PAD:PW], p, ACT.Copy))
            evict("inp", 16, 20, lambda n, p: act.activation(projT[:, n, PAD:PW], p, ACT.Silu))
            with act.Fori(0, 12) as n:
                act.wait_ge(conv_step, n * 4 + 4)
                act.activation(qkvT[:, n, :], qkvT[:, n, :], ACT.Silu).then_inc(conv_silu, 1)
            for g in range(4):
                act.wait_ge(pool_mm, g + 1)
                act.activation(mixT[:, g, :], ps[:, g, :], ACT.Copy, scale=param("pool_scale")[:, g:g + 1]).then_inc(pool_out, 1)
            act.wait_ge(conv_silu, 8)
            act.wait_ge(ab_ready, 1)
            act.wait_ge(conv_silu, 12)
            for i in range(8):
                act.activation(uT[:, i, :], qkvT[:, i, :], ACT.Square).then_inc(l2_sq, 1)
            for i in range(8):
                act.wait_ge(l2_sum, i + 1)
                if i >= 2:
                    act.wait_ge(l2_out, i - 1)
                act.activation(l2n[:, i % 2, :], ps[:, 4 + i % 2, :], ACT.Sqrt, bias=eps_ap).then_inc(l2_std, 1)
            act.wait_ge(gate_b, 1)
            own(act.activation(ge, ga, ACT.Exp, scale=-1.0))
            act.activation(gl, ge, ACT.Ln, bias=one_ap).then_inc(gate_a, 1)
            act.activation(nalog, param("a_log"), ACT.Exp).then_inc(gate_a, 1)
            act.activation(bta.rearrange("p (t h) -> p t h", h=4), abS[:, :, 4:8], ACT.Sigmoid).then_inc(gate_a, 1)
            act.wait_ge(gate_b, 4)
            act.activation(eg, ps[:, 0, 0:16], ACT.Exp).then_inc(gate_a, 1)
            act.activation(egl, ps[:, 0, 32:64], ACT.Exp).then_inc(gate_a, 1)
            act.activation(ekd, gl, ACT.Exp).then_inc(gate_a, 1)
            for tt in range(TT):
                act.wait_ge(row_dec, tt + 1)
                for h in range(NHG):
                    i = act.activation(hd(dec, tt, h), hd(dec, tt, h), ACT.Exp, bias=gc[:, tt * 4 + h:tt * 4 + h + 1])
                i.then_inc(dec_exp, 1)
            for tt in range(TT):
                act.wait_ge(row_mm, tt + 1)
                act.activation(A4T[:, tt, :], ps[:, 4 + tt, :], ACT.Exp).then_inc(row_exp, 1)
            for c in range(NCH):
                act.wait_ge(sc_o, c + 1)
                src = ps[:, 5 + 2 * (c % 2), 0:NHG * CH].rearrange("p (h c) -> p h c", c=CH)
                act.activation(gdnO[:, :, c * CH:(c + 1) * CH], src, ACT.Copy).then_inc(sc_oe, 1)
            act.wait_ge(sc_oe, NCH)
            sq = urr[1].rearrange("p a b -> p (a b)")
            for h in range(NHG):
                act.activation(sq[:, h * T:(h + 1) * T], gdnO[:, h, :], ACT.Square).then_inc(go_sq, 1)
            for h in range(NHG):
                act.wait_ge(go_sum, h + 1)
                act.activation(qkvT[:, h, :], ps[:, h, :], ACT.Sqrt, scale=1.0 / 128, bias=eps_ap).then_inc(go_std, 1)
            for k in range(KT):
                lead(mH[:, k, :])
            act.wait_ge(tile_evicted, TILE0["out"] + 8)
            rms_act(1)
            for x, n in enumerate("kv"):
                act.dma_start(w1[x], A[f"cmp_{n}_w1"]).then_inc(s_w1, 16)
                act.dma_start(w2[x], A[f"cmp_{n}_w2"]).then_inc(s_w2, 16)
            act.dma_start(w_gate, A["w_gate"]).then_inc(s_wgate, 16)
            for k in range(KT):
                lead(uH[:, k, :])
            for part in range(2):
                name = f"up{part}"
                if part:
                    act.wait_ge(tile_evicted, TILE0[name])
                with act.Fori(0, FT // 8) as m:
                    for j in range(4):
                        act.wait_ge(half_used, m * 8 + 2 * SLOT0[name] + 2 * j + 2)
                        act.activation(relu[:, j, :], ps[:, j, :], ACT.Relu).then_inc(tile_evicted, 1)
                        act.wait_ge(tile_evicted, m * 4 + TILE0[name] + j + 1)
                        act.wait_ge(ff_room, m * 4 + part * FT // 2 + j + 1)
                        act.activation(squared[:, j, :], relu[:, j, :], ACT.Square).then_inc(ff_sq, 1)
                        act.wait_ge(ff_sq, m * 4 + part * FT // 2 + j + 1)
                        act.activation(ffH[:, m * 4 + j, :], squared[:, j, :], ACT.Copy).then_inc(ff_lead, 1)
            act.wait_ge(tile_evicted, TILE0["down1"] + 8)
            rms_act(2)
            act.wait_ge(rms_out, 3 * KT)
            rms_act(3)
            for k in range(KT):
                lead(uH[:, k, :])
            evict("nsa", 0, 8, lambda n, p: act.activation(nsT[:, n, :], p, ACT.Copy, scale=DH ** -0.5))
            evict("nsa", 8, 16, lambda n, p: act.activation(nsT[:, n, :], p, ACT.Copy))
            act.wait_ge(half_used, 2 * SLOT0["val"] + KT)
            for tt in range(TT):
                act.activation(vtok[:, tt, :], ps[:, tt, :], ACT.Copy).then_inc(tile_evicted, 1)
            act.wait_ge(g_mm, 1)
            act.activation(small[:, 308:500], ps[:, 5, 0:192], ACT.Sigmoid).then_inc(g_out, 1)
            act.wait_ge(tile_evicted, TILE0["nsa"] + 16)
            for n in range(4):
                for par in range(2):
                    act.dma_start(swapped[64 * par:64 * par + 64, n, :], nsT[64 - 64 * par:128 - 64 * par, 8 + n, :]).then_inc(swapped_in, 16)
            evict("zed", 0, 8, lambda n, p: act.activation(zsT[:, n, :], p, ACT.Silu))
            for x in range(2):
                act.wait_ge(cmp_h, x + 1)
                i = act.activation(hid[x].rearrange("p t g n -> p t (g n)"),
                                   ps[:, 4 + x, 0:256].rearrange("p (t c) -> p t c", c=128)[:, :, 0:NG * NCMP], ACT.Silu)
                i.then_inc(cmp_act, 1)
            for tt in range(TT):
                act.wait_ge(cs_x, tt + 1)
                f = pc[tt].rearrange("p h n -> p (h n)")
                act.wait_ge(cs_sub, tt + 1)
                act.activation(f, f, ACT.Exp).then_inc(cs_exp, 1)
            for n in range(16):
                act.wait_ge(cs_t, n + 1)
                tt, b = n // 4, n % 4
                act.activation(pcT[:, b * 4:b * 4 + 4, tt * 128:(tt + 1) * 128],
                               ps[0:NCMP, 4 + n % 2, :].rearrange("p (h q) -> p h q", q=128), ACT.Copy).then_inc(cs_ev, 1)
            for n in range(len(UNITS) + 2):
                if n < len(UNITS):
                    t, half, qt = UNITS[n]
                    W = (qt + 1) * 128
                    act.wait_ge(at_m, n + 1)
                    for b in range(2):
                        i = act.activation(prob[:, n % 3, b, 0:W], prob[:, n % 3, b, 0:W], ACT.Exp,
                                           bias=anmax[:, n % 3, b:b + 1], accum_out=asum[:, n % 3, b:b + 1])
                    i.then_inc(at_e, 1)
                if n >= 2:
                    u = n - 2
                    W = (UNITS[u][2] + 1) * 128
                    act.wait_ge(at_t, u + 1)
                    if u >= 3:
                        act.wait_ge(at_v, u - 2)
                    act.activation(probT[:, u % 3, :, 0:W], ps[:, 4:6, 0:W], ACT.Copy).then_inc(at_ev, 1)
                if n >= 14 and n % 8 == 6:
                    lead(uH[:, n // 8 - 1, :])
            lead(uH[:, KT - 1, :])
            for x, name in enumerate(("ssm_b_re", "ssm_b_im", "ssm_c_re", "ssm_c_im")):
                act.dma_start(bc[x].rearrange("p g c -> p (g c)"), A[name]).then_inc(s_bc, 16)
            act.activation(pk[0], param("log_dt"), ACT.Exp).then_inc(ssm_a, 1)
            act.wait_ge(ssm_b, 1)
            for k in range(9):
                i = act.activation(mag[:, k, :], pk[1], ACT.Exp, scale=float(k))
            i.then_inc(ssm_a, 1)
            act.activation(pk[6], pk[5], ACT.Sin).then_inc(ssm_a, 1)
            act.activation(pk[7], pk[5], ACT.Sin, scale=0.5).then_inc(ssm_a, 1)
            act.wait_ge(tile_evicted, TILE0["nout"] + 8)
            rms_act(4)
            for k in range(KT):
                lead(uH[:, k, :])

            def store_b(c):
                for ri in range(2):
                    for q in range(2):
                        act.wait_ge(bt_mm, c * 4 + ri * 2 + q + 1)
                        act.activation(BWT[ri].rearrange("p g c -> p (g c)")[:, (c * 8 + q * 4) * 128:(c * 8 + q * 4 + 4) * 128],
                                       ps[:, 4 + q, :], ACT.Copy).then_inc(bt_ev, 1)

            for c in range(2):
                evict("sin", c * 4, c * 4 + 4, lambda n, p: act.activation(
                    suP[:, n, :].rearrange("p (j c) -> p c j", c=NC8), p.rearrange("p (c j) -> p c j", j=FR), ACT.Copy))
                if c == 1:
                    act.wait_ge(tile_evicted, TILE0["sin"] + 8)
                    act.dma_start(scratch["u"], suP).then_inc(u_stored, 16)
                store_b(c)
            act.wait_ge(u_stored, 16)
            by_frame = scratch["u"].rearrange("(g c) t (j n) -> j c t g n", c=SC, j=FR)
            for j in range(FR):
                act.dma_start(uc[112 - 16 * j:128 - 16 * j, :, :].rearrange("p (t g) n -> p t g n", g=8),
                              by_frame[j]).then_inc(uc_in, 16)
            for c in range(2, 4):
                evict("sin", c * 4, c * 4 + 4, lambda n, p: act.activation(szT[:, n - 8, :], p, ACT.Silu))
                store_b(c)
            for n in range(8):
                q, ri = n // 2, n % 2
                act.wait_ge(w_mm, n + 1)
                act.activation(wri[ri].rearrange("p g c -> p (g c)")[:, q * 512:(q + 1) * 512], ps[:, 4 + n % 2, :], ACT.Copy).then_inc(w_ev, 1)
            act.wait_ge(rot_in, 1)

            def store_kernel(m):
                act.wait_ge(k_mm, m + 1)
                n = m % 4
                act.activation(Kl[:, n * 8:n * 8 + 8, :].rearrange("p (q h) c -> p h q c", h=2),
                               ps[0:SC, m % 2 * 2:m % 2 * 2 + 2, :].rearrange("p h (q c) -> p h q c", c=128),
                               ACT.Copy).then_inc(k_ev, 1)

            def fill_lags(part):
                act.wait_ge(k_ev, (part + 1) * 4)
                for j in range(FR):
                    act.dma_start(Tm[112 - 16 * j:128 - 16 * j, :, 16 * j:128], Kl[:, :, 0:128 - 16 * j]).then_inc(t_in, 16)

            def store_y(part):
                for m in range(2 * part, 2 * part + 2):
                    act.wait_ge(y_mm, m + 1)
                    act.activation(uc[:, m * 16:m * 16 + 16, :].rearrange("p (q h) c -> p h q c", h=2),
                                   ps[:, 4 + m % 2 * 2:6 + m % 2 * 2, :].rearrange("p h (q c) -> p h q c", c=NC8),
                                   ACT.Copy).then_inc(y_ev, 1)
                act.wait_ge(y_ev, 2 * part + 2)
                act.dma_start(scratch["y"][part], uc[:, part * 32:part * 32 + 32, :]).then_inc(y_stored, 16)

            def load_y(part):
                act.wait_ge(y_stored, 16 * part + 16)
                by_group = scratch["y"][part].rearrange("(j c) (t g) n -> g c t j n", c=SC, g=8)
                for g in range(8):
                    for t in range(4):
                        act.dma_start(yF[16 * g:16 * g + 16, 4 * part + t, :].rearrange("p (j n) -> p j n", n=NC8),
                                      by_group[g, :, t]).then_inc(y_in, 16)

            def gelu(part):
                for k in range(4 * part, 4 * part + 4):
                    act.wait_ge(y_d, k + 1)
                    act.activation(yD[:, k, :], yD[:, k, :], ACT.Gelu_apprx_tanh).then_inc(y_act, 1)
                    act.wait_ge(y_act, k + 1)
                    act.activation(uH[:, k, :], yD[:, k, :], ACT.Copy).then_inc(y_lead, 1)

            for m in range(4):
                store_kernel(m)
            act.wait_ge(t_zero, 1)
            fill_lags(0)
            act.wait_ge(t_in, 8 * 16)
            store_kernel(4)
            store_kernel(5)
            store_y(0)
            store_kernel(6)
            store_kernel(7)
            fill_lags(1)
            load_y(0)
            store_y(1)
            gelu(0)
            load_y(1)
            gelu(1)
            with act.Fori(0, 4) as m:
                for x in range(2):
                    act.wait_ge(half_used, m * 8 + 2 * SLOT0["glu"] + 4 * x + 4)
                    act.wait_ge(tile_evicted, m * 4 + TILE0["glu"] + 2 * x - 2)
                    act.activation(sg[:, x, :], ps[:, 2 * x + 1, :], ACT.Sigmoid).then_inc(glu_s, 1)
                for x in range(2):
                    act.wait_ge(glu_m, m * 2 + x + 1)
                    act.activation(mH[:, m * 2 + x, :], gprod[:, x, :], ACT.Copy).then_inc(glu_lead, 1)
            act.wait_ge(tile_evicted, NTILE)
            rms_act(5)
            act.wait_ge(rms_out, 6 * KT)
            act.dma_start(out_dram, hT[:, :, :]).then_inc(out_done, 16)
            act.wait_ge(out_done, 16)

        @block.gpsimd
        def _(pool):
            def split_weights(lo, hi):
                hi = min(hi, LIM)
                if hi <= lo:
                    return
                with pool.Fori(lo // RING, hi // RING) as m:
                    for j in range(RING):
                        pool.wait_ge(half_loaded[j], m * 16 + 16)
                        if lo:
                            pool.wait_ge(half_used, m * RING + j - RING + 1)
                        pool.tensor_tensor(wh[:, j, :], raw[:, j, :], zero_ap.to_broadcast([128, 512]), ALU.add).then_inc(half_lead, 1)
                        pool.wait_ge(half_lead, m * RING + j + 1)
                        pool.tensor_tensor(wl[:, j, :], raw[:, j, :], wh[:, j, :].bitcast(f32), ALU.subtract).then_inc(half_split, 1)

            pool.memset(projT[:, :, 0:PAD], 0.0).then_inc(pads0, 1)
            pool.memset(eps_ap, EPS).then_inc(pads0, 1)
            pool.memset(one_ap, 1.0).then_inc(pads0, 1)
            pool.memset(zero_ap, 0.0).then_inc(pads0, 1)
            pool.wait_ge(pads0, 4)
            split_weights(0, RING)
            split_weights(RING, 2 * 20)
            split_weights(2 * 20, 2 * SLOT0["nout"] + RING)
            pool.wait_ge(cmp_act, 2)
            for n in range(NH):
                t, half = n // 2, n % 2
                if n >= 2:
                    pool.wait_ge(at_s, 4 * (n - 1))
                pool.tensor_scalar(dsl[:, n % 2, :], const("dist"), const("slope")[:, half * 8 + t:half * 8 + t + 1], 0.0,
                                   ALU.mult, ALU.add).then_inc(ds_ready, 1)
            split_weights(2 * SLOT0["nout"] + RING, 2 * SLOT0["glu"])
            pool.wait_ge(tables, 1)
            pool.wait_ge(half_used, 2 * SLOT0["glu"])
            for c in range(4):
                gs = slice(16 + c * 4, 20 + c * 4)
                cc = [bc[2 + q][:, gs, :].unsqueeze(2).to_broadcast([128, 4, FR, SC]) for q in range(2)]
                pp = [p[:, 1:9, gs].rearrange("p k g -> p g k").unsqueeze(3).to_broadcast([128, 4, FR, SC]) for p in ptab[2:]]
                o = [CA[q][:, gs, :].rearrange("p g (k c) -> p g k c", c=SC) for q in range(2)]
                tv = [xs[:, q, :].rearrange("p (g j c) -> p g j c", g=4, j=FR) for q in range(2)]
                for ri, (x, y, op) in enumerate(((0, 1, ALU.add), (1, 0, ALU.subtract))):
                    if c or ri:
                        pool.wait_ge(ca_pool, 2 * c + ri)
                    pool.tensor_tensor(tv[0], pp[0], cc[x], ALU.mult).then_inc(ca_chain, 1)
                    pool.tensor_tensor(tv[1], pp[1], cc[y], ALU.mult).then_inc(ca_chain, 1)
                    pool.wait_ge(ca_chain, 2 * (2 * c + ri) + 2)
                    pool.tensor_tensor(o[ri], tv[0], tv[1], op).then_inc(ca_pool, 1)
            pool.wait_ge(w_mm, 8)
            pool.memset(Tm, 0.0).then_inc(t_zero, 1)
            split_weights(2 * SLOT0["glu"], 2 * NSLOT)

        @block.vector
        def _(dve):
            count = [0]

            def own(i):
                count[0] += 1
                i.then_inc(dvc, 1)
                dve.wait_ge(dvc, count[0])

            full, split = [0], [0]

            def rest(dst, leading):
                n = split[0]
                split[0] += 1
                dve.wait_ge(x_lead, n + 1)
                return dve.tensor_tensor(dst, xs[:, n % 2, :], leading.bitcast(f32), ALU.subtract)

            def rms_dve(n, weight, dst):
                dve.wait_ge(rms_std, n + 1)
                own(dve.reciprocal(rms[:, :], rms[:, :]))
                for k in range(KT + 1):
                    if k < KT:
                        if dst is None:
                            if k >= 2:
                                dve.wait_ge(rms_out, n * KT + k - 1)
                            i = dve.scalar_tensor_tensor(xs[:, k % 2, :], hT[:, k, :], param(weight)[:, k:k + 1], rms[:, :],
                                                         ALU.mult, ALU.mult)
                            i.then_inc(x_full, 1)
                            full[0] += 1
                        else:
                            dve.scalar_tensor_tensor(dst[:, k, :], hT[:, k, :], param(weight)[:, k:k + 1], rms[:, :],
                                                     ALU.mult, ALU.mult).then_inc(rms_out, 1)
                    if k and dst is None:
                        rest(uL[:, k - 1, :], uH[:, k - 1, :]).then_inc(rms_out, 1)

            def residual(name):
                with dve.Fori(0, 2) as m:
                    for j in range(4):
                        per = 2 * SLOTS[name] // TILES[name]
                        dve.wait_ge(half_used, (m * 4 + j + 1) * per + 2 * SLOT0[name])
                        dve.tensor_tensor(hT[:, m * 4 + j, :], hT[:, m * 4 + j, :], ps[:, j, :], ALU.add).then_inc(tile_evicted, 1)

            dve.wait_ge(s_param, 16)
            dve.wait_ge(s_x, 16)
            rms_dve(0, "norm_mix", None)
            dve.wait_ge(s_const, 16)
            for g in range(4):
                dve.wait_ge(tile_evicted, g + 1)
                w, src = 1, projT[:, g, :]
                for d in range(g + 1):
                    dst = ptmp[d % 2]
                    own(dve.tensor_tensor(dst[:, 2 * w - 1:PW], src[:, 2 * w - 1:PW], src[:, w - 1:PW - w], ALU.add))
                    src, w = dst, 2 * w
                mean = ptmp[(g + 1) % 2]
                own(dve.tensor_scalar(mean[:, PAD:PW], src[:, PAD:PW], 1.0 / w, 0.0, ALU.mult, ALU.add))
                own(dve.tensor_tensor(mean[:, PAD:PAD + w], src[:, PAD:PAD + w], const("invcount")[:, g * PAD:g * PAD + w], ALU.mult))
                i = dve.tensor_tensor(pooled[:, g, :], mean[:, PAD:PW], projT[:, g, PAD:PW], ALU.subtract)
                i.then_inc(pooled_done, 1)
                dve.wait_ge(pooled_done, g + 1)
            cw = param("conv")
            with dve.Fori(0, 12) as n:
                dve.wait_ge(tile_evicted, n + 5)
                x = projT[:, n + 4, :]
                y = qkvT[:, n, :]
                dve.tensor_scalar(y, projT[:, n + 4, PAD - 3:PW - 3], cw[:, bass.ds(n * CONV, 1)], None, ALU.mult).then_inc(conv_step, 1)
                for i in range(1, CONV):
                    dve.wait_ge(conv_step, n * 4 + i)
                    dve.scalar_tensor_tensor(y, projT[:, n + 4, PAD - 3 + i:PW - 3 + i], cw[:, bass.ds(n * CONV + i, 1)], y,
                                             ALU.mult, ALU.add).then_inc(conv_step, 1)
            dve.wait_ge(ab_ready, 1)
            dve.tensor_copy(abS.rearrange("p t c -> p (t c)"), ps[:, 5, 0:32]).then_inc(ab_copied, 1)
            dve.wait_ge(ab_copied, 1)
            own(dve.tensor_tensor(gx.rearrange("p (t h) -> p t h", h=4), abS[:, :, 0:4],
                                  param("dt_bias").rearrange("p (t h) -> p t h", h=4), ALU.add))
            own(dve.tensor_scalar(gg, gx, -1.0, None, ALU.mult))
            dve.tensor_tensor(ga, gx, gg, ALU.max).then_inc(gate_b, 1)
            for i in range(8):
                dve.wait_ge(l2_std, i + 1)
                own(dve.reciprocal(l2n[:, i % 2, :], l2n[:, i % 2, :]))
                dve.scalar_tensor_tensor(qkvT[:, i, :], qkvT[:, i, :], 128 ** -0.5 if i < 4 else 1.0, l2n[:, i % 2, :],
                                         ALU.mult, ALU.mult).then_inc(l2_out, 1)
            dve.wait_ge(gate_a, 3)
            own(dve.scalar_tensor_tensor(gx, gx, 0.0, gl, ALU.max, ALU.add))
            dve.scalar_tensor_tensor(gg, gx, -1.0, nalog, ALU.mult, ALU.mult).then_inc(gate_b, 1)
            dve.wait_ge(gate_b, 2)
            dve.wait_ge(pool_mm, 4)
            dve.tensor_copy(gB.rearrange("p t (h c) -> p (t h) c", c=128),
                            gg.unsqueeze(2).to_broadcast([128, 16, 128])).then_inc(gate_b, 1)
            dve.wait_ge(gate_mm, 1)
            own(dve.tensor_copy(gc, ps[:, 0, 0:16]))
            dve.tensor_tensor(gl, ps[:, 0, 16:32], gc, ALU.subtract).then_inc(gate_b, 1)
            dve.wait_ge(gate_a, 4)
            own(dve.tensor_tensor(beg, bta, eg, ALU.mult))
            mneg = const("maskneg").unsqueeze(1).to_broadcast([128, 4, 128])
            for tt in range(TT):
                dve.wait_ge(row_mm, tt + 1)
                dve.scalar_tensor_tensor(dec[:, tt, :].rearrange("p (h c) -> p h c", c=128),
                                         ps[:, 4 + tt, :].rearrange("p (h c) -> p h c", c=128), -1.0, mneg,
                                         ALU.mult, ALU.add).then_inc(row_dec, 1)
            dve.wait_ge(dec_exp, TT)
            dve.wait_ge(gate_a, 6)

            def masked(dst, tt, mask):
                return dve.tensor_tensor(dst[:, tt, :].rearrange("p (h c) -> p h c", c=128),
                                         Mm[:, tt, :].rearrange("p (h c) -> p h c", c=128),
                                         const(mask).unsqueeze(1).to_broadcast([128, 4, 128]), ALU.mult)

            for r, name in enumerate(ROUNDS):
                for tt in range(TT):
                    dve.wait_ge(rnd_mm, 4 * r + tt + 1)
                    p = ps[:, 4 + tt, :]

                    def by_head(dst, scalars):
                        for h in range(NHG):
                            i = dve.tensor_scalar(hd(dst, tt, h), p[:, h * 128:(h + 1) * 128],
                                                  scalars[:, tt * 4 + h:tt * 4 + h + 1], None, ALU.mult)
                        return i

                    if name == "attn":
                        i = dve.tensor_tensor(aS[:, tt, :], p, dec[:, tt, :], ALU.mult)
                    elif name == "attnT":
                        i = dve.tensor_copy(aiT[:, tt, :], p)
                    elif name == "ktok":
                        by_head(kd, ekd)
                        i = by_head(kbe, beg)
                    elif name == "vtok":
                        i = by_head(vb, bta)
                    elif name == "gram":
                        for h in range(NHG):
                            i = dve.scalar_tensor_tensor(hd(Mm, tt, h), p[:, h * 128:(h + 1) * 128],
                                                         bta[:, tt * 4 + h:tt * 4 + h + 1], hd(dec, tt, h),
                                                         ALU.mult, ALU.mult)
                        own(i)
                        i = masked(Aa, tt, "neg16")
                    elif name == "AT":
                        dve.tensor_copy(AT[:, tt, :], p)
                        i = dve.tensor_tensor(Rr[:, tt, :].rearrange("p (h c) -> p h c", c=128),
                                              p.rearrange("p (h c) -> p h c", c=128),
                                              ident.unsqueeze(1).to_broadcast([128, 4, 128]), ALU.add)
                    elif name in ("R2", "R4", "R8"):
                        i = dve.tensor_tensor(Rr[:, tt, :], p, Rr[:, tt, :], ALU.add)
                    elif name in ("R32", "R64"):
                        i = dve.tensor_tensor(Rr[:, tt, :], Rr[:, tt, :], p, ALU.subtract)
                    elif name == "A4T":
                        dve.tensor_copy(A4T[:, tt, :], p)
                        i = masked(Bm32, tt, "low32")
                    elif name == "A8":
                        dve.tensor_copy(A8[:, tt, :], p)
                        i = masked(Bm64, tt, "low64")
                    else:
                        dst = {"A2": A2, "A2T": A2T, "A4": A4, "X32": Xx, "X64": Xx, "Y32": Yy, "Y64": Yy,
                               "val": val, "kcT": kcT}[name]
                        i = dve.tensor_copy(dst[:, tt, :], p)
                    i.then_inc(rnd_ev, 1)
                if name == "attn":
                    dve.wait_ge(row_exp, TT)
                    for tt in range(TT):
                        q = qkvT[:, 0:4, tt * 128:(tt + 1) * 128]
                        dve.tensor_tensor(q, q, A4T[:, tt, :].rearrange("p (h c) -> p h c", c=128), ALU.mult).then_inc(qd_done, 1)
            dve.memset(Sst[:, 0, :], 0.0).then_inc(sc_s, 1)
            for c in range(NCH):
                tt, half = c // 2, c % 2
                P = slice(64 * half, 64 * half + 64)
                dve.wait_ge(sc_k, c + 1)
                if c >= 2:
                    dve.wait_ge(sc_o, c - 1)
                dve.tensor_tensor(vnew[P, :], val[P, tt, :], ps[P, 4, :], ALU.subtract).then_inc(sc_v, 1)
                dve.wait_ge(sc_u, c + 1)
                if c >= 1:
                    dve.wait_ge(sc_o, c)
                for h in range(NHG):
                    i = dve.scalar_tensor_tensor(Sst[:, (c + 1) % 2, h * 128:(h + 1) * 128], Sst[:, c % 2, h * 128:(h + 1) * 128],
                                                 egl[:, half * 16 + tt * 4 + h:half * 16 + tt * 4 + h + 1],
                                                 ps[:, 6, h * 128:(h + 1) * 128], ALU.mult, ALU.add)
                i.then_inc(sc_s, 1)
            dve.wait_ge(sc_s, NCH + 1)
            dve.wait_ge(sc_o, NCH)
            for h in range(NHG):
                dve.wait_ge(go_std, h + 1)
                own(dve.reciprocal(qkvT[:, h, :], qkvT[:, h, :]))
                own(dve.scalar_tensor_tensor(gdnO[:, h, :], gdnO[:, h, :], param("gdn_norm"), qkvT[:, h, :], ALU.mult, ALU.mult))
                dve.tensor_tensor(mixT[:, 4 + h, :], gdnO[:, h, :], projT[:, 16 + h, PAD:PW], ALU.mult).then_inc(go_out, 1)
            dve.wait_ge(go_out, NHG)
            for k in range(KT + 1):
                if k < KT:
                    if k >= 2:
                        dve.wait_ge(m_split, k - 1)
                    dve.tensor_copy(xs[:, k % 2, :], mixT[:, k, :]).then_inc(x_full, 1)
                if k:
                    rest(mL[:, k - 1, :], mH[:, k - 1, :]).then_inc(m_split, 1)
            residual("out")
            rms_dve(1, "norm_mlp", None)
            dve.memset(small[:, 306:307], 0.0).then_inc(ff_room, RING_FF)
            for part in range(2):
                with dve.Fori(0, FT // 8) as m:
                    for j in range(4):
                        dve.wait_ge(ff_lead, m * 4 + part * FT // 2 + j + 1)
                        dve.tensor_tensor(ffL[:, m * 4 + j, :], squared[:, j, :], ffH[:, m * 4 + j, :].bitcast(f32),
                                          ALU.subtract).then_inc(ff_room, 1)
                residual(f"down{part}")
            rms_dve(2, "norm_final", hT)
            rms_dve(3, "l0_norm", None)
            dve.wait_ge(swapped_in, 8 * 16)
            for x, name in enumerate(("kpe", "vpe")):
                for g in range(NG):
                    for par in range(2):
                        P = slice(64 * par, 64 * par + 64)
                        src = nsT[P, 8 + 2 * x + g // 2, :] if g % 2 == par else swapped[P, 2 * x + g // 2, :]
                        frames = src.rearrange("p (n s) -> p s n", s=CMPS)
                        for o in range(2):
                            i = dve.tensor_tensor(blk[x][P, g, o * 8:(o + 1) * 8, :], frames[:, par::2, o:o + NCMP],
                                                  param(name)[P, o * 8:(o + 1) * 8].unsqueeze(2).to_broadcast([64, 8, NCMP]), ALU.add)
                i.then_inc(blk_done, 1)
            dve.wait_ge(cmp_mm, 1)
            dve.tensor_copy(kcmp.rearrange("p g n -> p (g n)"), ps[:, 7, 0:2 * NCMP]).then_inc(cmp_out, 1)
            dve.wait_ge(cmp_mm, 2)
            dve.tensor_copy(vcmp, ps[0:NCMP, 6, 0:NG * DH]).then_inc(cmp_out, 1)
            dve.wait_ge(cmp_out, 2)
            dve.wait_ge(cmp_h, 2)
            dve.wait_ge(g_out, 1)

            def wide(x):
                return x.unsqueeze(2).to_broadcast([128, NH, NCMP])

            for tt in range(TT):
                cols = slice(tt * NCMP, (tt + 1) * NCMP)
                own(dve.tensor_tensor(pc[tt], wide(const("slope")), const("cdist")[:, cols].unsqueeze(1).to_broadcast([128, NH, NCMP]), ALU.mult))
                dve.wait_ge(cs_mm, tt + 1)
                two = pc[tt].rearrange("p (a h) n -> p a (h n)", a=2)
                dve.tensor_tensor(two, two, ps[:, tt % 2 * 2:tt % 2 * 2 + 2, 0:8 * NCMP], ALU.add).then_inc(cs_x, 1)
                dve.wait_ge(cs_x, tt + 1)
                own(dve.tensor_reduce(cm, pc[tt], AX.X, ALU.max))
                dve.tensor_tensor(pc[tt], pc[tt], wide(cm), ALU.subtract).then_inc(cs_sub, 1)
            for tt in range(TT):
                cols = slice(tt * NCMP, (tt + 1) * NCMP)
                dve.wait_ge(cs_exp, tt + 1)
                own(dve.tensor_tensor(pc[tt], pc[tt], const("cmask")[:, cols].unsqueeze(1).to_broadcast([128, NH, NCMP]), ALU.mult))
                own(dve.tensor_reduce(cs_, pc[tt], AX.X, ALU.add))
                own(dve.tensor_scalar(cs_, cs_, 1e-30, None, ALU.max))
                own(dve.reciprocal(cs_, cs_))
                own(dve.tensor_tensor(cs_, cs_, gate[:, tt, 0, :], ALU.mult))
                dve.tensor_tensor(pc[tt], pc[tt], wide(cs_), ALU.mult).then_inc(cs_p, 1)

            def shift(u):
                t, half, qt = UNITS[u]
                W = (qt + 1) * 128
                n = u // 4
                dve.wait_ge(ds_ready, n + 1)
                dve.wait_ge(at_qk, u + 1)
                if u >= 3:
                    dve.wait_ge(at_t, u - 2)
                for b in range(2):
                    i = dve.tensor_tensor_reduce(prob[:, u % 3, b, 0:W], ps[:, u % 2 * 2 + b, 0:W],
                                                 dsl[:, n % 2, 512 - W:512], 1.0, -3e38, ALU.add, ALU.max,
                                                 amax[:, u % 3, b:b + 1])
                i.then_inc(at_s, 1)
                dve.wait_ge(at_s, u + 1)
                dve.tensor_scalar(anmax[:, u % 3, :], amax[:, u % 3, :], -1.0, None, ALU.mult).then_inc(at_m, 1)

            def weigh(u):
                t, half, qt = UNITS[u]
                W = (qt + 1) * 128
                dve.wait_ge(at_e, u + 1)
                own(dve.reciprocal(asum[:, u % 3, :], asum[:, u % 3, :]))
                own(dve.tensor_tensor(asum[:, u % 3, :], asum[:, u % 3, :], gate[:, qt, 1:3, half * 8 + t], ALU.mult))
                for b in range(2):
                    i = dve.tensor_scalar(prob[:, u % 3, b, 0:W], prob[:, u % 3, b, 0:W], asum[:, u % 3, b:b + 1], None, ALU.mult)
                i.then_inc(at_p, 1)

            def finish(t):
                dve.wait_ge(at_v, 8 * (t + 1))
                if t >= 2:
                    dve.wait_ge(at_o, t - 1)
                dve.tensor_tensor(xs[:, t % 2, :], ps[:, 6 + t % 2, :], zsT[:, t, :], ALU.mult).then_inc(x_full, 1)

            def finish_rest(t):
                rest(uL[:, t, :], uH[:, t, :]).then_inc(at_o, 1)

            for n in range(len(UNITS) + 1):
                if n < len(UNITS):
                    shift(n)
                if n >= 1:
                    weigh(n - 1)
                if n >= 12 and n % 8 == 4:
                    finish(n // 8 - 1)
                if n >= 15 and n % 8 == 7:
                    finish_rest(n // 8 - 1)
            finish(KT - 1)
            finish_rest(KT - 1)
            dt, x_, lre, th, r_, s1, sh, c1, den, nr, cr, ci, t1, t2 = (
                pk[0], pk[1], pk[2], pk[3], pk[5], pk[6], pk[7], pk[8], pk[9], pk[10], pk[11], pk[12], pk[13], pk[14])
            dve.wait_ge(ssm_a, 1)
            own(dve.tensor_scalar(lre, param("lre"), -1e-4, None, ALU.min))
            own(dve.tensor_tensor(th, param("lim"), dt, ALU.mult))
            own(dve.tensor_tensor(x_, lre, dt, ALU.mult))
            own(dve.tensor_scalar(t1, th, 1.0 / (2 * np.pi), ROUND, ALU.mult, ALU.add))
            own(dve.tensor_scalar(t1, t1, ROUND, None, ALU.subtract))
            own(dve.scalar_tensor_tensor(r_, t1, -TWO_PI[0], th, ALU.mult, ALU.add))
            own(dve.scalar_tensor_tensor(r_, t1, -TWO_PI[1], r_, ALU.mult, ALU.add))
            own(dve.scalar_tensor_tensor(r_, t1, -TWO_PI[2], r_, ALU.mult, ALU.add))
            dve.tensor_scalar(r_, r_, PI32, -PI32, ALU.min, ALU.max).then_inc(ssm_b, 1)
            dve.wait_ge(ssm_a, 4)
            own(dve.tensor_tensor(c1, sh, sh, ALU.mult))
            own(dve.tensor_scalar(c1, c1, -2.0, 1.0, ALU.mult, ALU.add))
            U, V, Pr, Pi = ptab

            def cmul(o_re, o_im, a_re, a_im, b_re, b_im, ta, tb, last=None):
                own(dve.tensor_tensor(ta, a_re, b_re, ALU.mult))
                own(dve.tensor_tensor(tb, a_im, b_im, ALU.mult))
                own(dve.tensor_tensor(o_re, ta, tb, ALU.subtract))
                own(dve.tensor_tensor(ta, a_re, b_im, ALU.mult))
                own(dve.tensor_tensor(tb, a_im, b_re, ALU.mult))
                i = dve.tensor_tensor(o_im, ta, tb, ALU.add)
                if last is None:
                    own(i)
                return i

            dve.memset(U[:, 0, :], 1.0)
            dve.memset(V[:, 0, :], 0.0)
            own(dve.tensor_copy(U[:, 1, :], c1))
            own(dve.tensor_copy(V[:, 1, :], s1))
            for m in (1, 2, 4):
                bcast = lambda x: x[:, m:m + 1, :].to_broadcast([128, m, NPAIR])
                tv = [tmpS[q][:, 0:m * NPAIR].rearrange("p (m g) -> p m g", g=NPAIR) for q in range(2)]
                cmul(U[:, m + 1:2 * m + 1, :], V[:, m + 1:2 * m + 1, :], U[:, 1:m + 1, :], V[:, 1:m + 1, :],
                     bcast(U), bcast(V), *tv)
            own(dve.tensor_tensor(Pr, U, mag, ALU.mult))
            own(dve.tensor_tensor(Pi, V, mag, ALU.mult))
            own(dve.tensor_tensor(den, lre, lre, ALU.mult))
            own(dve.tensor_tensor(t1, param("lim"), param("lim"), ALU.mult))
            own(dve.tensor_tensor(den, den, t1, ALU.add))
            own(dve.reciprocal(den, den))
            own(dve.tensor_scalar(nr, Pr[:, 1, :], -1.0, None, ALU.add))
            own(dve.tensor_tensor(t1, nr, lre, ALU.mult))
            own(dve.tensor_tensor(t2, Pi[:, 1, :], param("lim"), ALU.mult))
            own(dve.tensor_tensor(cr, t1, t2, ALU.add))
            own(dve.tensor_tensor(cr, cr, den, ALU.mult))
            own(dve.tensor_tensor(t1, Pi[:, 1, :], lre, ALU.mult))
            own(dve.tensor_tensor(t2, nr, param("lim"), ALU.mult))
            own(dve.tensor_tensor(ci, t1, t2, ALU.subtract))
            own(dve.tensor_tensor(ci, ci, den, ALU.mult))
            dve.wait_ge(s_bc, 64)
            wide16 = lambda x: x.unsqueeze(2).to_broadcast([128, NPAIR, SC])
            tv = [tmpS[q][:, 0:512].rearrange("p (g c) -> p g c", c=SC) for q in range(2)]
            own(dve.tensor_tensor(tv[0], bc[0], wide16(cr), ALU.mult))
            own(dve.tensor_tensor(tv[1], bc[1], wide16(ci), ALU.mult))
            own(dve.tensor_tensor(tv[0], tv[0], tv[1], ALU.subtract))
            own(dve.tensor_tensor(tv[1], bc[0], wide16(ci), ALU.mult))
            own(dve.tensor_tensor(bc[1], bc[1], wide16(cr), ALU.mult))
            own(dve.tensor_tensor(bc[1], bc[1], tv[1], ALU.add))
            own(dve.tensor_copy(bc[0], tv[0]))
            dve.tensor_scalar(bc[3], bc[3], -1.0, None, ALU.mult).then_inc(tables, 1)
            dve.wait_ge(tables, 1)
            residual("nout")
            rms_dve(4, "l1_norm", None)
            def powers_of_b(c):
                gs = slice(c * 8, c * 8 + 8)
                bb = [bc[q][:, gs, :].unsqueeze(2).to_broadcast([128, 8, FR, SC]) for q in range(2)]
                pp = [p[:, 0:FR, gs].rearrange("p k g -> p g k").unsqueeze(3).to_broadcast([128, 8, FR, SC]) for p in (Pr, Pi)]
                if c:
                    dve.wait_ge(bt_mm, 4 * c)
                o = [x.rearrange("p (g j c) -> p g j c", g=8, j=FR) for x in baS]
                tv = [x.rearrange("p (g j c) -> p g j c", g=8, j=FR) for x in tmpS]
                i = cmul(o[0], o[1], pp[0], pp[1], bb[0], bb[1], *tv, last=True)
                i.then_inc(ba_done, 1)
                dve.wait_ge(ba_done, c + 1)
            powers_of_b(0)
            Er, Ei = Eri
            own(dve.tensor_copy(rK[0], U[:, 8, :]))
            own(dve.tensor_copy(rK[1], V[:, 8, :]))
            own(dve.tensor_copy(mag8, mag[:, 8, :]))
            own(dve.memset(Er[:, :, 0], 1.0))
            own(dve.memset(Ei[:, :, 0], 0.0))
            m = 1
            while m < NC8:
                bcast = lambda x: x.unsqueeze(2).to_broadcast([128, NPAIR, m])
                tv = [tmpS[q][:, 0:m * NPAIR].rearrange("p (g m) -> p g m", m=m) for q in range(2)]
                cmul(Er[:, :, m:2 * m], Ei[:, :, m:2 * m], Er[:, :, 0:m], Ei[:, :, 0:m], bcast(rK[0]), bcast(rK[1]), *tv)
                if 2 * m < NC8:
                    own(dve.tensor_tensor(rK[2], rK[0], rK[0], ALU.mult))
                    own(dve.tensor_tensor(rK[3], rK[1], rK[1], ALU.mult))
                    own(dve.tensor_tensor(rK[4], rK[0], rK[1], ALU.mult))
                    own(dve.tensor_tensor(rK[0], rK[2], rK[3], ALU.subtract))
                    own(dve.tensor_scalar(rK[1], rK[4], 2.0, None, ALU.mult))
                m *= 2
            for c in range(1, 4):
                powers_of_b(c)
            dve.wait_ge(half_used, 2 * SLOT0["sin"] + 32)
            for c in range(2):
                gs = slice(c * 8, c * 8 + 8)
                cc = [bc[2 + q][:, gs, :].unsqueeze(2).to_broadcast([128, 8, FR, SC]) for q in range(2)]
                pp = [p[:, 1:9, gs].rearrange("p k g -> p g k").unsqueeze(3).to_broadcast([128, 8, FR, SC]) for p in (Pr, Pi)]
                o = [CA[q][:, gs, :].rearrange("p g (k c) -> p g k c", c=SC) for q in range(2)]
                tv = [x.rearrange("p (g j c) -> p g j c", g=8, j=FR) for x in tmpS]
                own(dve.tensor_tensor(tv[0], pp[0], cc[0], ALU.mult))
                own(dve.tensor_tensor(tv[1], pp[1], cc[1], ALU.mult))
                own(dve.tensor_tensor(o[0], tv[0], tv[1], ALU.add))
                own(dve.tensor_tensor(tv[0], pp[0], cc[1], ALU.mult))
                own(dve.tensor_tensor(tv[1], pp[1], cc[0], ALU.mult))
                dve.tensor_tensor(o[1], tv[0], tv[1], ALU.subtract).then_inc(ca_done, 1)
                dve.wait_ge(ca_done, c + 1)
            own(dve.tensor_copy(rho, mag8.unsqueeze(2).to_broadcast([128, NPAIR, NC8])))
            own(dve.memset(rho[:, :, 0], 0.0))
            flat = lambda x: x.rearrange("p g c -> p (g c)")
            Ef = [flat(x) for x in Eri]
            wf = [flat(x) for x in wri]
            dve.wait_ge(w_ev, 8)
            own(dve.tensor_tensor(rot[0], wf[0], Ef[1], ALU.mult))
            own(dve.tensor_tensor(rot[1], wf[1], Ef[1], ALU.mult))
            own(dve.tensor_tensor(wf[0], wf[0], Ef[0], ALU.mult))
            own(dve.tensor_tensor(wf[1], wf[1], Ef[0], ALU.mult))
            own(dve.tensor_tensor(wf[0], wf[0], rot[1], ALU.add))
            dve.tensor_tensor(wf[1], wf[1], rot[0], ALU.subtract).then_inc(rot_in, 1)
            dve.wait_ge(rot_in, 1)
            own(dve.tensor_tensor_scan(wf[0], flat(rho), wf[0], 0.0, ALU.mult, ALU.add))
            own(dve.tensor_tensor_scan(wf[1], flat(rho), wf[1], 0.0, ALU.mult, ALU.add))
            own(dve.tensor_tensor(flat(rho), wf[1], Ef[1], ALU.mult))
            own(dve.tensor_tensor(Ef[1], wf[0], Ef[1], ALU.mult))
            own(dve.tensor_tensor(wf[0], wf[0], Ef[0], ALU.mult))
            own(dve.tensor_tensor(wf[1], wf[1], Ef[0], ALU.mult))
            own(dve.tensor_tensor(wf[0], wf[0], flat(rho), ALU.subtract))
            dve.tensor_tensor(wf[1], wf[1], Ef[1], ALU.add).then_inc(x_done, 1)
            for part in range(2):
                dve.wait_ge(y_in, (part + 1) * 32 * 16)
                if part:
                    dve.wait_ge(k_mm, 8)
                for k in range(4 * part, 4 * part + 4):
                    o = yD[:, k, :].rearrange("p (c j) -> p j c", j=FR)
                    u_ = suP[:, k, :].rearrange("p (j c) -> p j c", c=NC8)
                    y_ = yF[:, k, :].rearrange("p (j c) -> p j c", c=NC8)
                    dve.scalar_tensor_tensor(o, u_, param("d_skip")[:, k:k + 1], y_, ALU.mult, ALU.add).then_inc(y_d, 1)
                for k in range(4 * part, 4 * part + 4):
                    dve.wait_ge(y_lead, k + 1)
                    dve.tensor_tensor(uL[:, k, :], yD[:, k, :], uH[:, k, :].bitcast(f32), ALU.subtract).then_inc(y_g, 1)
            with dve.Fori(0, 4) as m:
                for x in range(2):
                    dve.wait_ge(glu_s, m * 2 + x + 1)
                    dve.tensor_tensor(gprod[:, x, :], ps[:, 2 * x, :], sg[:, x, :], ALU.mult).then_inc(tile_evicted, 2)
                    dve.wait_ge(tile_evicted, m * 4 + TILE0["glu"] + 2 * x + 2)
                    dve.tensor_tensor(gprod[:, x, :], gprod[:, x, :], szT[:, m * 2 + x, :], ALU.mult).then_inc(glu_m, 1)
                for x in range(2):
                    dve.wait_ge(glu_lead, m * 2 + x + 1)
                    dve.tensor_tensor(mL[:, m * 2 + x, :], gprod[:, x, :], mH[:, m * 2 + x, :].bitcast(f32),
                                      ALU.subtract).then_inc(glu_o, 1)
                dve.wait_ge(glu_o, m * 2 + 2)
            residual("sout")
            rms_dve(5, "final_norm", hT)


def constants():
    p, c = np.arange(128)[:, None], np.arange(128)[None, :]
    same = p // CH == c // CH
    t = {}
    t["ident"] = p == c
    t["ones"] = np.ones((128, 128))
    t["cumsum"] = same & (p <= c)
    t["block"] = same
    t["half"] = np.concatenate([np.broadcast_to(p // CH == i, (128, 128)) for i in range(2)], 1)
    t["maskneg"] = np.where(same & (c <= p), 0.0, NEG)
    t["neg16"] = np.where((p // 16 == c // 16) & (c < p), -1.0, 0.0)
    t["low32"] = (p // 32 == c // 32) & (p // 16 > c // 16)
    t["low64"] = (p // 64 == c // 64) & (p // 32 > c // 32)
    k = np.arange(T)[None, :]
    ahead = k - (T - 128) - p
    t["dist"] = np.where(ahead <= 0, ahead, NEG)
    n = np.arange(NCMP)[None, None, :]
    tok = p[:, :, None] + 128 * np.arange(TT)[None, :, None]
    seen = CMPS * n + CMPB - 1 <= tok
    t["cdist"] = np.where(seen, CMPS * n + 0.5 * (CMPB - 1) - tok, NEG).reshape(128, -1)
    t["cmask"] = seen.reshape(128, -1)
    t["slope"] = np.broadcast_to(2.0 ** (-8.0 * (np.array(HALF_ORDER) + 1) / NH), (128, NH))
    t["invcount"] = np.broadcast_to(np.concatenate(
        [1.0 / np.minimum(np.arange(1, PAD + 1), 2 ** (g + 1)) for g in range(4)]), (128, 4 * PAD))
    return np.concatenate([np.asarray(t[name], np.float32) for name in CONST_W], 1)


def slots(w):
    k, m = w.shape
    return w.reshape(k // 128, 128, m // 128, 128).transpose(2, 1, 0, 3).reshape(m // 128, 128, k)


def by_partition(v):
    return v.reshape(-1, 128).T


def tall(w):
    return w.reshape(-1, 128, w.shape[1]).transpose(1, 0, 2).reshape(128, -1)


def lay_out(i):
    a = {}
    w_in = i["w_in"][0]
    nsa = i["l0_w_in_2"]
    qcols = np.concatenate([h * DH + np.arange(DH) for h in HEAD_ORDER])
    s = NH * DH
    kv = NG * DH
    zcols = s + 6 * kv + 3 * NH + qcols
    branches = [nsa[:, s + b * kv:s + (b + 1) * kv] for b in range(6)]
    nsa_feature = np.concatenate([nsa[:, qcols], branches[0], branches[1], branches[2], branches[4]], 1)
    v_both = np.concatenate([branches[3], branches[5]], 1)
    val = v_both.reshape(4, 2, 128, 512).transpose(0, 2, 1, 3).reshape(4, 128, 1024)
    glu = i["l1_w_glu_2"].reshape(D, 2, KT, 128).transpose(0, 2, 1, 3).reshape(D, 2 * D)
    up = slots(i["w_up"][0])
    down = i["w_down"][0].reshape(4, D, D)
    down = [np.stack([slots(d) for d in down[2 * n:2 * n + 2]], 1).reshape(16, 128, 1024) for n in range(2)]
    stream = np.concatenate([
        slots(w_in[:, :20 * 128]), slots(i["w_out"][0]), up[:16], down[0], up[16:], down[1],
        slots(nsa_feature), val, slots(nsa[:, zcols]), slots(i["l0_w_out_2"][qcols]),
        slots(i["l1_w_in_2"]), slots(glu), slots(i["l1_w_out_2"])])
    a["wstream"] = stream.reshape(-1, 128, 2, 512).transpose(0, 2, 1, 3).reshape(-1, 128, 512)
    a["x"] = i["x"][0].T.reshape(KT, 128, T).transpose(1, 0, 2)
    a["consts"] = constants()
    a["w_ab"] = tall(w_in[:, 20 * 128:])
    a["w_gate"] = tall(nsa[:, s + 6 * kv + np.concatenate([b * NH + np.array(HALF_ORDER) for b in range(3)])])
    a["w_pool"] = i["w_pool"][0].transpose(1, 0, 2).reshape(128, 512)
    for n in "kv":
        a[f"cmp_{n}_w1"] = tall(i[f"l0_cmp_{n}_w1_2"])
        a[f"cmp_{n}_w2"] = tall(i[f"l0_cmp_{n}_w2_2"])
    pair = lambda v: v.reshape(NPAIR, 128, -1).transpose(1, 0, 2).reshape(128, -1)
    a["ssm_b_re"] = pair(i["l1_b_re_2"])
    a["ssm_b_im"] = pair(i["l1_b_im_2"])
    a["ssm_c_re"] = pair(i["l1_c_re_2"].transpose(0, 2, 1))
    a["ssm_c_im"] = pair(i["l1_c_im_2"].transpose(0, 2, 1))
    t = dict(norm_mix=by_partition(i["norm_mix"]), norm_mlp=by_partition(i["norm_mlp"]),
             norm_final=by_partition(i["norm_final"]), l0_norm=by_partition(i["l0_norm_2"]),
             l1_norm=by_partition(i["l1_norm_2"]), final_norm=by_partition(i["final_norm_2"]),
             conv=i["conv_w"][0].reshape(CONV, 12, 128).transpose(2, 1, 0).reshape(128, -1),
             pool_scale=by_partition(i["pool_scale"]), gdn_norm=i["gdn_norm"].T,
             a_log=np.broadcast_to(np.tile(i["a_log"][0], TT), (128, 16)),
             dt_bias=np.broadcast_to(np.tile(i["dt_bias"][0], TT), (128, 16)),
             kpe=i["l0_cmp_k_pe_2"].reshape(CMPB // 2, 128).T, vpe=i["l0_cmp_v_pe_2"].reshape(CMPB // 2, 128).T,
             d_skip=by_partition(i["l1_d_2"]),
             log_dt=np.repeat(i["l1_log_dt_2"].reshape(NPAIR, 2).T, SP, 0),
             lre=pair(i["l1_lambda_re_2"]), lim=pair(i["l1_lambda_im_2"]))
    a["params"] = np.concatenate([t[name] for name in PARAM_W], 1)
    return {n: np.ascontiguousarray(v) for n, v in a.items()}


HEAD_ORDER = [(2 * gp + g2) * 4 + r for gp in range(2) for r in range(4) for g2 in range(2)]
HALF_ORDER = HEAD_ORDER[0::2] + HEAD_ORDER[1::2]


def kernel(**inputs):
    from concourse import bacc
    from concourse.bass_utils import run_bass_kernel_spmd

    nc = bacc.Bacc("TRN2", target_bir_lowering=False, num_devices=1, dynamic_dma_scratch_size=64)
    arrays = lay_out({n: np.asarray(v) for n, v in inputs.items()})
    A = {n: nc.dram_tensor(n, v.shape, mybir.dt.from_np(v.dtype), kind="ExternalInput").ap() for n, v in arrays.items()}
    out = nc.dram_tensor("out", (128, KT, T), mybir.dt.float32, kind="ExternalOutput").ap()
    scratch = {"u": nc.dram_tensor("u_scratch", (128, KT, T), mybir.dt.float32).ap(),
               "y": nc.dram_tensor("y_scratch", (2, 128, SG // 2, NC8), mybir.dt.float32).ap()}
    build(nc, A, scratch, out)
    r = run_bass_kernel_spmd(nc, [arrays], core_ids=[0])
    y = r.results[0]["out"]
    return y.transpose(1, 0, 2).reshape(D, T).T.reshape(1, T, D)
```

```python
import numpy as np
import concourse.bass as bass
from concourse import mybir
from contextlib import ExitStack

D = 1024
T = 512
KT = D // 128
TT = T // 128
EPS = 1e-6
NEG = -1e30

NHG = 4
CH = 64
NCH = T // CH
FT = 4 * D // 128
PAD = 16
PW = T + PAD
CONV = 4

NH = 16
NG = 4
DH = 64
CMPB, CMPS = 32, 16
NCMP = (T - CMPB) // CMPS + 1

SG = 64
SC = 16
SP = 64
FR = 8
NC8 = T // FR
NPAIR = SG // 2

SLOTS = dict(inp=20, out=8, up0=16, down0=16, up1=16, down1=16, nsa=16, val=4, zed=8, nout=8, sin=16, glu=16, sout=8)
TILES = dict(inp=20, out=8, up0=16, down0=8, up1=16, down1=8, nsa=16, val=4, zed=8, nout=8, sin=16, glu=16, sout=8)


def bases(counts):
    at, out = 0, {}
    for name, n in counts.items():
        out[name] = at
        at += n
    return out, at


SLOT0, NSLOT = bases(SLOTS)
TILE0, NTILE = bases(TILES)

_mid = round((2 * np.pi - 6.28125) * 2.0 ** 21) / 2.0 ** 21
TWO_PI = [6.28125, _mid, 2 * np.pi - 6.28125 - _mid]
PI32 = float(np.nextafter(np.float32(np.pi), np.float32(0)))
ROUND = 1.5 * 2.0 ** 23

CONST_W = dict(ident=128, ones=128, cumsum=128, block=128, half=256, maskneg=128, neg16=128,
               low32=128, low64=128, dist=512, cdist=TT * NCMP, cmask=TT * NCMP, slope=NH,
               invcount=4 * PAD)
CONST_AT, NCONST = bases(CONST_W)
PARAM_W = dict(norm_mix=8, norm_mlp=8, norm_final=8, l0_norm=8, l1_norm=8, final_norm=8,
               conv=12 * CONV, pool_scale=4, gdn_norm=1, a_log=16, dt_bias=16, kpe=CMPB // 2, vpe=CMPB // 2,
               d_skip=8, log_dt=NPAIR, lre=NPAIR, lim=NPAIR)
PARAM_AT, NPARAM = bases(PARAM_W)


def build(nc, A, scratch, out_dram):
    f32 = mybir.dt.float32
    ALU = mybir.AluOpType
    ACT = mybir.ActivationFunctionType
    AX = mybir.AxisListType

    ctx = ExitStack()
    with ctx:
        def sb(name, shape):
            return ctx.enter_context(nc.sbuf_tensor(name, shape, f32))

        def sem(name):
            return ctx.enter_context(nc.semaphore(name))

        f32r = mybir.dt.float32r
        plan = [nc.sbuf_base + -nc.sbuf_base % 64]

        def place(name, shape, dtype=f32, over=None, at=0):
            size = 4 * int(np.prod(shape[1:]))
            if over is None:
                start = plan[0]
                plan[0] += size + -size % 64
            else:
                start = PLACE[over] + at
            PLACE[name] = start
            return nc.alloc_sbuf_tensor_at(name, shape, dtype, offset=start)

        PLACE = {}
        KB = 1024
        hT = place("hT", [128, KT, T])
        uT = place("uT", [128, KT, T])
        mixT = place("mixT", [128, KT, T])
        uH = place("uH", [128, KT, T], f32r, over="uT")
        uL = place("uL", [128, KT, T], f32r, over="mixT")
        RING_FF = 4
        RING = 4
        raw = place("raw", [128, RING, 512])
        wh = place("wh", [128, RING, 512], f32r)
        wl = place("wl", [128, RING, 512], f32r)
        bigA = place("bigA", [128, 16704])
        bigB = place("bigB", [128, 16384])
        ffH = place("ffH", [128, FT // 2, T], f32r, over="bigA")
        ffL = place("ffL", [128, FT // 2, T], f32r, over="bigA", at=32 * KB)
        mH = place("mH", [128, KT, T], f32r, over="bigB")
        mL = place("mL", [128, KT, T], f32r, over="bigB", at=32 * KB)
        consts = place("const_table", [128, NCONST])
        params = place("param_table", [128, NPARAM])
        rms = place("rms", [128, T])
        xs = place("xs", [128, 2, T])
        small = place("small", [128, 704])
        wabH, wabL = place("wabH", [128, 64], f32r), place("wabL", [128, 64], f32r)
        wgH, wgL = (place(n, [128, 384], f32r, over="bigB", at=4 * (15360 + 384 * i)) for i, n in enumerate(("wgH", "wgL")))
        ps = ctx.enter_context(nc.psum_tensor("ps", [128, 8, 512], f32))

        def const(name):
            a = CONST_AT[name]
            return consts[:, a:a + CONST_W[name]]

        def param(name):
            a = PARAM_AT[name]
            return params[:, a:a + PARAM_W[name]]

        def view(t, at, *dims):
            n = int(np.prod(dims))
            v = t[:, at:at + n]
            if len(dims) == 2:
                return v.rearrange("p (a b) -> p a b", b=dims[1])
            if len(dims) == 3:
                return v.rearrange("p (a b c) -> p a b c", b=dims[1], c=dims[2])
            return v

        uflat = uT[:, :, :].rearrange("p a b -> p (a b)")
        ident, ones = const("ident"), const("ones")

        projT = view(bigA, 0, 20, PW)
        qkvT = view(bigA, 20 * PW, 12, T)
        GA = TT * NHG * 128
        arr = [view(bigB, i * GA, TT, NHG * 128) for i in range(8)]
        brr = [view(bigA, 4 * PW + i * GA, TT, NHG * 128) for i in range(3)]
        urr = [view(uflat, i * GA, TT, NHG * 128) for i in range(2)]
        dec, kd, kbe, vb, Mm, aiT, Aa, Xx = arr
        A2, A2T, A4 = brr
        A4T, Rr = urr
        kcT, val, AT, A8, Yy, Bm32, Bm64, aS = kbe, vb, Xx, Aa, A2, A2T, A4, A2
        gB = Mm
        abS = small[:, 0:32].rearrange("p (t c) -> p t c", c=8)
        w_ab = small[:, 32:96]
        ab_rows = xs[0:8, 1, :]
        gx, ga, ge, gl, gg, bta, gc, eg, ekd, beg = (small[:, 96 + 16 * i:112 + 16 * i] for i in range(10))
        nalog = small[:, 256:272]
        egl = small[:, 272:304]
        Sst = view(mixT[:, :, :].rearrange("p a b -> p (a b)"), 4 * T, 2, 512)
        vnew = mixT[:, 6, :]
        l2n = view(bigB, 10240, 4, T)
        mixed = projT[:, 0:4, PAD:PW]
        sq_qk = view(bigB, 12288, 8, T)
        gdnO = view(uflat, 0, NHG, T)
        w_pool = view(bigB, 0, 4, 128)
        ptmp = [bigB[:, 1024:1024 + PW], bigB[:, 2048:2048 + PW]]
        pooled = view(bigB, 4096, 4, T)

        eps_ap, one_ap, zero_ap = small[:, 304:305], small[:, 305:306], small[:, 307:308]

        nsT = view(bigA, 0, 16, T)
        zsT = view(bigA, 8192, KT, T)
        vtok = view(bigA, 12288, TT, 512)
        relu, squared = view(bigB, 8192, 4, T), view(bigB, 10240, 4, T)
        swapped = view(bigB, 8192, 4, T)
        blk = [view(bigB, 10240 + 1984 * i, NG, CMPB // 2, NCMP) for i in range(2)]
        kcmp = view(bigA, 16256, 2, 2 * NCMP)
        vcmp = bigA[0:NCMP, 16384:16384 + NG * DH]
        w1 = [bigB[:, 0:4096], bigB[:, 4096:8192]]
        w2 = [bigB[:, 14208:14336], bigB[:, 14336:14464]]
        w_gate = bigB[:, 14464:14848]
        hid = [view(bigB, 14848 + 248 * i, 2, NG, NCMP) for i in range(2)]
        gate_rows = xs[0:3 * NH, 0, :]
        gate = small[:, 308:500].rearrange("p (t b h) -> p t b h", b=3, h=NH)
        pcT = bigB[0:NCMP, 0:NH * T].rearrange("p (h q) -> p h q", q=T)
        pc = [view(bigB, 13312 + i * 496, NH, NCMP) for i in range(TT)]
        dsl = view(bigB, 8192, 2, 512)
        prob = view(bigB, 9216, 3, 2, 512)
        probT = view(bigB, 12288, 3, 2, 512)
        cm, cs_ = small[:, 500:516], small[:, 516:532]
        amax = small[:, 532:538].rearrange("p (u b) -> p u b", b=2)
        anmax = small[:, 538:544].rearrange("p (u b) -> p u b", b=2)
        asum = small[:, 544:550].rearrange("p (u b) -> p u b", b=2)
        UNITS = [(t, half, qt) for t in range(KT) for half in range(2) for qt in range(TT)]

        suP = view(bigA, 0, KT, T)
        szT = view(bigA, 4096, KT, T)
        uc = view(bigA, 8192, SG, NC8)
        wri = [view(bigA, 12288 + 2048 * i, NPAIR, NC8) for i in range(2)]
        yF = view(bigB, 8192, KT, T)
        yD = view(bigB, 12288, KT, T)
        ptab = ([view(bigA, 12288 + 288 * i, 9, NPAIR) for i in range(2)]
                + [view(consts, CONST_AT["dist"] + 288 * i, 9, NPAIR) for i in range(2)])
        pk = [bigA[:, 13440 + 32 * i:13472 + 32 * i] for i in range(16)]
        BWT = [view(bigB, 4096 * i, NPAIR, 128) for i in range(2)]
        Tm = view(bigB, 4096, SG // 2, 128)
        Kl = bigB[0:SC, 0:4096].rearrange("p (g c) -> p g c", c=128)
        Eri = [view(bigB, 8192 + 2048 * i, NPAIR, NC8) for i in range(2)]
        tmpS = [bigB[:, 12288 + 1024 * i:13312 + 1024 * i] for i in range(2)]
        rho = view(bigB, 12288, NPAIR, NC8)
        rot = [bigB[:, 2048 * i:2048 * i + 2048] for i in range(2)]
        bc = [view(bigB, 14336 + 512 * i, NPAIR, SC) for i in range(4)]
        CA = [view(uflat, 0, NPAIR, 128), view(mixT[:, :, :].rearrange("p a b -> p (a b)"), 0, NPAIR, 128)]
        mag = view(bigA, 13952, 9, NPAIR)
        mag8 = small[:, 308:340]
        rK = [small[:, 340 + 32 * i:372 + 32 * i] for i in range(6)]
        baS = [bigA[:, 14240 + 1024 * i:15264 + 1024 * i] for i in range(2)]
        sg = view(bigB, 4096, 2, T)
        gprod = view(bigB, 5120, 2, T)

        s_w1 = sem("cmp_w1_loaded")
        swapped_in = sem("halves_swapped")
        s_w2 = sem("cmp_w2_loaded")
        s_wgate, wgate_split = sem("w_gate_loaded"), sem("w_gate_split")
        g_mm, g_rows, g_out = sem("gate_product"), sem("gate_rows"), sem("gates_ready")
        blk_done, cmp_h, cmp_act, cmp_mm, cmp_out = (sem(f"compress_{n}") for n in
                                                     ("windows", "hidden", "silu", "product", "ready"))
        cs_sub = sem("cmp_max_subtracted")
        cs_mm, cs_x, cs_exp, cs_p, cs_t, cs_ev = (sem(f"cmp_{n}") for n in
                                                  ("scores", "shifted", "exp", "probs", "transposed", "probsT"))
        ds_ready = sem("slopes_ready")
        at_qk, at_s, at_m, at_e, at_p, at_t, at_ev, at_v, at_o = (sem(f"att_{n}") for n in
            ("scores", "scores_read", "max", "exp", "probs", "transposed", "probsT", "value", "out"))
        s_bc = sem("ssm_bc_loaded")
        ssm_a, ssm_b = sem("ssm_scalar_engine"), sem("ssm_params")
        ba_done, bt_mm, bt_ev = sem("ssm_b_powers"), sem("ssm_b_transposed"), sem("ssm_b_stored")
        ca_done, ca_pool = sem("ssm_c_powers"), sem("ssm_c_powers_gpsimd")
        tables, ca_chain = sem("ssm_tables"), sem("ssm_c_products")
        u_stored, uc_in = sem("u_stored"), sem("u_regrouped")
        w_mm, w_ev = sem("chunk_input_product"), sem("chunk_input_stored")
        rot_in, x_done = sem("rotated"), sem("chunk_states")
        k_mm, k_ev = sem("lag_kernel_product"), sem("lag_kernel_stored")
        t_zero, t_in = sem("lag_matrix_zero"), sem("lag_matrix_filled")
        y_mm, y_ev, y_stored, y_in, y_d, y_act, y_g = (sem(f"y_{n}") for n in (
            "product", "evicted", "stored", "regrouped", "skip", "gelu", "split"))
        glu_s, glu_m, glu_lead, glu_o = sem("glu_sigmoid"), sem("glu_gated"), sem("glu_lead"), sem("glu_out")
        y_lead = sem("y_lead")

        s_x = sem("x_loaded")
        s_const = sem("consts_loaded")
        s_param = sem("params_loaded")
        s_wab, wab_split = sem("w_ab_loaded"), sem("w_ab_split")
        s_wpool = sem("w_pool_loaded")
        half_loaded = [sem(f"half{j}_loaded") for j in range(RING)]
        half_lead, half_split = sem("half_lead"), sem("half_split")
        half_used = sem("half_used")
        x_full, x_lead = sem("x_full"), sem("x_lead")
        tile_evicted = sem("tile_evicted")
        rms_sq, rms_sum, rms_std, rms_out = sem("rms_squares"), sem("rms_sum"), sem("rms_std"), sem("rms_out")
        dvc = sem("dve_chain")
        acc_ = sem("act_chain")
        pads0 = sem("pads_zero")
        ab_ready, ab_copied = sem("ab_ready"), sem("ab_copied")
        pooled_done, pool_mm, pool_out = sem("pooled"), sem("pool_product"), sem("pool_out")
        conv_step, conv_silu = sem("conv_step"), sem("conv_silu")
        l2_sq, l2_sum, l2_std, l2_out = sem("l2_squares"), sem("l2_sum"), sem("l2_std"), sem("l2_out")
        gate_a, gate_b = sem("gate_scalar_engine"), sem("gate_vector_engine")
        gate_mm = sem("gate_cumsum")
        row_mm, row_dec, row_exp, dec_exp = sem("row_sums"), sem("row_masked"), sem("row_exp"), sem("decay_ready")
        qd_done = sem("q_decayed")
        rnd_mm, rnd_ev = sem("round_product"), sem("round_evicted")
        sc_k, sc_v, sc_u, sc_s, sc_o, sc_oe = (sem(f"scan_{n}") for n in
                                              ("k_state", "v_new", "update", "state", "out", "out_copied"))
        go_sq, go_sum, go_std = sem("gdn_squares"), sem("gdn_sum"), sem("gdn_std")
        ff_sq, ff_lead, ff_room = sem("ff_squared"), sem("ff_lead"), sem("ff_places_freed")
        m_lead, m_split = sem("mixed_lead"), sem("mixed_split")
        out_done = sem("out_written")

        block = ctx.enter_context(nc.Block())

        ROUNDS = ["attn", "attnT", "ktok", "vtok", "gram", "AT", "A2", "A2T", "R2", "A4", "A4T", "R4",
                  "A8", "R8", "X32", "Y32", "R32", "X64", "Y64", "R64", "val", "kcT"]

        def hd(x, tt, h):
            return x[:, tt, h * 128:(h + 1) * 128]

        @block.sync
        def _(sp):
            for j in range(RING):
                sp.dma_start(raw[:, j, :], A["wstream"][j]).then_inc(half_loaded[j], 16)
            with sp.Fori(1, 2 * NSLOT // RING) as m:
                for j in range(RING):
                    sp.wait_ge(half_split, m * RING + j - RING + 1)
                    sp.dma_start(raw[:, j, :], A["wstream"][m * RING + j]).then_inc(half_loaded[j], 16)

        @block.tensor
        def _(pe):
            u_parts = (uH, uL)

            def rms_pe(n):
                for k in range(KT):
                    pe.wait_ge(rms_sq, n * KT + k + 1)
                    i = pe.matmul(ps[:, 4, :], ones, uT[:, k, :], start=k == 0, stop=k == KT - 1)
                i.then_inc(rms_sum, 1)

            def product(out, left, right, first, last):
                (lh, ll), (rh, rl) = left, right
                pe.matmul(out, lh, rh, start=first, stop=False)
                pe.matmul(out, lh, rl, start=False, stop=False)
                return pe.matmul(out, ll, rh, start=False, stop=last)

            def half_slot(out, n, j, right, first, last, ready=None):
                pe.wait_ge(half_split, n + 1)
                for k in range(4):
                    if ready is not None:
                        pe.wait_ge(ready[0], ready[1] + k + 1)
                    i = product(out, (wh[:, j, k * 128:(k + 1) * 128], wl[:, j, k * 128:(k + 1) * 128]),
                                right(k), first and k == 0, last and k == 3)
                i.then_inc(half_used, 1)

            def tile_group(name, m, x, first=False, ready=None):
                for t in range(4):
                    if not first:
                        pe.wait_ge(tile_evicted, m * 4 + TILE0[name] + t - 3)
                    for h in range(2):
                        half_slot(ps[:, t, :], m * 8 + 2 * SLOT0[name] + 2 * t + h, (2 * t + h) % RING,
                                  lambda k: (x[0][:, h * 4 + k, :], x[1][:, h * 4 + k, :]), h == 0, h == 1,
                                  (ready[0], ready[1] + 4 * h) if ready is not None and t == 0 else None)

            def linear(name, x=(uH, uL), first=False, ready=None):
                tile_group(name, 0, x, first=first, ready=ready)
                with pe.Fori(1, TILES[name] // 4) as m:
                    tile_group(name, m, x)

            pe.wait_ge(s_const, 16)
            rms_pe(0)
            tile_group("inp", 0, u_parts, first=True, ready=(rms_out, 0))
            pe.wait_ge(wab_split, 2)
            for k in range(KT):
                i = product(ps[0:8, 5, :], (wabH[:, k * 8:(k + 1) * 8], wabL[:, k * 8:(k + 1) * 8]),
                            (uH[:, k, :], uL[:, k, :]), k == 0, k == KT - 1)
            i.then_inc(ab_ready, 1)

            def l2_sums(lo, hi):
                for i in range(lo, hi):
                    pe.wait_ge(l2_sq, i + 1)
                    if i < 1:
                        pe.wait_ge(ab_copied, 2)
                    if i >= 4:
                        pe.wait_ge(l2_std, i - 3)
                    pe.matmul(ps[:, 4 + i % 4, :], ones, sq_qk[:, i, :], start=True, stop=True).then_inc(l2_sum, 1)

            tile_group("inp", 1, u_parts)
            pe.wait_ge(ab_copied, 1)
            for tt in range(TT):
                i = pe.transpose(ps[:, 5, tt * 8:(tt + 1) * 8], ab_rows[:, tt * 128:(tt + 1) * 128], ident[0:8, 0:8])
            i.then_inc(ab_ready, 1)
            pe.wait_ge(s_wpool, 16)
            for g in range(4):
                pe.wait_ge(pooled_done, g + 1)
                if g >= 2:
                    pe.wait_ge(pool_out, g - 1)
                pe.matmul(ps[:, 6 + g % 2, :], w_pool[:, g, :], pooled[:, g, :], start=True, stop=True).then_inc(pool_mm, 1)
            tile_group("inp", 2, u_parts)
            tile_group("inp", 3, u_parts)
            l2_sums(0, 2)
            pe.wait_ge(gate_b, 2)
            pe.wait_ge(pool_out, 4)
            pe.matmul(ps[:, 6, 0:16], const("cumsum"), gg, start=True, stop=True)
            pe.matmul(ps[:, 6, 16:32], const("block"), gg, start=True, stop=True)
            for c in range(2):
                i = pe.matmul(ps[:, 6, 32 + 16 * c:48 + 16 * c], const("half")[:, 128 * c:128 * c + 128], gg,
                              start=True, stop=True)
            i.then_inc(gate_mm, 1)
            tile_group("inp", 4, u_parts)
            pe.wait_ge(gate_a, 5)
            pe.wait_ge(gate_b, 4)
            l2_sums(2, 8)
            for tt in range(TT):
                if tt == 0:
                    pe.wait_ge(gate_b, 3)
                pe.wait_ge(tile_evicted, 17 + tt)
                for h in range(NHG):
                    i = pe.matmul(ps[:, tt, h * 128:(h + 1) * 128], hd(gB, tt, h), const("cumsum"),
                                  start=True, stop=True)
                i.then_inc(row_mm, 1)

            def qk(i, tt, h):
                return qkvT[:, i * 4 + h, tt * 128:(tt + 1) * 128]

            def operands(name, tt, h):
                return {
                    "attn": lambda: (qk(0, tt, h), qk(1, tt, h)),
                    "attnT": lambda: (hd(aS, tt, h), None),
                    "ktok": lambda: (qk(1, tt, h), None),
                    "vtok": lambda: (qk(2, tt, h), None),
                    "gram": lambda: (qk(1, tt, h), qk(1, tt, h)),
                    "AT": lambda: (hd(Aa, tt, h), None),
                    "A2": lambda: (hd(AT, tt, h), hd(Aa, tt, h)),
                    "A2T": lambda: (hd(Aa, tt, h), hd(AT, tt, h)),
                    "R2": lambda: (hd(A2, tt, h), hd(Rr, tt, h)),
                    "A4": lambda: (hd(A2T, tt, h), hd(A2, tt, h)),
                    "A4T": lambda: (hd(A2, tt, h), hd(A2T, tt, h)),
                    "R4": lambda: (hd(A4, tt, h), hd(Rr, tt, h)),
                    "A8": lambda: (hd(A4T, tt, h), hd(A4, tt, h)),
                    "R8": lambda: (hd(A8, tt, h), hd(Rr, tt, h)),
                    "X32": lambda: (hd(Rr, tt, h), None),
                    "Y32": lambda: (hd(Bm32, tt, h), hd(Rr, tt, h)),
                    "R32": lambda: (hd(Xx, tt, h), hd(Yy, tt, h)),
                    "X64": lambda: (hd(Rr, tt, h), None),
                    "Y64": lambda: (hd(Bm64, tt, h), hd(Rr, tt, h)),
                    "R64": lambda: (hd(Xx, tt, h), hd(Yy, tt, h)),
                    "val": lambda: (hd(Rr, tt, h), hd(vb, tt, h)),
                    "kcT": lambda: (hd(kbe, tt, h), hd(Rr, tt, h)),
                }[name]()

            pe.wait_ge(l2_out, 8)
            for r, name in enumerate(ROUNDS):
                if name == "vtok":
                    pe.wait_ge(conv_silu, 12)
                for tt in range(TT):
                    if r:
                        pe.wait_ge(rnd_ev, 4 * (r - 1) + tt + 1)
                    for h in range(NHG):
                        left, right = operands(name, tt, h)
                        o = ps[:, 4 + tt, h * 128:(h + 1) * 128]
                        if right is None:
                            i = pe.transpose(o, left, ident)
                        else:
                            i = pe.matmul(o, left, right, start=True, stop=True)
                    i.then_inc(rnd_mm, 1)

            pe.wait_ge(rnd_ev, 4 * len(ROUNDS))
            pe.wait_ge(qd_done, TT)
            for c in range(NCH):
                tt, half = c // 2, c % 2
                P = slice(64 * half, 64 * half + 64)
                S = Sst[:, c % 2, :]
                for pair in range(2):
                    pe.wait_ge(sc_s, 2 * c + pair + 1)
                    for h in (2 * pair, 2 * pair + 1):
                        i = pe.matmul(ps[P, pair, h * 128:(h + 1) * 128], kcT[:, tt, h * 128 + 64 * half:h * 128 + 64 * half + 64],
                                      S[:, h * 128:(h + 1) * 128], start=True, stop=True)
                    i.then_inc(sc_k, 1)
                for pair in range(2):
                    pe.wait_ge(sc_v, 2 * c + pair + 1)
                    for h in (2 * pair, 2 * pair + 1):
                        i = pe.matmul(ps[:, 2 + pair, h * 128:(h + 1) * 128], kd[P, tt, h * 128:(h + 1) * 128],
                                      vnew[P, h * 128:(h + 1) * 128], start=True, stop=True)
                    i.then_inc(sc_u, 1)
                if c >= 2:
                    pe.wait_ge(sc_oe, c - 1)
                for h in range(NHG):
                    o = ps[:, 5 + 2 * half, h * CH:(h + 1) * CH]
                    pe.matmul(o, S[:, h * 128:(h + 1) * 128], qkvT[:, h, c * CH:(c + 1) * CH], start=True, stop=False)
                    i = pe.matmul(o, vnew[P, h * 128:(h + 1) * 128],
                                  aiT[P, tt, h * 128 + 64 * half:h * 128 + 64 * half + 64], start=False, stop=True)
                i.then_inc(sc_o, 1)
            for h in range(NHG):
                pe.wait_ge(go_sq, h + 1)
                pe.matmul(ps[:, 4 + h, :], ones, urr[1].rearrange("p a b -> p (a b)")[:, h * T:(h + 1) * T],
                          start=True, stop=True).then_inc(go_sum, 1)
            pe.wait_ge(sc_s, 2 * (NCH + 1))
            linear("out", x=(mH, mL), ready=(m_split, 0))
            rms_pe(1)
            for part in range(2):
                linear(f"up{part}", ready=(rms_out, KT) if part == 0 else None)
                pe.wait_ge(ff_room, RING_FF + FT // 2 * (part + 1))
                with pe.Fori(0, 2) as m:
                    for t in range(4):
                        pe.wait_ge(tile_evicted, m * 4 + TILE0[f"down{part}"] + t - 3)
                        for h in range(4):
                            half_slot(ps[:, t, :], m * 16 + 2 * SLOT0[f"down{part}"] + 4 * t + h, h,
                                      lambda k: (ffH[:, h * 4 + k, :], ffL[:, h * 4 + k, :]), h == 0, h == 3)
            rms_pe(2)
            rms_pe(3)
            linear("nsa", ready=(rms_out, 3 * KT))
            pe.wait_ge(tile_evicted, TILE0["val"])
            for k in range(KT):
                pe.wait_ge(half_split, 2 * SLOT0["val"] + k + 1)
                for tt in range(TT):
                    tok = slice(tt * 128, (tt + 1) * 128)
                    i = product(ps[:, tt, :], (uH[:, k, tok], uL[:, k, tok]), (wh[:, k % RING, :], wl[:, k % RING, :]),
                                k == 0, k == KT - 1)
                i.then_inc(half_used, 1)
            pe.wait_ge(wgate_split, 2)
            for k in range(KT):
                i = product(ps[0:3 * NH, 5, :], (wgH[:, k * 48:(k + 1) * 48], wgL[:, k * 48:(k + 1) * 48]),
                            (uH[:, k, :], uL[:, k, :]), k == 0, k == KT - 1)
            i.then_inc(g_mm, 1)
            linear("zed")
            pe.wait_ge(g_rows, 1)
            for tt in range(TT):
                i = pe.transpose(ps[:, 5, tt * 48:(tt + 1) * 48], gate_rows[:, tt * 128:(tt + 1) * 128], ident[0:48, 0:48])
            i.then_inc(g_mm, 1)
            pe.wait_ge(g_out, 1)
            pe.wait_ge(s_w1, 32)
            for x in range(2):
                pe.wait_ge(blk_done, x + 1)
                for ht in range(2):
                    for l in range(CMPB // 2):
                        i = pe.matmul(ps[:, 4 + x, ht * 128:ht * 128 + NG * NCMP],
                                      w1[x][:, l * 256 + ht * 128:l * 256 + ht * 128 + 128], blk[x][:, :, l, :],
                                      start=l == 0, stop=l == CMPB // 2 - 1)
                i.then_inc(cmp_h, 1)
            pe.wait_ge(s_w2, 32)
            pe.wait_ge(cmp_act, 1)
            for half in range(2):
                for ht in range(2):
                    i = pe.matmul(ps[64 * half:64 * half + 64, 7, 0:2 * NCMP], w2[0][:, ht * 64:(ht + 1) * 64],
                                  hid[0][:, ht, half::2, :], start=ht == 0, stop=ht == 1)
            i.then_inc(cmp_mm, 1)
            pe.wait_ge(cmp_act, 2)
            for g in range(NG):
                for ht in range(2):
                    i = pe.matmul(ps[0:NCMP, 6, g * DH:(g + 1) * DH], hid[1][:, ht, g, :],
                                  w2[1][:, ht * 64:(ht + 1) * 64], start=ht == 0, stop=ht == 1)
            i.then_inc(cmp_mm, 1)
            pe.wait_ge(cmp_out, 3)
            pe.wait_ge(tile_evicted, TILE0["zed"] + 8)
            for tt in range(TT):
                if tt >= 2:
                    pe.wait_ge(cs_x, tt - 1)
                for t in range(KT):
                    i = pe.matmul(ps[:, tt % 2, t * 2 * NCMP:(t + 1) * 2 * NCMP],
                                  nsT[:, t, tt * 128:(tt + 1) * 128], kcmp[:, t // 4, :], start=True, stop=True)
                i.then_inc(cs_mm, 1)
            for tt in range(TT):
                pe.wait_ge(cs_p, tt + 1)
                for b in range(4):
                    n = tt * 4 + b
                    if n >= 2:
                        pe.wait_ge(cs_ev, n - 1)
                    for h in range(4):
                        i = pe.transpose(ps[0:NCMP, 4 + n % 2, h * 128:(h + 1) * 128], pc[tt][:, b * 4 + h, :], ident)
                    i.then_inc(cs_t, 1)
            pe.wait_ge(cs_ev, 16)

            def scores(u):
                t, half, qt = UNITS[u]
                P = slice(64 * half, 64 * half + 64)
                W = (qt + 1) * 128
                if u >= 2:
                    pe.wait_ge(at_s, u - 1)
                for b in range(2):
                    i = pe.matmul(ps[:, u % 2 * 2 + b, 0:W], nsT[P, t, qt * 128:(qt + 1) * 128],
                                  nsT[P, 12 + 2 * b + t // 4, 0:W], start=True, stop=True)
                i.then_inc(at_qk, 1)

            def turn(u):
                t, half, qt = UNITS[u]
                pe.wait_ge(at_p, u + 1)
                if u >= 1:
                    pe.wait_ge(at_ev, u)
                for b in range(2):
                    for kt in range(qt + 1):
                        i = pe.transpose(ps[:, 4 + b, kt * 128:(kt + 1) * 128], prob[:, u % 3, b, kt * 128:(kt + 1) * 128], ident)
                i.then_inc(at_t, 1)

            def values(u):
                t, half, qt = UNITS[u]
                pe.wait_ge(at_ev, u + 1)
                if t >= 2 and half == 0 and qt == 0:
                    pe.wait_ge(at_o, t - 1)
                o = ps[64 * half:64 * half + 64, 6 + t % 2, qt * 128:(qt + 1) * 128]
                g = t // 4 * 2 + half
                for b in range(2):
                    for kt in range(qt + 1):
                        pe.matmul(o, vtok[:, kt, b * 256 + g * DH:b * 256 + (g + 1) * DH],
                                  probT[:, u % 3, b, kt * 128:(kt + 1) * 128], start=b == 0 and kt == 0, stop=False)
                pe.matmul(o, vcmp[:, g * DH:(g + 1) * DH], pcT[:, half * 8 + t, qt * 128:(qt + 1) * 128],
                          start=False, stop=True).then_inc(at_v, 1)

            for n in range(len(UNITS) + 3):
                if n < len(UNITS):
                    scores(n)
                if 2 <= n <= len(UNITS) + 1:
                    turn(n - 2)
                if n >= 3:
                    values(n - 3)
            pe.wait_ge(at_o, KT)
            linear("nout")
            rms_pe(4)
            for c in range(4):
                tile_group("sin", c, u_parts, ready=(rms_out, 4 * KT) if c == 0 else None)
                pe.wait_ge(ba_done, c + 1)
                for ri in range(2):
                    for q in range(2):
                        if c or ri:
                            pe.wait_ge(bt_ev, c * 4 + ri * 2 + q - 1)
                        for g in range(4):
                            i = pe.transpose(ps[:, 4 + q, g * 128:(g + 1) * 128],
                                             baS[ri][:, (q * 4 + g) * 128:(q * 4 + g + 1) * 128], ident)
                        i.then_inc(bt_mm, 1)
            pe.wait_ge(uc_in, 8 * 16)
            for n in range(8):
                q, ri = n // 2, n % 2
                pe.wait_ge(bt_ev, min(16, 15 + n))
                if n >= 2:
                    pe.wait_ge(w_ev, n - 1)
                for gp in range(8):
                    for g2 in range(2):
                        i = pe.matmul(ps[64 * g2:64 * g2 + 64, 4 + n % 2, gp * 64:gp * 64 + 64],
                                      BWT[ri][:, q * 8 + gp, 64 * g2:64 * g2 + 64], uc[:, 2 * (q * 8 + gp) + g2, :],
                                      start=True, stop=True)
                i.then_inc(w_mm, 1)

            def lag_kernel(m):
                if m >= 2:
                    pe.wait_ge(k_ev, m - 1)
                for q in range(4):
                    for half in range(2):
                        pair = m * 4 + q
                        P = slice(64 * half, 64 * half + 64)
                        bank = m % 2 * 2 + half
                        for ri in range(2):
                            pe.matmul(ps[0:SC, bank, q * 128:q * 128 + SC], bc[ri][P, pair, :], bc[2 + ri][P, pair, :],
                                      start=ri == 0, stop=ri == 1)
                        for ri in range(2):
                            i = pe.matmul(ps[0:SC, bank, q * 128 + SC:(q + 1) * 128], bc[ri][P, pair, :],
                                          CA[ri][P, pair, 0:112], start=ri == 0, stop=ri == 1)
                i.then_inc(k_mm, 1)

            def chunk_outputs(m):
                if m >= 2:
                    pe.wait_ge(y_ev, m - 1)
                for q in range(8):
                    for half in range(2):
                        pair = m * 8 + q
                        g = 2 * pair + half
                        P = slice(64 * half, 64 * half + 64)
                        bank = 4 + m % 2 * 2 + half
                        pe.matmul(ps[:, bank, q * 64:(q + 1) * 64], Tm[:, g % 32, :], uc[:, g, :],
                                  start=True, stop=False)
                        o = ps[:, bank, q * 64 + 1:(q + 1) * 64]
                        pe.matmul(o, CA[0][P, pair, :], wri[0][P, pair, 0:NC8 - 1], start=False, stop=False)
                        i = pe.matmul(o, CA[1][P, pair, :], wri[1][P, pair, 0:NC8 - 1], start=False, stop=True)
                i.then_inc(y_mm, 1)

            pe.wait_ge(ca_done, 2)
            pe.wait_ge(tile_evicted, TILE0["sin"] + 16)
            for m in range(4):
                lag_kernel(m)
            pe.wait_ge(ca_pool, 8)
            lag_kernel(4)
            lag_kernel(5)
            pe.wait_ge(t_in, 8 * 16)
            pe.wait_ge(x_done, 1)
            chunk_outputs(0)
            chunk_outputs(1)
            lag_kernel(6)
            lag_kernel(7)
            pe.wait_ge(t_in, 16 * 16)
            chunk_outputs(2)
            chunk_outputs(3)
            linear("glu", ready=(y_g, 0))
            pe.wait_ge(glu_o, KT)
            linear("sout", x=(mH, mL))
            rms_pe(5)

        @block.scalar
        def _(act):
            count = [0]

            def own(i):
                count[0] += 1
                i.then_inc(acc_, 1)
                act.wait_ge(acc_, count[0])

            act.dma_start(hT[:, :, :], A["x"]).then_inc(s_x, 16)
            act.dma_start(consts[:, :], A["consts"]).then_inc(s_const, 16)
            act.dma_start(params[:, :], A["params"]).then_inc(s_param, 16)
            act.dma_start(w_ab, A["w_ab"]).then_inc(s_wab, 16)
            act.dma_start(bigB[:, 0:512], A["w_pool"]).then_inc(s_wpool, 16)

            def inverse_roots(group, dst, src, scale, arrived, done):
                for i in group:
                    arrived(i)
                    last = act.activation(dst(i), src(i), ACT.Ln, scale=scale, bias=eps_ap)
                own(last)
                for i in group:
                    act.activation(dst(i), dst(i), ACT.Exp, scale=-0.5).then_inc(done, 1)

            def rms_act(n):
                for k in range(KT):
                    act.activation(uT[:, k, :], hT[:, k, :], ACT.Square).then_inc(rms_sq, 1)
                inverse_roots([n], lambda i: rms[:, :], lambda i: ps[:, 4, :], 1.0 / D,
                              lambda i: act.wait_ge(rms_sum, i + 1), rms_std)

            full = [0]

            def lead(dst):
                n = full[0]
                full[0] += 1
                act.wait_ge(x_full, n + 1)
                act.activation(dst, xs[:, n % 2, :], ACT.Copy).then_inc(x_lead, 1)

            act.wait_ge(s_x, 16)
            act.wait_ge(pads0, 3)
            rms_act(0)
            for k in range(KT):
                lead(uH[:, k, :])

            def evict(name, lo, hi, f):
                with act.Fori(lo // 4, hi // 4) as m:
                    for j in range(4):
                        act.wait_ge(half_used, m * 8 + 2 * SLOT0[name] + 2 * j + 2)
                        f(m * 4 + j, ps[:, j, :]).then_inc(tile_evicted, 1)

            def silu_convolved(lo):
                with act.Fori(lo, lo + 4) as n:
                    act.wait_ge(conv_step, n * 4 + 4)
                    act.activation(qkvT[:, n, :], qkvT[:, n, :], ACT.Silu).then_inc(conv_silu, 1)
                    if lo < 8:
                        act.wait_ge(conv_silu, n + 1)
                        act.activation(sq_qk[:, n, :], qkvT[:, n, :], ACT.Square).then_inc(l2_sq, 1)

            evict("inp", 0, 8, lambda n, p: act.activation(projT[:, n, PAD:PW], p, ACT.Copy))
            act.wait_ge(gate_b, 1)
            own(act.activation(ge, ga, ACT.Exp, scale=-1.0))
            act.activation(gl, ge, ACT.Ln, bias=one_ap).then_inc(gate_a, 1)
            act.activation(nalog, param("a_log"), ACT.Exp).then_inc(gate_a, 1)
            act.activation(bta.rearrange("p (t h) -> p t h", h=4), abS[:, :, 4:8], ACT.Sigmoid).then_inc(gate_a, 1)
            for g in range(4):
                act.wait_ge(pool_mm, g + 1)
                act.activation(mixed[:, g, :], ps[:, 6 + g % 2, :], ACT.Copy, scale=param("pool_scale")[:, g:g + 1]).then_inc(pool_out, 1)
            evict("inp", 8, 12, lambda n, p: act.activation(projT[:, n, PAD:PW], p, ACT.Copy))
            silu_convolved(0)
            def l2_norms(lo, hi):
                def arrived(i):
                    act.wait_ge(l2_sum, i + 1)
                    if i >= 4:
                        act.wait_ge(l2_out, i - 3)

                inverse_roots(range(lo, hi), lambda i: l2n[:, i % 4, :], lambda i: ps[:, 4 + i % 4, :], 1.0, arrived, l2_std)

            evict("inp", 12, 16, lambda n, p: act.activation(projT[:, n, PAD:PW], p, ACT.Copy))
            silu_convolved(4)
            l2_norms(0, 2)
            evict("inp", 16, 20, lambda n, p: act.activation(projT[:, n, PAD:PW], p, ACT.Silu))
            act.wait_ge(gate_b, 4)
            act.activation(eg, ps[:, 6, 0:16], ACT.Exp).then_inc(gate_a, 1)
            act.activation(egl, ps[:, 6, 32:64], ACT.Exp).then_inc(gate_a, 1)
            act.activation(ekd, gl, ACT.Exp).then_inc(gate_a, 1)
            l2_norms(2, 6)
            l2_norms(6, 8)
            for tt in range(TT):
                act.wait_ge(row_dec, tt + 1)
                for h in range(NHG):
                    i = act.activation(hd(dec, tt, h), hd(dec, tt, h), ACT.Exp, bias=gc[:, tt * 4 + h:tt * 4 + h + 1])
                i.then_inc(dec_exp, 1)
            for tt in range(TT):
                act.wait_ge(row_mm, tt + 1)
                act.activation(A4T[:, tt, :], ps[:, tt, :], ACT.Exp).then_inc(row_exp, 1)
            silu_convolved(8)
            act.wait_ge(rnd_ev, 4 * (ROUNDS.index("gram") + 1))
            act.wait_ge(pool_out, 4)
            for g in range(4):
                act.activation(mH[:, g, :], mixed[:, g, :], ACT.Copy).then_inc(m_lead, 1)
            for c in range(NCH):
                act.wait_ge(sc_o, c + 1)
                src = ps[:, 5 + 2 * (c % 2), 0:NHG * CH].rearrange("p (h c) -> p h c", c=CH)
                act.activation(gdnO[:, :, c * CH:(c + 1) * CH], src, ACT.Copy).then_inc(sc_oe, 1)
            act.wait_ge(sc_oe, NCH)
            sq = urr[1].rearrange("p a b -> p (a b)")
            for h in range(NHG):
                act.activation(sq[:, h * T:(h + 1) * T], gdnO[:, h, :], ACT.Square).then_inc(go_sq, 1)
            inverse_roots(range(NHG), lambda h: qkvT[:, h, :], lambda h: ps[:, 4 + h, :], 1.0 / 128,
                          lambda h: act.wait_ge(go_sum, h + 1), go_std)
            for h in range(NHG):
                lead(mH[:, 4 + h, :])
            act.wait_ge(tile_evicted, TILE0["out"] + 8)
            rms_act(1)
            for x, n in enumerate("kv"):
                act.dma_start(w1[x], A[f"cmp_{n}_w1"]).then_inc(s_w1, 16)
                act.dma_start(w2[x], A[f"cmp_{n}_w2"]).then_inc(s_w2, 16)
            act.dma_start(w_gate, A["w_gate"]).then_inc(s_wgate, 16)
            for k in range(KT):
                lead(uH[:, k, :])
            for part in range(2):
                name = f"up{part}"
                if part:
                    act.wait_ge(tile_evicted, TILE0[name])
                with act.Fori(0, FT // 8) as m:
                    for j in range(4):
                        act.wait_ge(half_used, m * 8 + 2 * SLOT0[name] + 2 * j + 2)
                        act.activation(relu[:, j, :], ps[:, j, :], ACT.Relu).then_inc(tile_evicted, 1)
                        act.wait_ge(tile_evicted, m * 4 + TILE0[name] + j + 1)
                        act.wait_ge(ff_room, m * 4 + part * FT // 2 + j + 1)
                        act.activation(squared[:, j, :], relu[:, j, :], ACT.Square).then_inc(ff_sq, 1)
                        act.wait_ge(ff_sq, m * 4 + part * FT // 2 + j + 1)
                        act.activation(ffH[:, m * 4 + j, :], squared[:, j, :], ACT.Copy).then_inc(ff_lead, 1)
            act.wait_ge(tile_evicted, TILE0["down1"] + 8)
            rms_act(2)
            act.wait_ge(rms_out, 3 * KT)
            rms_act(3)
            for k in range(KT):
                lead(uH[:, k, :])
            evict("nsa", 0, 8, lambda n, p: act.activation(nsT[:, n, :], p, ACT.Copy, scale=DH ** -0.5))
            evict("nsa", 8, 16, lambda n, p: act.activation(nsT[:, n, :], p, ACT.Copy))
            act.wait_ge(half_used, 2 * SLOT0["val"] + KT)
            for tt in range(TT):
                act.activation(vtok[:, tt, :], ps[:, tt, :], ACT.Copy).then_inc(tile_evicted, 1)
            act.wait_ge(g_mm, 1)
            act.activation(gate_rows, ps[0:3 * NH, 5, :], ACT.Sigmoid).then_inc(g_rows, 1)
            act.wait_ge(tile_evicted, TILE0["nsa"] + 16)
            for n in range(4):
                for par in range(2):
                    act.dma_start(swapped[64 * par:64 * par + 64, n, :], nsT[64 - 64 * par:128 - 64 * par, 8 + n, :]).then_inc(swapped_in, 16)
            evict("zed", 0, 8, lambda n, p: act.activation(zsT[:, n, :], p, ACT.Silu))
            act.wait_ge(g_mm, 2)
            act.activation(small[:, 308:500], ps[:, 5, 0:192], ACT.Copy).then_inc(g_out, 1)
            for x in range(2):
                act.wait_ge(cmp_h, x + 1)
                i = act.activation(hid[x].rearrange("p t g n -> p t (g n)"),
                                   ps[:, 4 + x, 0:256].rearrange("p (t c) -> p t c", c=128)[:, :, 0:NG * NCMP], ACT.Silu)
                i.then_inc(cmp_act, 1)
            for tt in range(TT):
                act.wait_ge(cs_x, tt + 1)
                f = pc[tt].rearrange("p h n -> p (h n)")
                act.wait_ge(cs_sub, tt + 1)
                act.activation(f, f, ACT.Exp).then_inc(cs_exp, 1)
            for n in range(16):
                act.wait_ge(cs_t, n + 1)
                tt, b = n // 4, n % 4
                act.activation(pcT[:, b * 4:b * 4 + 4, tt * 128:(tt + 1) * 128],
                               ps[0:NCMP, 4 + n % 2, :].rearrange("p (h q) -> p h q", q=128), ACT.Copy).then_inc(cs_ev, 1)
            for n in range(len(UNITS) + 2):
                if n < len(UNITS):
                    t, half, qt = UNITS[n]
                    W = (qt + 1) * 128
                    act.wait_ge(at_m, n + 1)
                    for b in range(2):
                        i = act.activation(prob[:, n % 3, b, 0:W], prob[:, n % 3, b, 0:W], ACT.Exp,
                                           bias=anmax[:, n % 3, b:b + 1], accum_out=asum[:, n % 3, b:b + 1])
                    i.then_inc(at_e, 1)
                if n >= 2:
                    u = n - 2
                    W = (UNITS[u][2] + 1) * 128
                    act.wait_ge(at_t, u + 1)
                    if u >= 3:
                        act.wait_ge(at_v, u - 2)
                    act.activation(probT[:, u % 3, :, 0:W], ps[:, 4:6, 0:W], ACT.Copy).then_inc(at_ev, 1)
                if n >= 14 and n % 8 == 6:
                    lead(uH[:, n // 8 - 1, :])
            lead(uH[:, KT - 1, :])
            for x, name in enumerate(("ssm_b_re", "ssm_b_im", "ssm_c_re", "ssm_c_im")):
                act.dma_start(bc[x].rearrange("p g c -> p (g c)"), A[name]).then_inc(s_bc, 16)
            act.activation(pk[0], param("log_dt"), ACT.Exp).then_inc(ssm_a, 1)
            act.wait_ge(ssm_b, 1)
            for k in range(9):
                i = act.activation(mag[:, k, :], pk[1], ACT.Exp, scale=float(k))
            i.then_inc(ssm_a, 1)
            act.activation(pk[6], pk[5], ACT.Sin).then_inc(ssm_a, 1)
            act.activation(pk[7], pk[5], ACT.Sin, scale=0.5).then_inc(ssm_a, 1)
            act.wait_ge(tile_evicted, TILE0["nout"] + 8)
            rms_act(4)
            for k in range(KT):
                lead(uH[:, k, :])

            def store_b(c):
                for ri in range(2):
                    for q in range(2):
                        act.wait_ge(bt_mm, c * 4 + ri * 2 + q + 1)
                        act.activation(BWT[ri].rearrange("p g c -> p (g c)")[:, (c * 8 + q * 4) * 128:(c * 8 + q * 4 + 4) * 128],
                                       ps[:, 4 + q, :], ACT.Copy).then_inc(bt_ev, 1)

            for c in range(2):
                evict("sin", c * 4, c * 4 + 4, lambda n, p: act.activation(
                    suP[:, n, :].rearrange("p (j c) -> p c j", c=NC8), p.rearrange("p (c j) -> p c j", j=FR), ACT.Copy))
                if c == 1:
                    act.wait_ge(tile_evicted, TILE0["sin"] + 8)
                    act.dma_start(scratch["u"], suP).then_inc(u_stored, 16)
                store_b(c)
            act.wait_ge(u_stored, 16)
            by_frame = scratch["u"].rearrange("(g c) t (j n) -> j c t g n", c=SC, j=FR)
            for j in range(FR):
                act.dma_start(uc[112 - 16 * j:128 - 16 * j, :, :].rearrange("p (t g) n -> p t g n", g=8),
                              by_frame[j]).then_inc(uc_in, 16)
            for c in range(2, 4):
                evict("sin", c * 4, c * 4 + 4, lambda n, p: act.activation(szT[:, n - 8, :], p, ACT.Silu))
                store_b(c)
            for n in range(8):
                q, ri = n // 2, n % 2
                act.wait_ge(w_mm, n + 1)
                act.activation(wri[ri].rearrange("p g c -> p (g c)")[:, q * 512:(q + 1) * 512], ps[:, 4 + n % 2, :], ACT.Copy).then_inc(w_ev, 1)
            act.wait_ge(rot_in, 1)

            def store_kernel(m):
                act.wait_ge(k_mm, m + 1)
                n = m % 4
                act.activation(Kl[:, n * 8:n * 8 + 8, :].rearrange("p (q h) c -> p h q c", h=2),
                               ps[0:SC, m % 2 * 2:m % 2 * 2 + 2, :].rearrange("p h (q c) -> p h q c", c=128),
                               ACT.Copy).then_inc(k_ev, 1)

            def fill_lags(part):
                act.wait_ge(k_ev, (part + 1) * 4)
                for j in range(FR):
                    act.dma_start(Tm[112 - 16 * j:128 - 16 * j, :, 16 * j:128], Kl[:, :, 0:128 - 16 * j]).then_inc(t_in, 16)

            def store_y(part):
                for m in range(2 * part, 2 * part + 2):
                    act.wait_ge(y_mm, m + 1)
                    act.activation(uc[:, m * 16:m * 16 + 16, :].rearrange("p (q h) c -> p h q c", h=2),
                                   ps[:, 4 + m % 2 * 2:6 + m % 2 * 2, :].rearrange("p h (q c) -> p h q c", c=NC8),
                                   ACT.Copy).then_inc(y_ev, 1)
                act.wait_ge(y_ev, 2 * part + 2)
                act.dma_start(scratch["y"][part], uc[:, part * 32:part * 32 + 32, :]).then_inc(y_stored, 16)

            def load_y(part):
                act.wait_ge(y_stored, 16 * part + 16)
                by_group = scratch["y"][part].rearrange("(j c) (t g) n -> g c t j n", c=SC, g=8)
                for g in range(8):
                    act.dma_start(yF[16 * g:16 * g + 16, 4 * part:4 * part + 4, :].rearrange("p t (j n) -> p t j n", n=NC8),
                                  by_group[g]).then_inc(y_in, 16)

            def gelu(part):
                for k in range(4 * part, 4 * part + 4):
                    act.wait_ge(y_d, k + 1)
                    act.activation(yD[:, k, :], yD[:, k, :], ACT.Gelu_apprx_tanh).then_inc(y_act, 1)
                    act.wait_ge(y_act, k + 1)
                    act.activation(uH[:, k, :], yD[:, k, :], ACT.Copy).then_inc(y_lead, 1)

            for m in range(4):
                store_kernel(m)
            act.wait_ge(t_zero, 1)
            fill_lags(0)
            act.wait_ge(t_in, 8 * 16)
            store_kernel(4)
            store_kernel(5)
            store_y(0)
            store_kernel(6)
            store_kernel(7)
            fill_lags(1)
            load_y(0)
            store_y(1)
            gelu(0)
            load_y(1)
            gelu(1)
            with act.Fori(0, 4) as m:
                for x in range(2):
                    act.wait_ge(half_used, m * 8 + 2 * SLOT0["glu"] + 4 * x + 4)
                    act.wait_ge(tile_evicted, m * 4 + TILE0["glu"] + 2 * x - 2)
                    act.activation(sg[:, x, :], ps[:, 2 * x + 1, :], ACT.Sigmoid).then_inc(glu_s, 1)
                for x in range(2):
                    act.wait_ge(glu_m, m * 2 + x + 1)
                    act.activation(mH[:, m * 2 + x, :], gprod[:, x, :], ACT.Copy).then_inc(glu_lead, 1)
            act.wait_ge(tile_evicted, NTILE)
            rms_act(5)
            for k in range(0, KT, 2):
                act.wait_ge(rms_out, 5 * KT + k + 2)
                act.dma_start(out_dram[:, k:k + 2, :], hT[:, k:k + 2, :]).then_inc(out_done, 16)
            act.wait_ge(out_done, KT // 2 * 16)

        @block.gpsimd
        def _(pool):
            def split_weights(lo, hi):
                with pool.Fori(lo // RING, hi // RING) as m:
                    for j in range(RING):
                        pool.wait_ge(half_loaded[j], m * 16 + 16)
                        if lo:
                            pool.wait_ge(half_used, m * RING + j - RING + 1)
                        pool.tensor_tensor(wh[:, j, :], raw[:, j, :], zero_ap.to_broadcast([128, 512]), ALU.add).then_inc(half_lead, 1)
                        pool.wait_ge(half_lead, m * RING + j + 1)
                        pool.tensor_tensor(wl[:, j, :], raw[:, j, :], wh[:, j, :].bitcast(f32), ALU.subtract).then_inc(half_split, 1)

            pool.memset(projT[:, :, 0:PAD], 0.0).then_inc(pads0, 1)
            pool.memset(eps_ap, EPS).then_inc(pads0, 1)
            pool.memset(one_ap, 1.0).then_inc(pads0, 1)
            pool.memset(zero_ap, 0.0).then_inc(pads0, 1)
            pool.wait_ge(pads0, 4)

            def split_small(loaded, done, w, parts):
                pool.wait_ge(loaded, 16)
                pool.tensor_copy(parts[0][:, :], w).then_inc(done, 1)
                pool.wait_ge(done, 1)
                pool.tensor_tensor(parts[1][:, :], w, parts[0][:, :].bitcast(f32), ALU.subtract).then_inc(done, 1)

            split_weights(0, RING)
            split_small(s_wab, wab_split, w_ab, (wabH, wabL))
            split_weights(RING, 2 * SLOT0["out"] + RING)
            for g in range(4):
                pool.wait_ge(m_lead, g + 1)
                if g == 0:
                    pool.wait_ge(rnd_ev, 4 * (ROUNDS.index("A8") + 1))
                pool.tensor_tensor(mL[:, g, :], mixed[:, g, :], mH[:, g, :].bitcast(f32), ALU.subtract).then_inc(m_split, 1)
            split_weights(2 * SLOT0["out"] + RING, 2 * SLOT0["nsa"])
            split_small(s_wgate, wgate_split, w_gate, (wgH, wgL))
            split_weights(2 * SLOT0["nsa"], 2 * SLOT0["nout"] + RING)
            pool.wait_ge(cmp_act, 2)
            for n in range(NH):
                t, half = n // 2, n % 2
                if n >= 2:
                    pool.wait_ge(at_s, 4 * (n - 1))
                pool.tensor_scalar(dsl[:, n % 2, :], const("dist"), const("slope")[:, half * 8 + t:half * 8 + t + 1], 0.0,
                                   ALU.mult, ALU.add).then_inc(ds_ready, 1)
            split_weights(2 * SLOT0["nout"] + RING, 2 * SLOT0["glu"])
            pool.wait_ge(tables, 1)
            pool.wait_ge(half_used, 2 * SLOT0["glu"])
            for c in range(4):
                gs = slice(16 + c * 4, 20 + c * 4)
                cc = [bc[2 + q][:, gs, :].unsqueeze(2).to_broadcast([128, 4, FR, SC]) for q in range(2)]
                pp = [p[:, 1:9, gs].rearrange("p k g -> p g k").unsqueeze(3).to_broadcast([128, 4, FR, SC]) for p in ptab[2:]]
                o = [CA[q][:, gs, :].rearrange("p g (k c) -> p g k c", c=SC) for q in range(2)]
                tv = [xs[:, q, :].rearrange("p (g j c) -> p g j c", g=4, j=FR) for q in range(2)]
                for ri, (x, y, op) in enumerate(((0, 1, ALU.add), (1, 0, ALU.subtract))):
                    if c or ri:
                        pool.wait_ge(ca_pool, 2 * c + ri)
                    pool.tensor_tensor(tv[0], pp[0], cc[x], ALU.mult).then_inc(ca_chain, 1)
                    pool.tensor_tensor(tv[1], pp[1], cc[y], ALU.mult).then_inc(ca_chain, 1)
                    pool.wait_ge(ca_chain, 2 * (2 * c + ri) + 2)
                    pool.tensor_tensor(o[ri], tv[0], tv[1], op).then_inc(ca_pool, 1)
            pool.wait_ge(w_mm, 8)
            pool.memset(Tm, 0.0).then_inc(t_zero, 1)
            split_weights(2 * SLOT0["glu"], 2 * NSLOT)

        @block.vector
        def _(dve):
            count = [0]

            def own(i):
                count[0] += 1
                i.then_inc(dvc, 1)
                dve.wait_ge(dvc, count[0])

            full, split = [0], [0]

            def rest(dst, leading):
                n = split[0]
                split[0] += 1
                dve.wait_ge(x_lead, n + 1)
                return dve.tensor_tensor(dst, xs[:, n % 2, :], leading.bitcast(f32), ALU.subtract)

            def rms_dve(n, weight, dst):
                dve.wait_ge(rms_std, n + 1)
                for k in range(KT + 1):
                    if k < KT:
                        if dst is None:
                            if k >= 2:
                                dve.wait_ge(rms_out, n * KT + k - 1)
                            i = dve.scalar_tensor_tensor(xs[:, k % 2, :], hT[:, k, :], param(weight)[:, k:k + 1], rms[:, :],
                                                         ALU.mult, ALU.mult)
                            i.then_inc(x_full, 1)
                            full[0] += 1
                        else:
                            dve.scalar_tensor_tensor(dst[:, k, :], hT[:, k, :], param(weight)[:, k:k + 1], rms[:, :],
                                                     ALU.mult, ALU.mult).then_inc(rms_out, 1)
                    if k and dst is None:
                        rest(uL[:, k - 1, :], uH[:, k - 1, :]).then_inc(rms_out, 1)

            def residual(name):
                with dve.Fori(0, 2) as m:
                    for j in range(4):
                        per = 2 * SLOTS[name] // TILES[name]
                        dve.wait_ge(half_used, (m * 4 + j + 1) * per + 2 * SLOT0[name])
                        dve.tensor_tensor(hT[:, m * 4 + j, :], hT[:, m * 4 + j, :], ps[:, j, :], ALU.add).then_inc(tile_evicted, 1)

            dve.wait_ge(s_param, 16)
            dve.wait_ge(s_x, 16)
            rms_dve(0, "norm_mix", None)
            dve.wait_ge(s_const, 16)
            for g in range(4):
                dve.wait_ge(tile_evicted, g + 1)
                w, src = 1, projT[:, g, :]
                for d in range(g + 1):
                    dst = ptmp[d % 2]
                    own(dve.tensor_tensor(dst[:, 2 * w - 1:PW], src[:, 2 * w - 1:PW], src[:, w - 1:PW - w], ALU.add))
                    src, w = dst, 2 * w
                mean = ptmp[(g + 1) % 2]
                own(dve.tensor_scalar(mean[:, PAD:PW], src[:, PAD:PW], 1.0 / w, 0.0, ALU.mult, ALU.add))
                own(dve.tensor_tensor(mean[:, PAD:PAD + w], src[:, PAD:PAD + w], const("invcount")[:, g * PAD:g * PAD + w], ALU.mult))
                i = dve.tensor_tensor(pooled[:, g, :], mean[:, PAD:PW], projT[:, g, PAD:PW], ALU.subtract)
                i.then_inc(pooled_done, 1)
                dve.wait_ge(pooled_done, g + 1)
            dve.wait_ge(ab_ready, 1)
            dve.tensor_copy(ab_rows, ps[0:8, 5, :]).then_inc(ab_copied, 1)
            cw = param("conv")

            def convolve(lo, hi):
                with dve.Fori(lo, hi) as n:
                    dve.wait_ge(tile_evicted, n + 5)
                    x = projT[:, n + 4, :]
                    y = qkvT[:, n, :]
                    dve.tensor_scalar(y, projT[:, n + 4, PAD - 3:PW - 3], cw[:, bass.ds(n * CONV, 1)], None, ALU.mult).then_inc(conv_step, 1)
                    for i in range(1, CONV):
                        dve.wait_ge(conv_step, n * 4 + i)
                        dve.scalar_tensor_tensor(y, projT[:, n + 4, PAD - 3 + i:PW - 3 + i], cw[:, bass.ds(n * CONV + i, 1)], y,
                                                 ALU.mult, ALU.add).then_inc(conv_step, 1)

            def normalise(lo, hi):
                for i in range(lo, hi):
                    dve.wait_ge(l2_std, i + 1)
                    dve.scalar_tensor_tensor(qkvT[:, i, :], qkvT[:, i, :], 128 ** -0.5 if i < 4 else 1.0, l2n[:, i % 4, :],
                                             ALU.mult, ALU.mult).then_inc(l2_out, 1)

            convolve(0, 4)
            dve.wait_ge(ab_ready, 2)
            dve.tensor_copy(abS.rearrange("p t c -> p (t c)"), ps[:, 5, 0:32]).then_inc(ab_copied, 1)
            dve.wait_ge(ab_copied, 2)
            own(dve.tensor_tensor(gx.rearrange("p (t h) -> p t h", h=4), abS[:, :, 0:4],
                                  param("dt_bias").rearrange("p (t h) -> p t h", h=4), ALU.add))
            own(dve.tensor_scalar(gg, gx, -1.0, None, ALU.mult))
            dve.tensor_tensor(ga, gx, gg, ALU.max).then_inc(gate_b, 1)
            convolve(4, 8)
            dve.wait_ge(gate_a, 3)
            own(dve.scalar_tensor_tensor(gx, gx, 0.0, gl, ALU.max, ALU.add))
            dve.scalar_tensor_tensor(gg, gx, -1.0, nalog, ALU.mult, ALU.mult).then_inc(gate_b, 1)
            dve.wait_ge(gate_b, 2)
            dve.wait_ge(pool_mm, 4)
            dve.tensor_copy(gB.rearrange("p t (h c) -> p (t h) c", c=128),
                            gg.unsqueeze(2).to_broadcast([128, 16, 128])).then_inc(gate_b, 1)
            normalise(0, 2)
            dve.wait_ge(gate_mm, 1)
            own(dve.tensor_copy(gc, ps[:, 6, 0:16]))
            dve.tensor_tensor(gl, ps[:, 6, 16:32], gc, ALU.subtract).then_inc(gate_b, 1)
            convolve(8, 12)
            dve.wait_ge(gate_a, 4)
            own(dve.tensor_tensor(beg, bta, eg, ALU.mult))
            normalise(2, 8)
            mneg = const("maskneg").unsqueeze(1).to_broadcast([128, 4, 128])
            for tt in range(TT):
                dve.wait_ge(row_mm, tt + 1)
                dve.scalar_tensor_tensor(dec[:, tt, :].rearrange("p (h c) -> p h c", c=128),
                                         ps[:, tt, :].rearrange("p (h c) -> p h c", c=128), -1.0, mneg,
                                         ALU.mult, ALU.add).then_inc(row_dec, 1)
            dve.wait_ge(dec_exp, TT)
            dve.wait_ge(gate_a, 6)

            def masked(dst, tt, mask):
                return dve.tensor_tensor(dst[:, tt, :].rearrange("p (h c) -> p h c", c=128),
                                         Mm[:, tt, :].rearrange("p (h c) -> p h c", c=128),
                                         const(mask).unsqueeze(1).to_broadcast([128, 4, 128]), ALU.mult)

            for r, name in enumerate(ROUNDS):
                for tt in range(TT):
                    dve.wait_ge(rnd_mm, 4 * r + tt + 1)
                    p = ps[:, 4 + tt, :]

                    def by_head(dst, scalars):
                        for h in range(NHG):
                            i = dve.tensor_scalar(hd(dst, tt, h), p[:, h * 128:(h + 1) * 128],
                                                  scalars[:, tt * 4 + h:tt * 4 + h + 1], None, ALU.mult)
                        return i

                    if name == "attn":
                        i = dve.tensor_tensor(aS[:, tt, :], p, dec[:, tt, :], ALU.mult)
                    elif name == "attnT":
                        i = dve.tensor_copy(aiT[:, tt, :], p)
                    elif name == "ktok":
                        by_head(kd, ekd)
                        i = by_head(kbe, beg)
                    elif name == "vtok":
                        i = by_head(vb, bta)
                    elif name == "gram":
                        for h in range(NHG):
                            i = dve.scalar_tensor_tensor(hd(Mm, tt, h), p[:, h * 128:(h + 1) * 128],
                                                         bta[:, tt * 4 + h:tt * 4 + h + 1], hd(dec, tt, h),
                                                         ALU.mult, ALU.mult)
                        own(i)
                        i = masked(Aa, tt, "neg16")
                    elif name == "AT":
                        dve.tensor_copy(AT[:, tt, :], p)
                        i = dve.tensor_tensor(Rr[:, tt, :].rearrange("p (h c) -> p h c", c=128),
                                              p.rearrange("p (h c) -> p h c", c=128),
                                              ident.unsqueeze(1).to_broadcast([128, 4, 128]), ALU.add)
                    elif name in ("R2", "R4", "R8"):
                        i = dve.tensor_tensor(Rr[:, tt, :], p, Rr[:, tt, :], ALU.add)
                    elif name in ("R32", "R64"):
                        i = dve.tensor_tensor(Rr[:, tt, :], Rr[:, tt, :], p, ALU.subtract)
                    elif name == "A4T":
                        dve.tensor_copy(A4T[:, tt, :], p)
                        i = masked(Bm32, tt, "low32")
                    elif name == "A8":
                        dve.tensor_copy(A8[:, tt, :], p)
                        i = masked(Bm64, tt, "low64")
                    else:
                        dst = {"A2": A2, "A2T": A2T, "A4": A4, "X32": Xx, "X64": Xx, "Y32": Yy, "Y64": Yy,
                               "val": val, "kcT": kcT}[name]
                        i = dve.tensor_copy(dst[:, tt, :], p)
                    i.then_inc(rnd_ev, 1)
                if name == "attn":
                    dve.wait_ge(row_exp, TT)
                    for tt in range(TT):
                        q = qkvT[:, 0:4, tt * 128:(tt + 1) * 128]
                        dve.tensor_tensor(q, q, A4T[:, tt, :].rearrange("p (h c) -> p h c", c=128), ALU.mult).then_inc(qd_done, 1)
            dve.memset(Sst[:, 0, :], 0.0).then_inc(sc_s, 2)
            for c in range(NCH):
                tt, half = c // 2, c % 2
                P = slice(64 * half, 64 * half + 64)
                for pair in range(2):
                    cols = slice(256 * pair, 256 * pair + 256)
                    dve.wait_ge(sc_k, 2 * c + pair + 1)
                    if c >= 2 and pair == 0:
                        dve.wait_ge(sc_o, c - 1)
                    dve.tensor_tensor(vnew[P, cols], val[P, tt, cols], ps[P, pair, cols], ALU.subtract).then_inc(sc_v, 1)
                for pair in range(2):
                    dve.wait_ge(sc_u, 2 * c + pair + 1)
                    if c >= 1 and pair == 0:
                        dve.wait_ge(sc_o, c)
                    for h in (2 * pair, 2 * pair + 1):
                        i = dve.scalar_tensor_tensor(Sst[:, (c + 1) % 2, h * 128:(h + 1) * 128], Sst[:, c % 2, h * 128:(h + 1) * 128],
                                                     egl[:, half * 16 + tt * 4 + h:half * 16 + tt * 4 + h + 1],
                                                     ps[:, 2 + pair, h * 128:(h + 1) * 128], ALU.mult, ALU.add)
                    i.then_inc(sc_s, 1)
            dve.wait_ge(sc_s, 2 * (NCH + 1))
            dve.wait_ge(sc_o, NCH)
            for h in range(NHG):
                dve.wait_ge(go_std, h + 1)
                own(dve.scalar_tensor_tensor(gdnO[:, h, :], gdnO[:, h, :], param("gdn_norm"), qkvT[:, h, :], ALU.mult, ALU.mult))
                if h >= 2:
                    dve.wait_ge(m_split, 4 + h - 1)
                dve.tensor_tensor(xs[:, h % 2, :], gdnO[:, h, :], projT[:, 16 + h, PAD:PW], ALU.mult).then_inc(x_full, 1)
                if h >= 1:
                    if h == 1:
                        dve.wait_ge(m_split, 4)
                    rest(mL[:, 3 + h, :], mH[:, 3 + h, :]).then_inc(m_split, 1)
            rest(mL[:, 7, :], mH[:, 7, :]).then_inc(m_split, 1)
            residual("out")
            rms_dve(1, "norm_mlp", None)
            dve.memset(small[:, 306:307], 0.0).then_inc(ff_room, RING_FF)
            for part in range(2):
                with dve.Fori(0, FT // 8) as m:
                    for j in range(4):
                        dve.wait_ge(ff_lead, m * 4 + part * FT // 2 + j + 1)
                        dve.tensor_tensor(ffL[:, m * 4 + j, :], squared[:, j, :], ffH[:, m * 4 + j, :].bitcast(f32),
                                          ALU.subtract).then_inc(ff_room, 1)
                residual(f"down{part}")
            rms_dve(2, "norm_final", hT)
            rms_dve(3, "l0_norm", None)
            dve.wait_ge(swapped_in, 8 * 16)
            own(dve.memset(kcmp, 0.0))
            for x, name in enumerate(("kpe", "vpe")):
                for g in range(NG):
                    for par in range(2):
                        P = slice(64 * par, 64 * par + 64)
                        src = nsT[P, 8 + 2 * x + g // 2, :] if g % 2 == par else swapped[P, 2 * x + g // 2, :]
                        frames = src.rearrange("p (n s) -> p s n", s=CMPS)
                        for o in range(2):
                            i = dve.tensor_tensor(blk[x][P, g, o * 8:(o + 1) * 8, :], frames[:, par::2, o:o + NCMP],
                                                  param(name)[P, o * 8:(o + 1) * 8].unsqueeze(2).to_broadcast([64, 8, NCMP]), ALU.add)
                i.then_inc(blk_done, 1)
            dve.wait_ge(cmp_mm, 1)
            for half in range(2):
                P = slice(64 * half, 64 * half + 64)
                dve.tensor_copy(kcmp[P, :, half * NCMP:(half + 1) * NCMP],
                                ps[P, 7, 0:2 * NCMP].rearrange("p (g n) -> p g n", n=NCMP)).then_inc(cmp_out, 1)
            dve.wait_ge(cmp_mm, 2)
            dve.tensor_copy(vcmp, ps[0:NCMP, 6, 0:NG * DH]).then_inc(cmp_out, 1)
            dve.wait_ge(cmp_out, 3)
            dve.wait_ge(cmp_h, 2)
            dve.wait_ge(g_out, 1)

            def wide(x):
                return x.unsqueeze(2).to_broadcast([128, NH, NCMP])

            for tt in range(TT):
                cols = slice(tt * NCMP, (tt + 1) * NCMP)
                own(dve.tensor_tensor(pc[tt], wide(const("slope")), const("cdist")[:, cols].unsqueeze(1).to_broadcast([128, NH, NCMP]), ALU.mult))
                dve.wait_ge(cs_mm, tt + 1)
                by_half = pc[tt].rearrange("p (a t) n -> p a t n", a=2)
                dve.tensor_tensor(by_half, by_half, ps[:, tt % 2, 0:NH * NCMP].rearrange("p (t a n) -> p a t n", a=2, n=NCMP),
                                  ALU.add).then_inc(cs_x, 1)
                dve.wait_ge(cs_x, tt + 1)
                own(dve.tensor_reduce(cm, pc[tt], AX.X, ALU.max))
                dve.tensor_tensor(pc[tt], pc[tt], wide(cm), ALU.subtract).then_inc(cs_sub, 1)
            for tt in range(TT):
                cols = slice(tt * NCMP, (tt + 1) * NCMP)
                dve.wait_ge(cs_exp, tt + 1)
                own(dve.tensor_tensor(pc[tt], pc[tt], const("cmask")[:, cols].unsqueeze(1).to_broadcast([128, NH, NCMP]), ALU.mult))
                own(dve.tensor_reduce(cs_, pc[tt], AX.X, ALU.add))
                own(dve.tensor_scalar(cs_, cs_, 1e-30, None, ALU.max))
                own(dve.reciprocal(cs_, cs_))
                own(dve.tensor_tensor(cs_, cs_, gate[:, tt, 0, :], ALU.mult))
                dve.tensor_tensor(pc[tt], pc[tt], wide(cs_), ALU.mult).then_inc(cs_p, 1)

            def shift(u):
                t, half, qt = UNITS[u]
                W = (qt + 1) * 128
                n = u // 4
                dve.wait_ge(ds_ready, n + 1)
                dve.wait_ge(at_qk, u + 1)
                if u >= 3:
                    dve.wait_ge(at_t, u - 2)
                for b in range(2):
                    i = dve.tensor_tensor_reduce(prob[:, u % 3, b, 0:W], ps[:, u % 2 * 2 + b, 0:W],
                                                 dsl[:, n % 2, 512 - W:512], 1.0, -3e38, ALU.add, ALU.max,
                                                 amax[:, u % 3, b:b + 1])
                i.then_inc(at_s, 1)
                dve.wait_ge(at_s, u + 1)
                dve.tensor_scalar(anmax[:, u % 3, :], amax[:, u % 3, :], -1.0, None, ALU.mult).then_inc(at_m, 1)

            def weigh(u):
                t, half, qt = UNITS[u]
                W = (qt + 1) * 128
                dve.wait_ge(at_e, u + 1)
                own(dve.reciprocal(asum[:, u % 3, :], asum[:, u % 3, :]))
                own(dve.tensor_tensor(asum[:, u % 3, :], asum[:, u % 3, :], gate[:, qt, 1:3, half * 8 + t], ALU.mult))
                for b in range(2):
                    i = dve.tensor_scalar(prob[:, u % 3, b, 0:W], prob[:, u % 3, b, 0:W], asum[:, u % 3, b:b + 1], None, ALU.mult)
                i.then_inc(at_p, 1)

            def finish(t):
                dve.wait_ge(at_v, 8 * (t + 1))
                if t >= 2:
                    dve.wait_ge(at_o, t - 1)
                dve.tensor_tensor(xs[:, t % 2, :], ps[:, 6 + t % 2, :], zsT[:, t, :], ALU.mult).then_inc(x_full, 1)

            def finish_rest(t):
                rest(uL[:, t, :], uH[:, t, :]).then_inc(at_o, 1)

            for n in range(len(UNITS) + 1):
                if n < len(UNITS):
                    shift(n)
                if n >= 1:
                    weigh(n - 1)
                if n >= 12 and n % 8 == 4:
                    finish(n // 8 - 1)
                if n >= 15 and n % 8 == 7:
                    finish_rest(n // 8 - 1)
            finish(KT - 1)
            finish_rest(KT - 1)
            dt, x_, lre, th, r_, s1, sh, c1, den, nr, cr, ci, t1, t2 = (
                pk[0], pk[1], pk[2], pk[3], pk[5], pk[6], pk[7], pk[8], pk[9], pk[10], pk[11], pk[12], pk[13], pk[14])
            dve.wait_ge(ssm_a, 1)
            own(dve.tensor_scalar(lre, param("lre"), -1e-4, None, ALU.min))
            own(dve.tensor_tensor(th, param("lim"), dt, ALU.mult))
            own(dve.tensor_tensor(x_, lre, dt, ALU.mult))
            own(dve.tensor_scalar(t1, th, 1.0 / (2 * np.pi), ROUND, ALU.mult, ALU.add))
            own(dve.tensor_scalar(t1, t1, ROUND, None, ALU.subtract))
            own(dve.scalar_tensor_tensor(r_, t1, -TWO_PI[0], th, ALU.mult, ALU.add))
            own(dve.scalar_tensor_tensor(r_, t1, -TWO_PI[1], r_, ALU.mult, ALU.add))
            own(dve.scalar_tensor_tensor(r_, t1, -TWO_PI[2], r_, ALU.mult, ALU.add))
            dve.tensor_scalar(r_, r_, PI32, -PI32, ALU.min, ALU.max).then_inc(ssm_b, 1)
            dve.wait_ge(ssm_a, 4)
            own(dve.tensor_tensor(c1, sh, sh, ALU.mult))
            own(dve.tensor_scalar(c1, c1, -2.0, 1.0, ALU.mult, ALU.add))
            U, V, Pr, Pi = ptab

            def cmul(o_re, o_im, a_re, a_im, b_re, b_im, ta, tb, last=None):
                own(dve.tensor_tensor(ta, a_re, b_re, ALU.mult))
                own(dve.tensor_tensor(tb, a_im, b_im, ALU.mult))
                own(dve.tensor_tensor(o_re, ta, tb, ALU.subtract))
                own(dve.tensor_tensor(ta, a_re, b_im, ALU.mult))
                own(dve.tensor_tensor(tb, a_im, b_re, ALU.mult))
                i = dve.tensor_tensor(o_im, ta, tb, ALU.add)
                if last is None:
                    own(i)
                return i

            dve.memset(U[:, 0, :], 1.0)
            dve.memset(V[:, 0, :], 0.0)
            own(dve.tensor_copy(U[:, 1, :], c1))
            own(dve.tensor_copy(V[:, 1, :], s1))
            for m in (1, 2, 4):
                bcast = lambda x: x[:, m:m + 1, :].to_broadcast([128, m, NPAIR])
                tv = [tmpS[q][:, 0:m * NPAIR].rearrange("p (m g) -> p m g", g=NPAIR) for q in range(2)]
                cmul(U[:, m + 1:2 * m + 1, :], V[:, m + 1:2 * m + 1, :], U[:, 1:m + 1, :], V[:, 1:m + 1, :],
                     bcast(U), bcast(V), *tv)
            own(dve.tensor_tensor(Pr, U, mag, ALU.mult))
            own(dve.tensor_tensor(Pi, V, mag, ALU.mult))
            own(dve.tensor_tensor(den, lre, lre, ALU.mult))
            own(dve.tensor_tensor(t1, param("lim"), param("lim"), ALU.mult))
            own(dve.tensor_tensor(den, den, t1, ALU.add))
            own(dve.reciprocal(den, den))
            own(dve.tensor_scalar(nr, Pr[:, 1, :], -1.0, None, ALU.add))
            own(dve.tensor_tensor(t1, nr, lre, ALU.mult))
            own(dve.tensor_tensor(t2, Pi[:, 1, :], param("lim"), ALU.mult))
            own(dve.tensor_tensor(cr, t1, t2, ALU.add))
            own(dve.tensor_tensor(cr, cr, den, ALU.mult))
            own(dve.tensor_tensor(t1, Pi[:, 1, :], lre, ALU.mult))
            own(dve.tensor_tensor(t2, nr, param("lim"), ALU.mult))
            own(dve.tensor_tensor(ci, t1, t2, ALU.subtract))
            own(dve.tensor_tensor(ci, ci, den, ALU.mult))
            dve.wait_ge(s_bc, 64)
            wide16 = lambda x: x.unsqueeze(2).to_broadcast([128, NPAIR, SC])
            tv = [tmpS[q][:, 0:512].rearrange("p (g c) -> p g c", c=SC) for q in range(2)]
            own(dve.tensor_tensor(tv[0], bc[0], wide16(cr), ALU.mult))
            own(dve.tensor_tensor(tv[1], bc[1], wide16(ci), ALU.mult))
            own(dve.tensor_tensor(tv[0], tv[0], tv[1], ALU.subtract))
            own(dve.tensor_tensor(tv[1], bc[0], wide16(ci), ALU.mult))
            own(dve.tensor_tensor(bc[1], bc[1], wide16(cr), ALU.mult))
            own(dve.tensor_tensor(bc[1], bc[1], tv[1], ALU.add))
            own(dve.tensor_copy(bc[0], tv[0]))
            dve.tensor_scalar(bc[3], bc[3], -1.0, None, ALU.mult).then_inc(tables, 1)
            dve.wait_ge(tables, 1)
            residual("nout")
            rms_dve(4, "l1_norm", None)
            def powers_of_b(c):
                gs = slice(c * 8, c * 8 + 8)
                bb = [bc[q][:, gs, :].unsqueeze(2).to_broadcast([128, 8, FR, SC]) for q in range(2)]
                pp = [p[:, 0:FR, gs].rearrange("p k g -> p g k").unsqueeze(3).to_broadcast([128, 8, FR, SC]) for p in (Pr, Pi)]
                if c:
                    dve.wait_ge(bt_mm, 4 * c)
                o = [x.rearrange("p (g j c) -> p g j c", g=8, j=FR) for x in baS]
                tv = [x.rearrange("p (g j c) -> p g j c", g=8, j=FR) for x in tmpS]
                i = cmul(o[0], o[1], pp[0], pp[1], bb[0], bb[1], *tv, last=True)
                i.then_inc(ba_done, 1)
                dve.wait_ge(ba_done, c + 1)
            powers_of_b(0)
            Er, Ei = Eri
            own(dve.tensor_copy(rK[0], U[:, 8, :]))
            own(dve.tensor_copy(rK[1], V[:, 8, :]))
            own(dve.tensor_copy(mag8, mag[:, 8, :]))
            own(dve.memset(Er[:, :, 0], 1.0))
            own(dve.memset(Ei[:, :, 0], 0.0))
            m = 1
            while m < NC8:
                bcast = lambda x: x.unsqueeze(2).to_broadcast([128, NPAIR, m])
                tv = [tmpS[q][:, 0:m * NPAIR].rearrange("p (g m) -> p g m", m=m) for q in range(2)]
                cmul(Er[:, :, m:2 * m], Ei[:, :, m:2 * m], Er[:, :, 0:m], Ei[:, :, 0:m], bcast(rK[0]), bcast(rK[1]), *tv)
                if 2 * m < NC8:
                    own(dve.tensor_tensor(rK[2], rK[0], rK[0], ALU.mult))
                    own(dve.tensor_tensor(rK[3], rK[1], rK[1], ALU.mult))
                    own(dve.tensor_tensor(rK[4], rK[0], rK[1], ALU.mult))
                    own(dve.tensor_tensor(rK[0], rK[2], rK[3], ALU.subtract))
                    own(dve.tensor_scalar(rK[1], rK[4], 2.0, None, ALU.mult))
                m *= 2
            for c in range(1, 4):
                powers_of_b(c)
            dve.wait_ge(half_used, 2 * SLOT0["sin"] + 32)
            for c in range(2):
                gs = slice(c * 8, c * 8 + 8)
                cc = [bc[2 + q][:, gs, :].unsqueeze(2).to_broadcast([128, 8, FR, SC]) for q in range(2)]
                pp = [p[:, 1:9, gs].rearrange("p k g -> p g k").unsqueeze(3).to_broadcast([128, 8, FR, SC]) for p in (Pr, Pi)]
                o = [CA[q][:, gs, :].rearrange("p g (k c) -> p g k c", c=SC) for q in range(2)]
                tv = [x.rearrange("p (g j c) -> p g j c", g=8, j=FR) for x in tmpS]
                own(dve.tensor_tensor(tv[0], pp[0], cc[0], ALU.mult))
                own(dve.tensor_tensor(tv[1], pp[1], cc[1], ALU.mult))
                own(dve.tensor_tensor(o[0], tv[0], tv[1], ALU.add))
                own(dve.tensor_tensor(tv[0], pp[0], cc[1], ALU.mult))
                own(dve.tensor_tensor(tv[1], pp[1], cc[0], ALU.mult))
                dve.tensor_tensor(o[1], tv[0], tv[1], ALU.subtract).then_inc(ca_done, 1)
                dve.wait_ge(ca_done, c + 1)
            own(dve.tensor_copy(rho, mag8.unsqueeze(2).to_broadcast([128, NPAIR, NC8])))
            own(dve.memset(rho[:, :, 0], 0.0))
            flat = lambda x: x.rearrange("p g c -> p (g c)")
            Ef = [flat(x) for x in Eri]
            wf = [flat(x) for x in wri]
            dve.wait_ge(w_ev, 8)
            own(dve.tensor_tensor(rot[0], wf[0], Ef[1], ALU.mult))
            own(dve.tensor_tensor(rot[1], wf[1], Ef[1], ALU.mult))
            own(dve.tensor_tensor(wf[0], wf[0], Ef[0], ALU.mult))
            own(dve.tensor_tensor(wf[1], wf[1], Ef[0], ALU.mult))
            own(dve.tensor_tensor(wf[0], wf[0], rot[1], ALU.add))
            dve.tensor_tensor(wf[1], wf[1], rot[0], ALU.subtract).then_inc(rot_in, 1)
            dve.wait_ge(rot_in, 1)
            own(dve.tensor_tensor_scan(wf[0], flat(rho), wf[0], 0.0, ALU.mult, ALU.add))
            own(dve.tensor_tensor_scan(wf[1], flat(rho), wf[1], 0.0, ALU.mult, ALU.add))
            own(dve.tensor_tensor(flat(rho), wf[1], Ef[1], ALU.mult))
            own(dve.tensor_tensor(Ef[1], wf[0], Ef[1], ALU.mult))
            own(dve.tensor_tensor(wf[0], wf[0], Ef[0], ALU.mult))
            own(dve.tensor_tensor(wf[1], wf[1], Ef[0], ALU.mult))
            own(dve.tensor_tensor(wf[0], wf[0], flat(rho), ALU.subtract))
            dve.tensor_tensor(wf[1], wf[1], Ef[1], ALU.add).then_inc(x_done, 1)
            for part in range(2):
                dve.wait_ge(y_in, (part + 1) * 8 * 16)
                if part:
                    dve.wait_ge(k_mm, 8)
                for k in range(4 * part, 4 * part + 4):
                    o = yD[:, k, :].rearrange("p (c j) -> p j c", j=FR)
                    u_ = suP[:, k, :].rearrange("p (j c) -> p j c", c=NC8)
                    y_ = yF[:, k, :].rearrange("p (j c) -> p j c", c=NC8)
                    dve.scalar_tensor_tensor(o, u_, param("d_skip")[:, k:k + 1], y_, ALU.mult, ALU.add).then_inc(y_d, 1)
                for k in range(4 * part, 4 * part + 4):
                    dve.wait_ge(y_lead, k + 1)
                    dve.tensor_tensor(uL[:, k, :], yD[:, k, :], uH[:, k, :].bitcast(f32), ALU.subtract).then_inc(y_g, 1)
            with dve.Fori(0, 4) as m:
                for x in range(2):
                    dve.wait_ge(glu_s, m * 2 + x + 1)
                    dve.tensor_tensor(gprod[:, x, :], ps[:, 2 * x, :], sg[:, x, :], ALU.mult).then_inc(tile_evicted, 2)
                    dve.wait_ge(tile_evicted, m * 4 + TILE0["glu"] + 2 * x + 2)
                    dve.tensor_tensor(gprod[:, x, :], gprod[:, x, :], szT[:, m * 2 + x, :], ALU.mult).then_inc(glu_m, 1)
                for x in range(2):
                    dve.wait_ge(glu_lead, m * 2 + x + 1)
                    dve.tensor_tensor(mL[:, m * 2 + x, :], gprod[:, x, :], mH[:, m * 2 + x, :].bitcast(f32),
                                      ALU.subtract).then_inc(glu_o, 1)
                dve.wait_ge(glu_o, m * 2 + 2)
            residual("sout")
            rms_dve(5, "final_norm", hT)


def constants():
    p, c = np.arange(128)[:, None], np.arange(128)[None, :]
    same = p // CH == c // CH
    t = {}
    t["ident"] = p == c
    t["ones"] = np.ones((128, 128))
    t["cumsum"] = same & (p <= c)
    t["block"] = same
    t["half"] = np.concatenate([np.broadcast_to(p // CH == i, (128, 128)) for i in range(2)], 1)
    t["maskneg"] = np.where(same & (c <= p), 0.0, NEG)
    t["neg16"] = np.where((p // 16 == c // 16) & (c < p), -1.0, 0.0)
    t["low32"] = (p // 32 == c // 32) & (p // 16 > c // 16)
    t["low64"] = (p // 64 == c // 64) & (p // 32 > c // 32)
    k = np.arange(T)[None, :]
    ahead = k - (T - 128) - p
    t["dist"] = np.where(ahead <= 0, ahead, NEG)
    n = np.arange(NCMP)[None, None, :]
    tok = p[:, :, None] + 128 * np.arange(TT)[None, :, None]
    seen = CMPS * n + CMPB - 1 <= tok
    t["cdist"] = np.where(seen, CMPS * n + 0.5 * (CMPB - 1) - tok, NEG).reshape(128, -1)
    t["cmask"] = seen.reshape(128, -1)
    t["slope"] = np.broadcast_to(2.0 ** (-8.0 * (np.array(HALF_ORDER) + 1) / NH), (128, NH))
    t["invcount"] = np.broadcast_to(np.concatenate(
        [1.0 / np.minimum(np.arange(1, PAD + 1), 2 ** (g + 1)) for g in range(4)]), (128, 4 * PAD))
    return np.concatenate([np.asarray(t[name], np.float32) for name in CONST_W], 1)


def slots(w):
    k, m = w.shape
    return w.reshape(k // 128, 128, m // 128, 128).transpose(2, 1, 0, 3).reshape(m // 128, 128, k)


def by_partition(v):
    return v.reshape(-1, 128).T


def tall(w):
    return w.reshape(-1, 128, w.shape[1]).transpose(1, 0, 2).reshape(128, -1)


def lay_out(i):
    a = {}
    w_in = i["w_in"][0]
    nsa = i["l0_w_in_2"]
    qcols = np.concatenate([h * DH + np.arange(DH) for h in HEAD_ORDER])
    s = NH * DH
    kv = NG * DH
    zcols = s + 6 * kv + 3 * NH + qcols
    branches = [nsa[:, s + b * kv:s + (b + 1) * kv] for b in range(6)]
    nsa_feature = np.concatenate([nsa[:, qcols], branches[0], branches[1], branches[2], branches[4]], 1)
    v_both = np.concatenate([branches[3], branches[5]], 1)
    val = v_both.reshape(4, 2, 128, 512).transpose(0, 2, 1, 3).reshape(4, 128, 1024)
    glu = i["l1_w_glu_2"].reshape(D, 2, KT, 128).transpose(0, 2, 1, 3).reshape(D, 2 * D)
    up = slots(i["w_up"][0])
    down = i["w_down"][0].reshape(4, D, D)
    down = [np.stack([slots(d) for d in down[2 * n:2 * n + 2]], 1).reshape(16, 128, 1024) for n in range(2)]
    stream = np.concatenate([
        slots(w_in[:, :20 * 128]), slots(i["w_out"][0]), up[:16], down[0], up[16:], down[1],
        slots(nsa_feature), val, slots(nsa[:, zcols]), slots(i["l0_w_out_2"][qcols]),
        slots(i["l1_w_in_2"]), slots(glu), slots(i["l1_w_out_2"])])
    a["wstream"] = stream.reshape(-1, 128, 2, 512).transpose(0, 2, 1, 3).reshape(-1, 128, 512)
    a["x"] = i["x"][0].T.reshape(KT, 128, T).transpose(1, 0, 2)
    a["consts"] = constants()
    a["w_ab"] = tall(w_in[:, 20 * 128:])
    a["w_gate"] = tall(nsa[:, s + 6 * kv + np.concatenate([b * NH + np.array(HALF_ORDER) for b in range(3)])])
    a["w_pool"] = i["w_pool"][0].transpose(1, 0, 2).reshape(128, 512)
    for n in "kv":
        a[f"cmp_{n}_w1"] = tall(i[f"l0_cmp_{n}_w1_2"])
        a[f"cmp_{n}_w2"] = tall(i[f"l0_cmp_{n}_w2_2"])
    pair = lambda v: v.reshape(NPAIR, 128, -1).transpose(1, 0, 2).reshape(128, -1)
    a["ssm_b_re"] = pair(i["l1_b_re_2"])
    a["ssm_b_im"] = pair(i["l1_b_im_2"])
    a["ssm_c_re"] = pair(i["l1_c_re_2"].transpose(0, 2, 1))
    a["ssm_c_im"] = pair(i["l1_c_im_2"].transpose(0, 2, 1))
    t = dict(norm_mix=by_partition(i["norm_mix"]), norm_mlp=by_partition(i["norm_mlp"]),
             norm_final=by_partition(i["norm_final"]), l0_norm=by_partition(i["l0_norm_2"]),
             l1_norm=by_partition(i["l1_norm_2"]), final_norm=by_partition(i["final_norm_2"]),
             conv=i["conv_w"][0].reshape(CONV, 12, 128).transpose(2, 1, 0).reshape(128, -1),
             pool_scale=by_partition(i["pool_scale"]), gdn_norm=i["gdn_norm"].T,
             a_log=np.broadcast_to(np.tile(i["a_log"][0], TT), (128, 16)),
             dt_bias=np.broadcast_to(np.tile(i["dt_bias"][0], TT), (128, 16)),
             kpe=i["l0_cmp_k_pe_2"].reshape(CMPB // 2, 128).T, vpe=i["l0_cmp_v_pe_2"].reshape(CMPB // 2, 128).T,
             d_skip=by_partition(i["l1_d_2"]),
             log_dt=np.repeat(i["l1_log_dt_2"].reshape(NPAIR, 2).T, SP, 0),
             lre=pair(i["l1_lambda_re_2"]), lim=pair(i["l1_lambda_im_2"]))
    a["params"] = np.concatenate([t[name] for name in PARAM_W], 1)
    return {n: np.ascontiguousarray(v) for n, v in a.items()}


HEAD_ORDER = [(2 * gp + g2) * 4 + r for gp in range(2) for r in range(4) for g2 in range(2)]
HALF_ORDER = HEAD_ORDER[0::2] + HEAD_ORDER[1::2]


def kernel(**inputs):
    from concourse import bacc
    from concourse.bass_utils import run_bass_kernel_spmd

    nc = bacc.Bacc("TRN2", target_bir_lowering=False, num_devices=1, dynamic_dma_scratch_size=64)
    arrays = lay_out({n: np.asarray(v) for n, v in inputs.items()})
    A = {n: nc.dram_tensor(n, v.shape, mybir.dt.from_np(v.dtype), kind="ExternalInput").ap() for n, v in arrays.items()}
    out = nc.dram_tensor("out", (128, KT, T), mybir.dt.float32, kind="ExternalOutput").ap()
    scratch = {"u": nc.dram_tensor("u_scratch", (128, KT, T), mybir.dt.float32).ap(),
               "y": nc.dram_tensor("y_scratch", (2, 128, SG // 2, NC8), mybir.dt.float32).ap()}
    build(nc, A, scratch, out)
    r = run_bass_kernel_spmd(nc, [arrays], core_ids=[0])
    y = r.results[0]["out"]
    return y.transpose(1, 0, 2).reshape(D, T).T.reshape(1, T, D)
```
